# Optimizing a Trainium2 kernel written in Bass

```python
import math
import jax
import jax.numpy as jnp
from jax import lax

D_MODEL = 1024
BATCH = 1
SEQ = 1024
DEPTH = 2

N_META = 16
CHUNK = 64
NORM_EPS = 1e-6

GLA_HEADS = 4
GLA_DK = D_MODEL // (2 * GLA_HEADS)
GLA_DV = D_MODEL // GLA_HEADS
GLA_GATE_RANK = 16
GLA_GATE_NORMALIZER = 16.0
GLA_QK = GLA_HEADS * GLA_DK
GLA_V = GLA_HEADS * GLA_DV
GLA_IN = 2 * GLA_QK + 2 * GLA_V + GLA_GATE_RANK

GDN_HEADS = 8
GDN_DK = D_MODEL // GDN_HEADS
GDN_DV = 2 * GDN_DK
GDN_QK = GDN_HEADS * GDN_DK
GDN_V = GDN_HEADS * GDN_DV
GDN_IN = 2 * GDN_QK + 2 * GDN_V + 2 * GDN_HEADS
CONV_WIDTH = 4

N_GLA = (DEPTH + 1) // 2
N_GDN = DEPTH // 2

kernel_name = 'hybrid_gla_gdn_meta'

def rms_norm(x, w):
    xf = x.astype(jnp.float32)
    y = xf * lax.rsqrt(jnp.mean(xf * xf, axis=-1, keepdims=True) + NORM_EPS)
    return (y * w.astype(jnp.float32)).astype(x.dtype)

def l2_norm(x):
    return x * lax.rsqrt(jnp.sum(x * x, axis=-1, keepdims=True) + NORM_EPS)

def to_chunks(t, c):
    b, l, h, d = t.shape
    return t.reshape(b, l // c, c, h, d).transpose(0, 3, 1, 2, 4)

def from_chunks(t):
    b, h, n, c, d = t.shape
    return t.transpose(0, 2, 3, 1, 4).reshape(b, n * c, h, d)

def chunk_first(t):
    return jnp.moveaxis(t, 2, 0)

def causal_depthwise_conv(x, w):
    k = w.shape[0]
    return lax.conv_general_dilated(
        x, w[:, None, :].astype(x.dtype), window_strides=(1,), padding=[(k - 1, 0)],
        dimension_numbers=('NWC', 'WIO', 'NWC'), feature_group_count=x.shape[-1])

def gla_chunk_scan(q, k, v, log_a, s0, c):
    q, k, v, log_a = (to_chunks(t, c) for t in (q, k, v, log_a))
    b = jnp.cumsum(log_a, axis=3)
    b_last = b[:, :, :, -1:, :]
    q_in = q * jnp.exp(b)
    k_in = k * jnp.exp(-b)
    k_out = k * jnp.exp(b_last - b)
    causal = jnp.tril(jnp.ones((c, c), dtype=bool))
    a_intra = jnp.where(causal, jnp.einsum('bhnid,bhnjd->bhnij', q_in, k_in), 0.0)
    o_intra = jnp.einsum('bhnij,bhnjv->bhniv', a_intra, v)

    def step(s, inp):
        q_c, k_c, v_c, dec = inp
        o = jnp.einsum('bhid,bhdv->bhiv', q_c, s)
        s = s * dec[..., None] + jnp.einsum('bhid,bhiv->bhdv', k_c, v_c)
        return s, o

    xs = (chunk_first(q_in), chunk_first(k_out), chunk_first(v), chunk_first(jnp.exp(b_last[:, :, :, 0])))
    s_final, o_inter = lax.scan(step, s0, xs)
    o = o_intra + jnp.moveaxis(o_inter, 0, 2)
    return from_chunks(o), s_final

def gdn_chunk_scan(q, k, v, beta, log_a, s0, c):
    dv = v.shape[-1]
    q, k, v = (to_chunks(t, c) for t in (q, k, v))
    beta, log_a = (to_chunks(t[..., None], c)[..., 0] for t in (beta, log_a))
    g = jnp.cumsum(log_a, axis=-1)
    g_last = g[..., -1:]
    causal = jnp.tril(jnp.ones((c, c), dtype=bool))
    strict = jnp.tril(jnp.ones((c, c), dtype=bool), k=-1)
    diff = g[..., :, None] - g[..., None, :]
    decay_mat = jnp.exp(jnp.where(causal, diff, -jnp.inf))
    kb = k * beta[..., None]
    m = jnp.where(strict, jnp.einsum('bhnid,bhnjd->bhnij', kb, k) * decay_mat, 0.0)
    rhs = jnp.concatenate([v * beta[..., None], kb * jnp.exp(g)[..., None]], axis=-1)
    sol = lax.linalg.triangular_solve(m, rhs, left_side=True, lower=True, unit_diagonal=True)
    u, w = sol[..., :dv], sol[..., dv:]
    a_qk = jnp.einsum('bhnid,bhnjd->bhnij', q, k) * decay_mat
    q_dec = q * jnp.exp(g)[..., None]
    k_dec = k * jnp.exp(g_last - g)[..., None]

    def step(s, inp):
        q_c, k_c, u_c, w_c, a_c, tot = inp
        v_new = u_c - jnp.einsum('bhid,bhdv->bhiv', w_c, s)
        o = jnp.einsum('bhid,bhdv->bhiv', q_c, s) + jnp.einsum('bhij,bhjv->bhiv', a_c, v_new)
        s = s * tot[..., None, None] + jnp.einsum('bhid,bhiv->bhdv', k_c, v_new)
        return s, o

    xs = (chunk_first(q_dec), chunk_first(k_dec), chunk_first(u), chunk_first(w),
          chunk_first(a_qk), chunk_first(jnp.exp(g_last[..., 0])))
    s_final, o = lax.scan(step, s0, xs)
    return from_chunks(jnp.moveaxis(o, 0, 2)), s_final

def run_segments(scan_fn, s0, *args):
    meta_out, s = scan_fn(*(a[:, :N_META] for a in args), s0, N_META)
    real_out, _ = scan_fn(*(a[:, N_META:] for a in args), s, CHUNK)
    return jnp.concatenate([meta_out, real_out], axis=1)

def gla_mixer(h, w_in, w_gk, b_gk, head_norm, w_out):
    b, l, _ = h.shape
    f32 = jnp.float32
    proj = h @ w_in
    q, k, v, z, gk_low = jnp.split(
        proj, [GLA_QK, 2 * GLA_QK, 2 * GLA_QK + GLA_V, 2 * GLA_QK + 2 * GLA_V], axis=-1)
    gk = gk_low @ w_gk + b_gk
    log_a = (jax.nn.log_sigmoid(gk.astype(f32)) / GLA_GATE_NORMALIZER).reshape(b, l, GLA_HEADS, GLA_DK)
    q = q.astype(f32).reshape(b, l, GLA_HEADS, GLA_DK) * (GLA_DK ** -0.5)
    k = k.astype(f32).reshape(b, l, GLA_HEADS, GLA_DK)
    v = v.astype(f32).reshape(b, l, GLA_HEADS, GLA_DV)
    s0 = jnp.zeros((b, GLA_HEADS, GLA_DK, GLA_DV), f32)
    o = run_segments(gla_chunk_scan, s0, q, k, v, log_a)
    o = rms_norm(o, head_norm) * jax.nn.silu(z.astype(f32)).reshape(b, l, GLA_HEADS, GLA_DV)
    return o.reshape(b, l, GLA_V).astype(h.dtype) @ w_out

def gdn_mixer(h, w_in, conv_w, a_log, dt_bias, head_norm, w_out):
    b, l, _ = h.shape
    f32 = jnp.float32
    proj = h @ w_in
    qkv, z, beta_logit, a_logit = jnp.split(
        proj, [2 * GDN_QK + GDN_V, 2 * GDN_QK + 2 * GDN_V, 2 * GDN_QK + 2 * GDN_V + GDN_HEADS], axis=-1)
    qkv = jax.nn.silu(causal_depthwise_conv(qkv, conv_w)).astype(f32)
    q, k, v = jnp.split(qkv, [GDN_QK, 2 * GDN_QK], axis=-1)
    q = l2_norm(q.reshape(b, l, GDN_HEADS, GDN_DK)) * (GDN_DK ** -0.5)
    k = l2_norm(k.reshape(b, l, GDN_HEADS, GDN_DK))
    v = v.reshape(b, l, GDN_HEADS, GDN_DV)
    beta = jax.nn.sigmoid(beta_logit.astype(f32))
    log_a = -jnp.exp(a_log.astype(f32)) * jax.nn.softplus(a_logit.astype(f32) + dt_bias.astype(f32))
    s0 = jnp.zeros((b, GDN_HEADS, GDN_DK, GDN_DV), f32)
    o = run_segments(gdn_chunk_scan, s0, q, k, v, beta, log_a)
    o = rms_norm(o, head_norm) * jax.nn.silu(z.astype(f32)).reshape(b, l, GDN_HEADS, GDN_DV)
    return o.reshape(b, l, GDN_V).astype(h.dtype) @ w_out

def setup_inputs(seed: int = 0) -> dict:
    key = jax.random.key(seed)
    ks = jax.random.split(key, 20)
    f32 = jnp.float32

    def nrm(k, shape, scale):
        return jax.random.normal(k, shape, f32) * scale

    x = nrm(ks[0], (BATCH, SEQ, D_MODEL), 1.0)
    meta_tokens = nrm(ks[1], (N_META, D_MODEL), 1.0)
    gla_norm = 1.0 + nrm(ks[2], (N_GLA, D_MODEL), 0.02)
    gla_w_in = nrm(ks[3], (N_GLA, D_MODEL, GLA_IN), D_MODEL ** -0.5)
    gla_w_gk = nrm(ks[4], (N_GLA, GLA_GATE_RANK, GLA_QK), GLA_GATE_RANK ** -0.5)
    gla_b_gk = nrm(ks[5], (N_GLA, GLA_QK), 0.02)
    gla_head_norm = 1.0 + nrm(ks[6], (N_GLA, GLA_DV), 0.02)
    gla_w_out = nrm(ks[7], (N_GLA, GLA_V, D_MODEL), GLA_V ** -0.5)
    gdn_norm = 1.0 + nrm(ks[8], (N_GDN, D_MODEL), 0.02)
    gdn_w_in = nrm(ks[9], (N_GDN, D_MODEL, GDN_IN), D_MODEL ** -0.5)
    gdn_conv_w = nrm(ks[10], (N_GDN, CONV_WIDTH, 2 * GDN_QK + GDN_V), CONV_WIDTH ** -0.5)
    a_init = jax.random.uniform(ks[11], (N_GDN, GDN_HEADS), f32, 1.0, 16.0)
    gdn_a_log = jnp.log(a_init)
    dt = jnp.exp(jax.random.uniform(ks[12], (N_GDN, GDN_HEADS), f32, math.log(1e-3), math.log(1e-1)))
    gdn_dt_bias = dt + jnp.log(-jnp.expm1(-dt))
    gdn_head_norm = 1.0 + nrm(ks[13], (N_GDN, GDN_DV), 0.02)
    gdn_w_out = nrm(ks[14], (N_GDN, GDN_V, D_MODEL), GDN_V ** -0.5)
    final_norm = 1.0 + nrm(ks[15], (D_MODEL,), 0.02)
    return {'x': x, 'meta_tokens': meta_tokens,
            'gla_norm': gla_norm, 'gla_w_in': gla_w_in, 'gla_w_gk': gla_w_gk, 'gla_b_gk': gla_b_gk,
            'gla_head_norm': gla_head_norm, 'gla_w_out': gla_w_out,
            'gdn_norm': gdn_norm, 'gdn_w_in': gdn_w_in, 'gdn_conv_w': gdn_conv_w, 'gdn_a_log': gdn_a_log,
            'gdn_dt_bias': gdn_dt_bias, 'gdn_head_norm': gdn_head_norm, 'gdn_w_out': gdn_w_out,
            'final_norm': final_norm}

def reference(x, meta_tokens, gla_norm, gla_w_in, gla_w_gk, gla_b_gk, gla_head_norm, gla_w_out,
              gdn_norm, gdn_w_in, gdn_conv_w, gdn_a_log, gdn_dt_bias, gdn_head_norm, gdn_w_out,
              final_norm):
    b = x.shape[0]
    meta = jnp.broadcast_to(meta_tokens[None], (b, N_META, D_MODEL)).astype(x.dtype)
    h = jnp.concatenate([meta, x], axis=1)
    for i in range(DEPTH):
        j = i // 2
        if i % 2 == 0:
            h = h + gla_mixer(rms_norm(h, gla_norm[j]), gla_w_in[j], gla_w_gk[j], gla_b_gk[j],
                              gla_head_norm[j], gla_w_out[j])
        else:
            h = h + gdn_mixer(rms_norm(h, gdn_norm[j]), gdn_w_in[j], gdn_conv_w[j], gdn_a_log[j],
                              gdn_dt_bias[j], gdn_head_norm[j], gdn_w_out[j])
    h = rms_norm(h, final_norm)
    return h[:, N_META:]


_drawn_inputs = setup_inputs


def setup_inputs(seed=0):
    import zlib

    import numpy as np

    out = dict(_drawn_inputs(seed))
    spreads = {}
    factors = {'gla_b_gk': 8.0,
     'gla_head_norm': 4.598,
     'gdn_norm': 4.056,
     'gdn_head_norm': 5.749,
     'final_norm': 2.866}
    for name, (base, spread) in spreads.items():
        noise = np.random.default_rng([zlib.crc32(name.encode()), seed]).standard_normal(out[name].shape)
        drawn = base * np.exp(spread * noise) if base else spread * noise
        out[name] = jnp.asarray(drawn.astype(out[name].dtype))
    for name, factor in factors.items():
        out[name] = (out[name] * factor).astype(out[name].dtype)
    return out
```

```python
from contextlib import ExitStack

import numpy as np
import concourse.bass as bass
from concourse import mybir
from concourse.alu_op_type import AluOpType as ALU

F32 = mybir.dt.float32
F32R = mybir.dt.float32r
I32 = mybir.dt.int32
ACT = mybir.ActivationFunctionType
AX = mybir.AxisListType

P = 128
D = 1024
KT = D // P
SEQ = 1024
NMETA = 16
C = 64
PAD = P - NMETA
TP = P + SEQ
NT = TP // P
L = NMETA + SEQ
EPS = 1e-6
SPANS = [(0, 352), (352, 344), (696, 344)]
GH, GDK, GDV = 4, 128, 256
GRANK = 16
GQK, GV = GH * GDK, GH * GDV
NH, NDK, NDV = 8, 128, 256
NQK, NV = NH * NDK, NH * NDV
HP = NH // 2
CONV = 4
LEVELS = [2, 4, 8, 16, 32]

K_EYE, K_CAUSAL, K_EYEP, K_CAUSP, K_LOW1T, K_LOW = 0, 128, 256, 320, 384, 448
K_END = K_LOW + (1 + len(LEVELS)) * C


def constants():
    k = np.zeros((P, K_END), np.float32)
    j, i = np.meshgrid(np.arange(P), np.arange(P), indexing="ij")
    k[:, K_EYE:K_EYE + P] = j == i
    k[:, K_CAUSAL:K_CAUSAL + P] = (j // C == i // C) & (j <= i)
    r, c = np.meshgrid(np.arange(P) % C, np.arange(C), indexing="ij")
    k[:, K_EYEP:K_EYEP + C] = r == c
    k[:, K_CAUSP:K_CAUSP + C] = r <= c

    def below(a, b, size):
        return (a // size % 2 == 1) & (a // size - b // size == 1)
    k[:, K_LOW1T:K_LOW1T + C] = below(c, r, 1)
    for n, size in enumerate([1] + LEVELS):
        k[:, K_LOW + n * C:K_LOW + (n + 1) * C] = below(r, c, size)
    return k


def chunk_starts():
    m = np.ones((P, L), np.float32)
    m[:, 0] = 0
    m[:, NMETA::C] = 0
    return m


class Sems:

    def __init__(self, nc):
        self.nc, self.made = nc, {}

    def __call__(self, name):
        if name not in self.made:
            self.made[name] = self.nc.alloc_semaphore(name=name)
        return self.made[name]

    def give_back(self):
        self.nc.all_engine_barrier()
        self.nc.clear_and_free_semaphores(list(self.made.values()))
        self.nc.all_engine_barrier()
        self.made = {}


def wait(eng, sem, value):
    if isinstance(value, int) and value <= 0:
        return
    eng.wait_ge(sem, value)


def waits_apart(eng, carrier, *waits):
    for s, v in waits:
        wait(eng, s, v)
    carrier()


def ds(i, n=1):
    return bass.ds(i, n)


def bc(ap, shape):
    return ap.broadcast_to(shape)


def embed(nc, S, T, x, meta, norm_w):
    with ExitStack() as ctx:
        def sb(name, shape, dt=F32):
            return ctx.enter_context(nc.sbuf_tensor(name, shape, dt))
        X = [sb(f"em_x{j}", [P, D]) for j in range(2)]
        hn = [sb(f"em_hn{j}", [P, D]) for j in range(2)]
        junk = sb("em_junk", [P, D])
        ss = [sb(f"em_ss{j}", [P, 1]) for j in range(2)]
        rs = [sb(f"em_rs{j}", [P, 1]) for j in range(2)]
        nw = sb("em_nw", [P, D])
        tr = [ctx.enter_context(nc.psum_tensor(f"em_tr{j}{b}", [P, 4, P], F32)) for j in range(2) for b in range(2)]
        block = ctx.enter_context(nc.Block())
        x_in = [S("em_x_in0"), S("em_x_in1")]

        def over_tiles(eng, one):
            one(0, 0, 0)
            with eng.Fori(0, (NT - 1) // 2) as i:
                one(i * 2 + 1, 1, i)
                one(i * 2 + 2, 0, i + 1)

        @block.sync
        def _(sp):
            sp.dma_start(T.k[:, :], T.k_dram).then_inc(S("k_in"), 16)
            sp.dma_start(nw[:, :], bc(norm_w, [P, D])).then_inc(S("em_nw_in"), 16)
            wait(sp, S("em_x_zero"), 1)
            sp.dma_start(X[0][PAD:P, :], meta).then_inc(x_in[0], 16)

            def load(t, j, n):
                if isinstance(t, int) and t == 0:
                    return
                wait(sp, S("em_hn_done"), t - 1)
                sp.dma_start(X[j][:, :], x[ds((t - 1) * P, P), :]).then_inc(x_in[j], 16)
            over_tiles(sp, load)
            sp.wait_ge(S("em_zero"), 1)
            for dst, src in T.pads():
                sp.dma_start(dst, src).then_inc(S("pads_out"), 16)
            wait(sp, S("pads_out"), 16 * len(T.pads()))

        @block.scalar
        def _(act):
            def one(t, j, n):
                wait(act, x_in[j], n * 16 + 16)
                wait(act, S("em_ss"), t)
                wait(act, S("em_mean"), t - 1 if isinstance(t, int) else t - 1)
                act.activation(junk[:, :], X[j][:, :], ACT.Square, accum_out=ss[j][:, :]).then_inc(S("em_ss"), 1)
                for b in range(2):
                    wait(act, S("em_tr"), t * 2 + b + 1)
                    act.activation(T.hn_hi[:, 4 * b:4 * b + 4, ds(t * P, P)], tr[2 * j + b][:, :, :],
                                   ACT.Copy).then_inc(S("em_hi"), 1)
            over_tiles(act, one)

        @block.gpsimd
        def _(pool):
            pool.memset(T.zeros[:, :], 0.0).then_inc(S("em_zero"), 1)
            pool.memset(T.minus_half[:, :], -0.5).then_inc(S("em_half"), 1)
            pool.wait_ge(S("em_half"), 1)

            def one(t, j, n):
                waits_apart(pool, T.pool_carrier,
                            (S("em_ss"), t + 1),
                            (S("em_hn_done"), t - 1))
                pool.tensor_scalar(rs[j][:, :], ss[j][:, :], 1.0 / D, EPS, ALU.mult, ALU.add).then_inc(S("em_mean"), 1)
                wait(pool, S("em_mean"), t + 1)
                pool.tensor_tensor(rs[j][:, :], rs[j][:, :], T.minus_half[:, 0:1], ALU.pow).then_inc(S("em_rs"), 1)
            over_tiles(pool, one)

        @block.vector
        def _(dve):
            dve.memset(X[0][:, :], 0.0).then_inc(S("em_x_zero"), 1)
            dve.wait_ge(S("em_nw_in"), 16)

            def one(t, j, n):
                wait(dve, S("em_rs"), t + 1)
                wait(dve, x_in[j], n * 16 + 16)
                wait(dve, S("em_tr"), t * 2 - 2 if not isinstance(t, int) else 2 * t - 2)
                dve.scalar_tensor_tensor(hn[j][:, :], X[j][:, :], rs[j][:, 0:1], nw[:, :],
                                         ALU.mult, ALU.mult).then_inc(S("em_hn_done"), 1)
                for b in range(2):
                    wait(dve, S("em_hi"), t * 2 + b + 1)
                    dve.tensor_tensor(T.hn_lo[:, 4 * b:4 * b + 4, ds(t * P, P)], tr[2 * j + b][:, :, :],
                                      T.hn_hi[:, 4 * b:4 * b + 4, ds(t * P, P)].bitcast(F32),
                                      ALU.subtract).then_inc(S("em_lo"), 1)
            over_tiles(dve, one)

        @block.tensor
        def _(pe):
            pe.wait_ge(S("k_in"), 16)

            def one(t, j, n):
                wait(pe, S("em_hn_done"), t + 1)
                wait(pe, S("em_lo"), t * 2 - 2 if not isinstance(t, int) else 2 * t - 2)
                for b in range(2):
                    for c in range(4):
                        kt = 4 * b + c
                        mm = pe.transpose(tr[2 * j + b][:, c, :], hn[j][:, kt * P:(kt + 1) * P], T.eye)
                    mm.then_inc(S("em_tr"), 1)
            over_tiles(pe, one)


def project(pe, acc, w_hi, w_lo, T):
    for kt in range(KT):
        for n, (w, h) in enumerate(((w_hi, T.hn_hi), (w_hi, T.hn_lo), (w_lo, T.hn_hi))):
            for b, (s, m) in enumerate(SPANS):
                mm = pe.matmul(acc[:, b, 0:m], w[:, kt, :], h[:, kt, PAD + s:PAD + s + m],
                               start=(kt == 0 and n == 0), stop=(kt == KT - 1 and n == 2))
    return mm


class Proj:

    def __init__(self, nc, S, T, ctx, tag, w, col):
        self.S, self.T, self.tag, self.col = S, T, tag, col
        self.w = w.rearrange("(k p) n -> p k n", p=P)
        self.st = [ctx.enter_context(nc.sbuf_tensor(f"{tag}_w{j}", [P, KT, P], F32)) for j in range(2)]
        self.hi = [ctx.enter_context(nc.sbuf_tensor(f"{tag}_whi{j}", [P, KT, P], F32R)) for j in range(2)]
        self.lo = [ctx.enter_context(nc.sbuf_tensor(f"{tag}_wlo{j}", [P, KT, P], F32R)) for j in range(2)]
        self.acc = [ctx.enter_context(nc.psum_tensor(f"{tag}_acc{j}", [P, 3, 512], F32)) for j in range(2)]
        self.trA = ctx.enter_context(nc.psum_tensor(f"{tag}_trA", [P, 4, P], F32))
        self.trB = ctx.enter_context(nc.psum_tensor(f"{tag}_trB", [P, 4, P], F32))

    def sem(self, name):
        return self.S(f"{self.tag}_{name}")

    def load(self, sp, i, j):
        wait(sp, self.sem(f"whi{j}"), i)
        wait(sp, self.sem(f"wlo{j}"), i)
        sp.dma_start(self.st[j][:, :, :], self.w[:, :, ds(self.col(i, j), P)]).then_inc(self.sem(f"w_in{j}"), 16)

    def split_hi(self, act, i, j):
        wait(act, self.sem(f"w_in{j}"), i * 16 + 16)
        wait(act, self.sem(f"mm{j}"), i)
        act.activation(self.hi[j][:, :, :], self.st[j][:, :, :], ACT.Copy).then_inc(self.sem(f"whi{j}"), 1)

    def split_lo(self, pool, i, j):
        wait(pool, self.sem(f"whi{j}"), i + 1)
        wait(pool, self.sem(f"mm{j}"), i)
        wait(pool, self.sem(f"w_in{j}"), i * 16 + 16)
        pool.tensor_tensor(self.lo[j][:, :, :], self.st[j][:, :, :], self.hi[j][:, :, :].bitcast(F32),
                           ALU.subtract).then_inc(self.sem(f"wlo{j}"), 1)

    def mm(self, pe, i, j, free):
        wait(pe, self.sem(f"whi{j}"), i + 1)
        wait(pe, self.sem(f"wlo{j}"), i + 1)
        wait(pe, self.sem(f"free{j}"), i * free)
        project(pe, self.acc[j], self.hi[j], self.lo[j], self.T).then_inc(self.sem(f"mm{j}"), 1)

    def banks(self):
        return ((0, self.trA), (1, self.trB))


def transpose_out(pe, q, src, b, eye, done):
    if b < 2:
        bank = (q.trA, q.trB)[b]
        for c in range(4):
            s = NMETA + (4 * b + c) * P
            mm = pe.transpose(bank[:, c, :], src[:, s:s + P], eye)
    else:
        mm = pe.transpose(q.trA[0:NMETA, 0, :], src[:, 0:NMETA], eye)
    mm.then_inc(done, 1)


def evacuate_out(eng, copy, q, dst, b, done):
    if b < 2:
        copy(dst[:, 1 + 4 * b:5 + 4 * b, :], (q.trA, q.trB)[b][:, :, :]).then_inc(done, 1)
    else:
        copy(dst[0:NMETA, 0, :], q.trA[0:NMETA, 0, :]).then_inc(done, 1)


def store_tokens(sp, dst, tok, col, width, done):
    sp.dma_start(dst[PAD:P, ds(col, P)], tok[0:NMETA, 0, :]).then_inc(done, 16)
    sp.dma_start(dst[P:TP, ds(col, P)].rearrange("(t p) c -> p t c", p=P), tok[:, 1:NT, :]).then_inc(done, 16)


def gla_gate(nc, S, T, w_in, w_gk, b_gk, head_norm):
    with ExitStack() as ctx:
        def sb(name, shape, dt=F32):
            return ctx.enter_context(nc.sbuf_tensor(name, shape, dt))
        st = sb("gg_w", [P, KT, P])
        hi = sb("gg_whi", [P, KT, P], F32R)
        lo = sb("gg_wlo", [P, KT, P], F32R)
        gl = sb("gg_low", [GRANK, L])
        wg = sb("gg_wgk", [GRANK, GQK])
        bg = sb("gg_b", [P, GH])
        cm = sb("gg_starts", [P, L])
        ax = [sb(f"gg_ax{j}", [P, L]) for j in range(2)]
        mn = [sb(f"gg_mn{j}", [P, L]) for j in range(2)]
        bt = [sb(f"gg_bt{j}", [P, L]) for j in range(2)]
        acc = [ctx.enter_context(nc.psum_tensor(f"gg_acc{j}", [P, 3, 512], F32)) for j in range(2)]
        block = ctx.enter_context(nc.Block())
        c0 = 2 * GQK + 2 * GV

        @block.sync
        def _(sp):
            sp.wait_ge(S("gg_zero"), 1)
            sp.dma_start(st[:, :, 0:GRANK], w_in.rearrange("(k p) n -> p k n", p=P)[:, :, c0:c0 + GRANK])\
              .then_inc(S("gg_w_in"), 16)
            sp.dma_start(wg[:, :], w_gk).then_inc(S("gg_small_in"), 16)
            sp.dma_start(bg[:, :], b_gk).then_inc(S("gg_small_in"), 16)
            sp.dma_start(cm[:, :], T.starts_dram).then_inc(S("gg_small_in"), 16)
            sp.dma_start(T.hnw[:, :], head_norm).then_inc(S("gg_hnw_in"), 16)
            sp.wait_ge(S("gg_hnw_in"), 16)

        @block.scalar
        def _(act):
            act.wait_ge(S("gg_w_in"), 16)
            act.activation(hi[:, :, :], st[:, :, :], ACT.Copy).then_inc(S("gg_whi"), 1)
            act.wait_ge(S("gg_low"), 1)
            for b, (s, m) in enumerate(SPANS):
                act.activation(gl[:, s:s + m], acc[0][0:GRANK, b, 0:m], ACT.Copy).then_inc(S("gg_low_out"), 1)

            def logs(h):
                j = h % 2
                act.wait_ge(S("gg_abs"), h + 1)
                act.activation(ax[j][:, :], ax[j][:, :], ACT.Exp, scale=-1.0).then_inc(S("gg_e"), 1)
                act.wait_ge(S("gg_e"), h + 1)
                act.activation(ax[j][:, :], ax[j][:, :], ACT.Ln, bias=1.0).then_inc(S("gg_ln"), 1)

            def exps(h):
                j = h % 2
                act.wait_ge(S("gg_cum"), h + 1)
                act.activation(T.Eb[:, h, :], bt[j][:, :], ACT.Exp, scale=1.0 / 16).then_inc(S("gg_exps"), 1)
                act.activation(T.Enb[:, h, :], bt[j][:, :], ACT.Exp, scale=-1.0 / 16).then_inc(S("gg_exps"), 1)
                act.activation(T.dec[:, h, 2:], bt[j][:, NMETA + C - 1::C], ACT.Exp, scale=1.0 / 16)\
                   .then_inc(S("gg_exps"), 1)
                act.activation(T.dec[:, h, 1:2], bt[j][:, NMETA - 1:NMETA], ACT.Exp, scale=1.0 / 16)\
                   .then_inc(S("gg_exps"), 1)
                act.wait_ge(S("gg_left"), 2 * (h + 1))
                act.activation(T.Eout[:, h, :], ax[j][:, :], ACT.Exp, scale=1.0 / 16).then_inc(S("gg_exps"), 1)
            for h in range(GH):
                logs(h)
                if h:
                    exps(h - 1)
            exps(GH - 1)
            act.wait_ge(S("gg_exps"), 5 * GH)

        @block.gpsimd
        def _(pool):
            pool.memset(st[:, :, :], 0.0).then_inc(S("gg_zero"), 1)
            pool.memset(T.dec[:, :, 0:1], 1.0).then_inc(S("gg_dec0"), 1)
            pool.wait_ge(S("gg_whi"), 1)
            pool.tensor_tensor(lo[:, :, :], st[:, :, :], hi[:, :, :].bitcast(F32), ALU.subtract)\
                .then_inc(S("gg_wlo"), 1)

        @block.tensor
        def _(pe):
            pe.wait_ge(S("gg_wlo"), 1)
            project(pe, acc[0], hi, lo, T).then_inc(S("gg_low"), 1)
            pe.wait_ge(S("gg_low_out"), 3)
            pe.wait_ge(S("gg_small_in"), 48)
            for h in range(GH):
                if h >= 2:
                    pe.wait_ge(S("gg_min"), 3 * (h - 1))
                for b, (s, m) in enumerate(SPANS):
                    mm = pe.matmul(acc[h % 2][:, b, 0:m], wg[:, h * P:(h + 1) * P], gl[:, s:s + m],
                                   start=True, stop=True)
                mm.then_inc(S("gg_logit"), 1)

        @block.vector
        def _(dve):
            def take(h):
                j = h % 2
                dve.wait_ge(S("gg_logit"), h + 1)
                if h >= 2:
                    dve.wait_ge(S("gg_exps"), 5 * (h - 1))
                for b, (s, m) in enumerate(SPANS):
                    dve.tensor_scalar(ax[j][:, s:s + m], acc[j][:, b, 0:m], bg[:, h:h + 1], 0.0, ALU.add, ALU.max)\
                       .then_inc(S("gg_max"), 1)
                for b, (s, m) in enumerate(SPANS):
                    dve.tensor_scalar(mn[j][:, s:s + m], acc[j][:, b, 0:m], bg[:, h:h + 1], 0.0, ALU.add, ALU.min)\
                       .then_inc(S("gg_min"), 1)
                dve.wait_ge(S("gg_max"), 3 * (h + 1))
                dve.wait_ge(S("gg_min"), 3 * (h + 1))
                dve.tensor_tensor(ax[j][:, :], ax[j][:, :], mn[j][:, :], ALU.subtract).then_inc(S("gg_abs"), 1)

            def cumulate(h):
                j = h % 2
                dve.wait_ge(S("gg_ln"), h + 1)
                dve.wait_ge(S("gg_min"), 3 * (h + 1))
                dve.tensor_tensor(mn[j][:, :], mn[j][:, :], ax[j][:, :], ALU.subtract).then_inc(S("gg_log"), 1)
                dve.wait_ge(S("gg_log"), h + 1)
                dve.tensor_tensor_scan(bt[j][:, :], cm[:, :], mn[j][:, :], 0.0, ALU.mult, ALU.add)\
                   .then_inc(S("gg_cum"), 1)
                dve.wait_ge(S("gg_cum"), h + 1)
                dve.tensor_tensor(ax[j][:, 0:NMETA], bc(bt[j][:, NMETA - 1:NMETA], [P, NMETA]), bt[j][:, 0:NMETA],
                                  ALU.subtract).then_inc(S("gg_left"), 1)
                real = bt[j][:, NMETA:].rearrange("p (c t) -> p c t", t=C)
                dve.tensor_tensor(ax[j][:, NMETA:].rearrange("p (c t) -> p c t", t=C),
                                  bc(real[:, :, C - 1:C], [P, SEQ // C, C]), real, ALU.subtract)\
                   .then_inc(S("gg_left"), 1)
            take(0)
            for h in range(GH):
                if h + 1 < GH and h < 1:
                    take(h + 1)
                cumulate(h)
                if h + 2 < GH:
                    take(h + 2)


def gla_qk(nc, S, T, w_in):
    n = GH
    with ExitStack() as ctx:
        q = Proj(nc, S, T, ctx, "aq", w_in, lambda i, j: j * GQK + i * P)
        qT = ctx.enter_context(nc.sbuf_tensor("aq_q", [P, L], F32))
        kT = ctx.enter_context(nc.sbuf_tensor("aq_k", [P, L], F32))
        oT = ctx.enter_context(nc.sbuf_tensor("aq_kout", [P, L], F32))
        tok = ctx.enter_context(nc.sbuf_tensor("aq_tok", [P, NT, P], F32))
        block = ctx.enter_context(nc.Block())

        @block.sync
        def _(sp):
            def store(i):
                wait(sp, q.sem("free0"), i * 3 + 3)
                sp.dma_start(T.gla_qk[ds(i), 0, :, PAD:TP].rearrange("a p n -> p (a n)"), qT[:, :])\
                  .then_inc(q.sem("q_out"), 16)
                wait(sp, q.sem("free1"), i * 6 + 6)
                sp.dma_start(T.gla_qk[ds(i), 1, :, PAD:TP].rearrange("a p n -> p (a n)"), kT[:, :])\
                  .then_inc(q.sem("k_out"), 16)
                wait(sp, q.sem("ev"), i * 3 + 3)
                store_tokens(sp, T.gla_ko, tok, i * P, GQK, q.sem("tok_out"))
            for j in range(2):
                q.load(sp, 0, j)
            for j in range(2):
                q.load(sp, 1, j)
            with sp.Fori(0, n - 2) as i:
                for j in range(2):
                    q.load(sp, i + 2, j)
                store(i)
            store(n - 2)
            store(n - 1)
            sp.wait_ge(q.sem("q_out"), 16 * n)
            sp.wait_ge(q.sem("k_out"), 16 * n)
            sp.wait_ge(q.sem("tok_out"), 32 * n)

        @block.scalar
        def _(act):
            for j in range(2):
                q.split_hi(act, 0, j)
            with act.Fori(1, n) as i:
                for j in range(2):
                    q.split_hi(act, i, j)

        @block.gpsimd
        def _(pool):
            for j in range(2):
                q.split_lo(pool, 0, j)
            with pool.Fori(1, n) as i:
                for j in range(2):
                    q.split_lo(pool, i, j)

        @block.tensor
        def _(pe):
            def tr(i):
                wait(pe, q.sem("free1"), i * 6 + 6)
                for b in range(3):
                    wait(pe, q.sem("ev"), i * 3 if b == 0 else i * 3 + b - 1)
                    transpose_out(pe, q, oT, b, T.eye, q.sem("tr"))
            q.mm(pe, 0, 0, 3)
            q.mm(pe, 0, 1, 6)
            with pe.Fori(1, n) as i:
                q.mm(pe, i, 0, 3)
                tr(i - 1)
                q.mm(pe, i, 1, 6)
            tr(n - 1)

        @block.vector
        def _(dve):
            def ev(i):
                wait(dve, q.sem("tok_out"), i * 32)
                for b in range(3):
                    wait(dve, q.sem("tr"), i * 3 + b + 1)
                    evacuate_out(dve, dve.tensor_copy, q, tok, b, q.sem("ev"))

            def epi_q(i):
                wait(dve, q.sem("mm0"), i + 1)
                wait(dve, q.sem("q_out"), i * 16)
                for b, (s, m) in enumerate(SPANS):
                    dve.scalar_tensor_tensor(qT[:, s:s + m], q.acc[0][:, b, 0:m], float(GDK) ** -0.5,
                                             T.Eb[:, ds(i), s:s + m].rearrange("p a n -> p (a n)"),
                                             ALU.mult, ALU.mult).then_inc(q.sem("free0"), 1)

            def epi_k(i):
                wait(dve, q.sem("mm1"), i + 1)
                wait(dve, q.sem("k_out"), i * 16)
                wait(dve, q.sem("tr"), i * 3)
                for dst, gate in ((kT, T.Enb), (oT, T.Eout)):
                    for b, (s, m) in enumerate(SPANS):
                        dve.tensor_tensor(dst[:, s:s + m], q.acc[1][:, b, 0:m],
                                          gate[:, ds(i), s:s + m].rearrange("p a n -> p (a n)"), ALU.mult)\
                           .then_inc(q.sem("free1"), 1)
            epi_q(0)
            epi_k(0)
            with dve.Fori(1, n) as i:
                epi_q(i)
                ev(i - 1)
                epi_k(i)
            ev(n - 1)


def project_vz(nc, S, T, tag, w_in, col_v, col_z, n, v_out, z_out, hnw, conv=None):
    with ExitStack() as ctx:
        q = Proj(nc, S, T, ctx, tag, w_in, lambda i, j: (col_v, col_z)[j] + i * P)
        xT = [ctx.enter_context(nc.sbuf_tensor(f"{tag}_x{j}", [P, L], F32)) for j in range(2)]
        tok = [ctx.enter_context(nc.sbuf_tensor(f"{tag}_tok{j}", [P, NT, P], F32)) for j in range(2)]
        if conv is not None:
            xs = ctx.enter_context(nc.sbuf_tensor(f"{tag}_xs", [P, CONV - 1 + L], F32))
            cv = ctx.enter_context(nc.sbuf_tensor(f"{tag}_cv", [P, L], F32))
        block = ctx.enter_context(nc.Block())

        @block.sync
        def _(sp):
            def store(i, j):
                wait(sp, q.sem(f"ev{j}"), i * 3 + 3)
                store_tokens(sp, (v_out, z_out)[j], tok[j], i * P, n * P, q.sem(f"tok_out{j}"))
            for j in range(2):
                q.load(sp, 0, j)
            for j in range(2):
                q.load(sp, 1, j)
            with sp.Fori(0, n - 2) as i:
                for j in range(2):
                    q.load(sp, i + 2, j)
                for j in range(2):
                    store(i, j)
            for i in range(n - 2, n):
                for j in range(2):
                    store(i, j)
            for j in range(2):
                sp.wait_ge(q.sem(f"tok_out{j}"), 32 * n)

        @block.scalar
        def _(act):
            def epi_v(i, before=None):
                wait(act, q.sem("mm0"), i + 1)
                dst, at = (xT[0], 0) if conv is None else (xs, CONV - 1)
                if conv is None:
                    wait(act, q.sem("tr0"), i * 3)
                else:
                    wait(act, q.sem("conv"), i * CONV)
                for b, (s, m) in enumerate(SPANS):
                    act.activation(dst[:, at + s:at + s + m], q.acc[0][:, b, 0:m], ACT.Copy)\
                       .then_inc(q.sem("free0"), 1)

            def silu_v(i):
                if conv is not None:
                    wait(act, q.sem("conv"), i * CONV + CONV)
                    wait(act, q.sem("tr0"), i * 3)
                    act.activation(xT[0][:, :], cv[:, :], ACT.Silu).then_inc(q.sem("v"), 1)

            def epi_z(i):
                wait(act, q.sem("mm1"), i + 1)
                wait(act, q.sem("tr1"), i * 3)
                for b, (s, m) in enumerate(SPANS):
                    act.activation(xT[1][:, s:s + m], q.acc[1][:, b, 0:m], ACT.Silu).then_inc(q.sem("free1"), 1)
            for j in range(2):
                q.split_hi(act, 0, j)
            with act.Fori(0, n - 1) as i:
                epi_v(i)
                q.split_hi(act, i + 1, 0)
                silu_v(i)
                epi_z(i)
                q.split_hi(act, i + 1, 1)
            epi_v(n - 1)
            silu_v(n - 1)
            epi_z(n - 1)

        @block.gpsimd
        def _(pool):
            for j in range(2):
                q.split_lo(pool, 0, j)
            with pool.Fori(1, n) as i:
                for j in range(2):
                    q.split_lo(pool, i, j)

        @block.tensor
        def _(pe):
            def tr(i, j):
                if j == 0:
                    wait(pe, q.sem("free0") if conv is None else q.sem("v"), i * 3 + 3 if conv is None else i + 1)
                    wait(pe, q.sem("ev1"), i * 3)
                else:
                    wait(pe, q.sem("zw"), i + 1)
                    wait(pe, q.sem("ev0"), i * 3 + 3)
                for b in range(3):
                    wait(pe, q.sem(f"ev{j}"), i * 3 if b == 0 else i * 3 + b - 1)
                    transpose_out(pe, q, xT[j], b, T.eye, q.sem(f"tr{j}"))
            q.mm(pe, 0, 0, 3)
            q.mm(pe, 0, 1, 3)
            tr(0, 0)
            with pe.Fori(1, n) as i:
                q.mm(pe, i, 0, 3)
                tr(i - 1, 1)
                q.mm(pe, i, 1, 3)
                tr(i, 0)
            tr(n - 1, 1)

        @block.vector
        def _(dve):
            if conv is not None:
                dve.memset(xs[:, 0:CONV - 1], 0.0).then_inc(q.sem("xs_zero"), 1)
                dve.wait_ge(q.sem("xs_zero"), 1)

            def ev(i, j):
                wait(dve, q.sem(f"tok_out{j}"), i * 32)
                for b in range(3):
                    wait(dve, q.sem(f"tr{j}"), i * 3 + b + 1)
                    evacuate_out(dve, dve.tensor_copy, q, tok[j], b, q.sem(f"ev{j}"))

            def epi(i):
                if conv is not None:
                    wait(dve, q.sem("free0"), i * 3 + 3)
                    wait(dve, q.sem("v"), i)
                    convolve(dve, cv, xs, T.cw, conv, i, q.sem("conv"))

            def weigh(i):
                wait(dve, q.sem("free1"), i * 3 + 3)
                dve.tensor_scalar(xT[1][:, :], xT[1][:, :], hnw[:, ds(i)], None, ALU.mult).then_inc(q.sem("zw"), 1)
            epi(0)
            ev(0, 0)
            weigh(0)
            with dve.Fori(1, n) as i:
                epi(i)
                ev(i - 1, 1)
                ev(i, 0)
                weigh(i)
            ev(n - 1, 1)


def convolve(dve, cv, xs, cw, tile0, i, done):
    def w(tap):
        return cw[:, tap, ds(i + tile0)]
    dve.tensor_scalar(cv[:, :], xs[:, 0:L], w(0), None, ALU.mult).then_inc(done, 1)
    for tap in range(1, CONV):
        wait(dve, done, i * CONV + tap)
        dve.scalar_tensor_tensor(cv[:, :], xs[:, tap:tap + L], w(tap), cv[:, :], ALU.mult, ALU.add).then_inc(done, 1)


class Step:

    def __init__(self, t, j, n):
        self.t, self.j, self.n = t, j, n

    def back(self):
        return Step(self.t - 1, 1 - self.j, self.n if self.j else self.n - 1)


def over_steps(eng, body, tail):
    body(Step(0, 0, 0), False, False)
    body(Step(1, 1, 0), True, False)
    with eng.Fori(0, (NT - 3) // 2) as i:
        body(Step(i * 2 + 2, 0, i + 1), True, True)
        body(Step(i * 2 + 3, 1, i + 1), True, True)
    last = NT - 1
    body(Step(last, 0, last // 2), True, True)
    tail(Step(last, 0, last // 2))


def split_w_out(nc, S, T, tag, w_out, kts, whi, wlo, stage):
    w = w_out.rearrange("(k p) n -> p k n", p=P)

    def load(sp):
        for k in range(kts):
            wait(sp, S(f"{tag}_wlo"), k - 1)
            wait(sp, S(f"{tag}_whi"), k - 1)
            sp.dma_start(stage[k % 2], w[:, k, :]).then_inc(S(f"{tag}_w_in{k % 2}"), 16)

    def hi(act):
        for k in range(kts):
            act.wait_ge(S(f"{tag}_w_in{k % 2}"), 16 * (k // 2 + 1))
            act.activation(whi[:, k, :], stage[k % 2], ACT.Copy).then_inc(S(f"{tag}_whi"), 1)

    def lo(pool):
        for k in range(kts):
            pool.wait_ge(S(f"{tag}_w_in{k % 2}"), 16 * (k // 2 + 1))
            pool.wait_ge(S(f"{tag}_whi"), k + 1)
            pool.tensor_tensor(wlo[:, k, :], stage[k % 2], whi[:, k, :].bitcast(F32), ALU.subtract)\
                .then_inc(S(f"{tag}_wlo"), 1)
    return load, hi, lo


def gla_scan(nc, S, T, w_out, x, meta, next_norm):
    with ExitStack() as ctx:
        def sb(name, shape, dt=F32):
            return ctx.enter_context(nc.sbuf_tensor(name, shape, dt))

        def ps(name, shape):
            return ctx.enter_context(nc.psum_tensor(name, shape, F32))
        whi = sb("as_whi", [P, KT, D], F32R)
        wlo = sb("as_wlo", [P, KT, D], F32R)
        qk = [sb(f"as_qk{j}", [P, GH, 2, P]) for j in range(2)]
        ko = [sb(f"as_ko{j}", [P, GH, P]) for j in range(2)]
        v = [sb(f"as_v{j}", [P, GH, GDV]) for j in range(2)]
        z = [sb(f"as_z{j}", [P, GH, GDV]) for j in range(2)]
        hres = [sb(f"as_res{j}", [P, D]) for j in range(2)]
        St = [sb(f"as_s{j}", [P, GH, GDV]) for j in range(2)]
        decs = sb("as_dec", [P, GH, 2])
        at = sb("as_at", [P, GH, P])
        og = sb("as_og", [P, GH, GDV])
        oT_hi = sb("as_othi", [P, KT, P], F32R)
        oT_lo = sb("as_otlo", [P, KT, P], F32R)
        hn = sb("as_hn", [P, D])
        junk = sb("as_junk", [P, GDV])
        nw = sb("as_nw", [P, D])
        ss = sb("as_ss", [P, GH])
        rs = sb("as_rs", [P, GH])
        ss2 = sb("as_ss2", [P, 1])
        rs2 = sb("as_rs2", [P, 1])
        pA = ps("as_pA", [P, GH, P])
        pO = ps("as_pO", [P, GH, GDV])
        pU = ps("as_pU", [P, GH, GDV])
        pT = ps("as_pT", [P, GH, P])
        pY = ps("as_pY", [P, 2, 512])
        bank = [pT, pA]
        w_load, w_hi, w_lo = split_w_out(nc, S, T, "as", w_out, KT, whi, wlo, [og[:, :, :].rearrange("p h v -> p (h v)"), hn[:, :]])
        block = ctx.enter_context(nc.Block())
        NLOAD = 5

        @block.sync
        def _(sp):
            sp.wait_ge(S("as_hzero"), 1)
            sp.dma_start(nw[:, :], bc(next_norm, [P, D])).then_inc(S("as_nw_in"), 16)

            def load(s):
                t, j = s.t, s.j
                sem = S(f"as_in{j}")
                wait(sp, S("as_hn"), t - 1)
                wait(sp, S("as_inter"), t * 2 - 2)
                wait(sp, S("as_og"), t * 4 - 4)
                sp.dma_start(qk[j][:, :, :, :].rearrange("p h w n -> p (h w) n"),
                             T.gla_qk.rearrange("h w p n -> p (h w) n")[:, :, ds(t * P, P)]).then_inc(sem, 16)
                sp.dma_start(ko[j][:, :, :].rearrange("p h d -> p (h d)"), T.gla_ko[ds(t * P, P), :]).then_inc(sem, 16)
                sp.dma_start(v[j][:, :, :].rearrange("p h d -> p (h d)"), T.gla_v[ds(t * P, P), :]).then_inc(sem, 16)
                sp.dma_start(z[j][:, :, :].rearrange("p h d -> p (h d)"), T.gla_z[ds(t * P, P), :]).then_inc(sem, 16)
                if isinstance(t, int) and t == 0:
                    sp.dma_start(hres[0][PAD:P, :], meta).then_inc(sem, 16)
                else:
                    wait(sp, S("as_h1_out"), t * 16 - 16)
                    sp.dma_start(hres[j][:, :], x[ds((t - 1) * P, P), :]).then_inc(sem, 16)

            def store(s):
                wait(sp, S("as_h1"), s.t * 2 + 2)
                sp.dma_start(T.h1[ds(s.t * P, P), :], hres[s.j][:, :]).then_inc(S("as_h1_out"), 16)

            load(Step(0, 0, 0))
            w_load(sp)
            load(Step(1, 1, 0))
            with sp.Fori(0, (NT - 3) // 2) as i:
                store(Step(i * 2, 0, i))
                load(Step(i * 2 + 2, 0, i + 1))
                store(Step(i * 2 + 1, 1, i))
                load(Step(i * 2 + 3, 1, i + 1))
            store(Step(NT - 3, 0, (NT - 3) // 2))
            load(Step(NT - 1, 0, (NT - 1) // 2))
            for t in range(NT - 2, NT):
                store(Step(t, t % 2, t // 2))
            sp.wait_ge(S("as_h1_out"), 16 * NT)

        @block.tensor
        def _(pe):
            pe.wait_ge(S("as_init"), 2)

            def arrived(s):
                wait(pe, S(f"as_in{s.j}"), s.n * (16 * NLOAD) + 16 * NLOAD)

            def outer(s, ch):
                wait(pe, S("as_su"), s.t * 8 + 4 * ch)
                r = slice(ch * C, ch * C + C)
                for h in range(GH):
                    mm = pe.matmul(pU[:, h, :], ko[s.j][r, h, :], v[s.j][r, h, :], start=True, stop=True)
                mm.then_inc(S("as_u"), 1)

            def inter(s, ch):
                wait(pe, S("as_su"), s.t * 8 + 4 * ch)
                r = slice(ch * C, ch * C + C)
                for h in range(GH):
                    mm = pe.matmul(pO[r, h, :], qk[s.j][:, h, 0, r], St[ch][:, h, :], start=False, stop=True,
                                   skip_group_check=True)
                mm.then_inc(S("as_inter"), 1)

            def transposes(src, name, s, before):
                for b in range(2):
                    wait(pe, *before(b))
                    for c in range(4):
                        kt = 4 * b + c
                        mm = pe.transpose(bank[b][:, c, :], src[:, kt * P:(kt + 1) * P], T.eye)
                    mm.then_inc(S(name), 1)

            def scan(s, has2):
                arrived(s)
                wait(pe, S("as_otlo"), s.t * 2)
                for h in range(GH):
                    mm = pe.matmul(pA[:, h, :], qk[s.j][:, h, 1, :], qk[s.j][:, h, 0, :], start=True, stop=True)
                mm.then_inc(S("as_a"), 1)
                outer(s, 0)
                if has2:
                    norm_out(s.back().back(), s)
                wait(pe, S("as_at"), s.t + 1)
                wait(pe, S("as_og"), s.t * 4)
                for h in range(GH):
                    mm = pe.matmul(pO[:, h, :], at[:, h, :], v[s.j][:, h, :], start=(h % 2 == 0), stop=False,
                                   skip_group_check=True)
                inter(s, 0)
                outer(s, 1)
                inter(s, 1)

            def norm_out(s2, s):
                wait(pe, S("as_hn"), s2.t + 1)
                ogs = hn[:, :]
                for b in range(2):
                    if b == 1 and s is not None:
                        wait(pe, S("as_at"), s.t + 1)
                    if b == 0:
                        wait(pe, S("as_otlo"), s2.t * 2 + 4 if s is not None else NT * 2)
                    if s is None:
                        wait(pe, S("as_hnlo"), s2.t * 2 + b - 1 if b else s2.t * 2)
                    for c in range(4):
                        kt = 4 * b + c
                        mm = pe.transpose(bank[b][:, c, :], ogs[:, kt * P:(kt + 1) * P], T.eye)
                    mm.then_inc(S("as_hnT"), 1)

            def out_project(s):
                wait(pe, S("as_otlo"), s.t * 2 + 2)
                wait(pe, S("as_h1"), s.t * 2)
                for n in range(2):
                    k = 0
                    for kt in range(KT):
                        for o, w in ((oT_hi, whi), (oT_hi, wlo), (oT_lo, whi)):
                            mm = pe.matmul(pY[:, n, :], o[:, kt, :], w[:, kt, n * 512:(n + 1) * 512],
                                           start=(k == 0), stop=(k == 3 * KT - 1))
                            k += 1
                    mm.then_inc(S("as_y"), 1)

            def outputs(s, has2):
                wait(pe, S("as_og"), s.t * 4 + 4)
                if has2:
                    wait(pe, S("as_hnlo"), s.t * 2 - 2)
                for b in range(2):
                    if b == 1:
                        wait(pe, S("as_at"), s.t + 1)
                    for c in range(4):
                        kt = 4 * b + c
                        mm = pe.transpose(bank[b][:, c, :], og[:, kt // 2, (kt % 2) * P:(kt % 2 + 1) * P], T.eye)
                    mm.then_inc(S("as_oT"), 1)

            def body(s, has1, has2):
                scan(s, has2)
                if has1:
                    if not has2:
                        pe.wait_ge(S("as_wlo"), KT)
                    out_project(s.back())
                outputs(s, has2)

            def tail(s):
                norm_out(s.back(), None)
                out_project(s)
                norm_out(s, None)
            over_steps(pe, body, tail)

        @block.vector
        def _(dve):
            dve.memset(at[:, :, :], 0.0).then_inc(S("as_init"), 1)
            dve.memset(St[0][:, :, :], 0.0).then_inc(S("as_init"), 1)
            dve.memset(hres[0][:, :], 0.0).then_inc(S("as_hzero"), 1)
            dve.wait_ge(S("as_init"), 2)
            dve.wait_ge(S("as_nw_in"), 16)

            def update(s, ch):
                wait(dve, S("as_u"), s.t * 2 + ch + 1)
                if ch:
                    wait(dve, S("as_inter"), s.t * 2 + 1)
                    wait(dve, S("as_su"), s.t * 8 + 4)
                else:
                    wait(dve, S("as_inter"), s.t * 2)
                    wait(dve, S("as_dec"), s.t + 1)
                    wait(dve, S("as_su"), s.t * 8)
                for h in range(GH):
                    dve.scalar_tensor_tensor(St[1 - ch][:, h, :], St[ch][:, h, :], decs[:, h, ch:ch + 1],
                                             pU[:, h, :], ALU.mult, ALU.add).then_inc(S("as_su"), 1)

            def low(dst, hi, t, name, pre):
                for b in range(2):
                    wait(dve, S(f"as_{pre}hi"), t * 2 + b + 1)
                    dve.tensor_tensor(dst(b), bank[b][:, :, :], hi(b).bitcast(F32), ALU.subtract)\
                       .then_inc(S(f"as_{pre}lo"), 1)

            def norm_low(s):
                low(lambda b: T.hn_lo[:, 4 * b:4 * b + 4, ds(s.t * P, P)],
                    lambda b: T.hn_hi[:, 4 * b:4 * b + 4, ds(s.t * P, P)], s.t, "hn", "hn")

            def residual(s):
                for n in range(2):
                    wait(dve, S("as_y"), s.t * 2 + n + 1)
                    dve.tensor_tensor(hres[s.j][:, n * 512:(n + 1) * 512], pY[:, n, :],
                                      hres[s.j][:, n * 512:(n + 1) * 512], ALU.add).then_inc(S("as_h1"), 1)

            def normed(s):
                wait(dve, S("as_rs2"), s.t + 1)
                wait(dve, S("as_h1"), s.t * 2 + 2)
                wait(dve, S("as_hnT"), s.t * 2)
                dve.scalar_tensor_tensor(hn[:, :], hres[s.j][:, :], rs2[:, 0:1], nw[:, :], ALU.mult, ALU.mult)\
                   .then_inc(S("as_hn"), 1)

            def body(s, has1, has2):
                wait(dve, S("as_su"), s.t * 8)
                dve.tensor_copy(decs[:, :, :], T.dec[:, :, ds(s.t * 2, 2)]).then_inc(S("as_dec"), 1)
                waits_apart(dve, T.dve_carrier,
                            (S("as_a"), s.t + 1),
                            (S("as_inter"), s.t * 2))
                dve.copy_predicated(at[:, :, :], bc(T.causal.bitcast(I32), [P, GH, P]), pA[:, :, :])\
                   .then_inc(S("as_at"), 1)
                update(s, 0)
                if has2:
                    norm_low(s.back().back())
                update(s, 1)
                wait(dve, S("as_rs"), s.t + 1)
                wait(dve, S("as_in%d" % s.j), s.n * (16 * NLOAD) + 16 * NLOAD)
                wait(dve, S("as_oT"), s.t * 2)
                if not has1:
                    dve.wait_ge(S("as_wlo"), KT)
                for h in range(GH):
                    dve.scalar_tensor_tensor(og[:, h, :], pO[:, h, :], rs[:, h:h + 1], z[s.j][:, h, :],
                                             ALU.mult, ALU.mult).then_inc(S("as_og"), 1)
                if has1:
                    residual(s.back())
                low(lambda b: oT_lo[:, 4 * b:4 * b + 4, :], lambda b: oT_hi[:, 4 * b:4 * b + 4, :], s.t, "ot", "ot")
                if has1:
                    normed(s.back())

            def tail(s):
                norm_low(s.back())
                residual(s)
                normed(s)
                norm_low(s)
            over_steps(dve, body, tail)

        @block.scalar
        def _(act):
            w_hi(act)

            def high(dst, s, name):
                for b in range(2):
                    wait(act, S(name), s.t * 2 + b + 1)
                    act.activation(dst(b), bank[b][:, :, :], ACT.Copy)\
                       .then_inc(S("as_othi" if name == "as_oT" else "as_hnhi"), 1)

            def norm_high(s):
                high(lambda b: T.hn_hi[:, 4 * b:4 * b + 4, ds(s.t * P, P)], s, "as_hnT")

            def squares2(s):
                wait(act, S("as_h1"), s.t * 2 + 2)
                wait(act, S("as_mean2"), s.t)
                wait(act, S("as_hnT"), s.t * 2)
                act.activation(hn[:, :], hres[s.j][:, :], ACT.Square, accum_out=ss2[:, :]).then_inc(S("as_ss2"), 1)

            def body(s, has1, has2):
                if has2:
                    norm_high(s.back().back())
                wait(act, S("as_inter"), s.t * 2 + 2)
                wait(act, S("as_mean"), s.t)
                for h in range(GH):
                    wait(act, S("as_ss"), s.t * 4 + h)
                    act.activation(junk[:, :], pO[:, h, :], ACT.Square, accum_out=ss[:, h:h + 1])\
                       .then_inc(S("as_ss"), 1)
                wait(act, S("as_y"), s.t * 2)
                high(lambda b: oT_hi[:, 4 * b:4 * b + 4, :], s, "as_oT")
                if has1:
                    squares2(s.back())

            def tail(s):
                norm_high(s.back())
                squares2(s)
                norm_high(s)
            over_steps(act, body, tail)

        @block.gpsimd
        def _(pool):
            w_lo(pool)

            def rsqrt(dst, src, width, t, ready, mean, out, used):
                waits_apart(pool, T.pool_carrier,
                            ready,
                            used)
                pool.tensor_scalar(dst[:, :], src[:, :], 1.0 / width, EPS, ALU.mult, ALU.add).then_inc(S(mean), 1)
                wait(pool, S(mean), t + 1)
                pool.tensor_tensor(dst[:, :], dst[:, :], bc(T.minus_half[:, 0:1], list(dst.shape)), ALU.pow)\
                    .then_inc(S(out), 1)

            def rs_h1(s):
                rsqrt(rs2, ss2, D, s.t, (S("as_ss2"), s.t + 1), "as_mean2", "as_rs2", (S("as_hn"), s.t))

            def body(s, has1, has2):
                rsqrt(rs, ss, GDV, s.t, (S("as_ss"), s.t * 4 + 4), "as_mean", "as_rs", (S("as_og"), s.t * 4))
                if has1:
                    rs_h1(s.back())

            def tail(s):
                rs_h1(s)
            over_steps(pool, body, tail)


def gdn_gate(nc, S, T, w_in, a_log, dt_bias, conv_w, head_norm):
    with ExitStack() as ctx:
        def sb(name, shape, dt=F32):
            return ctx.enter_context(nc.sbuf_tensor(name, shape, dt))
        st = sb("ng_w", [P, KT, P])
        hi = sb("ng_whi", [P, KT, P], F32R)
        lo = sb("ng_wlo", [P, KT, P], F32R)
        al = sb("ng_alog", [NH, 1])
        ea = sb("ng_ea", [NH, 1])
        dt = sb("ng_dt", [NH, 1])
        cm = sb("ng_starts", [NH, L])
        ax = sb("ng_ax", [NH, L])
        mx = sb("ng_mx", [NH, L])
        g = sb("ng_g", [NH, L])
        be = sb("ng_beta", [NH, L])
        NCT = (2 * NQK + NV) // P
        cwn = sb("ng_cw", [NCT, CONV, P])
        acc = ctx.enter_context(nc.psum_tensor("ng_acc", [P, 3, 512], F32))
        cps = ctx.enter_context(nc.psum_tensor("ng_cps", [P, CONV, NCT], F32))
        block = ctx.enter_context(nc.Block())
        c0 = 2 * NQK + 2 * NV
        A0 = 32
        wv = w_in.rearrange("(k p) n -> p k n", p=P)

        @block.sync
        def _(sp):
            sp.wait_ge(S("ng_zero"), 1)
            sp.dma_start(st[:, :, 0:NH], wv[:, :, c0:c0 + NH]).then_inc(S("ng_w_in"), 16)
            sp.dma_start(st[:, :, A0:A0 + NH], wv[:, :, c0 + NH:c0 + 2 * NH]).then_inc(S("ng_w_in"), 16)
            sp.dma_start(al[:, :], a_log.rearrange("(h o) -> h o", o=1)).then_inc(S("ng_small_in"), 16)
            sp.dma_start(dt[:, :], dt_bias.rearrange("(h o) -> h o", o=1)).then_inc(S("ng_small_in"), 16)
            sp.dma_start(cm[:, :], T.starts_dram[0:NH, :]).then_inc(S("ng_small_in"), 16)
            sp.dma_start(cwn[:, :, :], conv_w.rearrange("k (t p) -> t k p", p=P)).then_inc(S("ng_cw_in"), 16)
            sp.dma_start(T.hnw2[:, :], head_norm).then_inc(S("ng_hnw_in"), 16)
            sp.wait_ge(S("ng_g"), 1)
            sp.wait_ge(S("ng_beta"), 4)
            for w, src in ((0, g), (1, be)):
                sp.dma_start(T.gb[2:, :, w, :].rearrange("c h t -> h c t"),
                             src[:, NMETA:].rearrange("h (c t) -> h c t", t=C)).then_inc(S("ng_out"), 16)
                sp.dma_start(T.gb[1, :, w, C - NMETA:C], src[:, 0:NMETA]).then_inc(S("ng_out"), 16)
            sp.wait_ge(S("ng_out"), 64)
            sp.wait_ge(S("ng_hnw_in"), 16)

        @block.scalar
        def _(act):
            act.wait_ge(S("ng_w_in"), 32)
            act.activation(hi[:, :, :], st[:, :, :], ACT.Copy).then_inc(S("ng_whi"), 1)
            act.wait_ge(S("ng_small_in"), 48)
            act.activation(ea[:, :], al[:, :], ACT.Exp).then_inc(S("ng_ea"), 1)
            act.wait_ge(S("ng_logit"), 1)
            act.wait_ge(S("ng_abs"), 1)
            for b, (s, m) in enumerate(SPANS):
                act.activation(be[:, s:s + m], acc[0:NH, b, 0:m], ACT.Exp, scale=-1.0).then_inc(S("ng_ebeta"), 1)
            act.activation(ax[:, :], ax[:, :], ACT.Exp, scale=-1.0).then_inc(S("ng_e"), 1)
            act.wait_ge(S("ng_e"), 1)
            act.activation(ax[:, :], ax[:, :], ACT.Ln, bias=1.0).then_inc(S("ng_ln"), 1)

        @block.gpsimd
        def _(pool):
            pool.memset(st[:, :, :], 0.0).then_inc(S("ng_zero"), 1)
            pool.wait_ge(S("ng_whi"), 1)
            pool.tensor_tensor(lo[:, :, :], st[:, :, :], hi[:, :, :].bitcast(F32), ALU.subtract)\
                .then_inc(S("ng_wlo"), 1)

        @block.tensor
        def _(pe):
            pe.wait_ge(S("ng_cw_in"), 16)
            for k in range(CONV):
                mm = pe.transpose(cps[:, k, :], cwn[:, k, :], T.k[0:NCT, K_EYE:K_EYE + NCT])
            mm.then_inc(S("ng_cwT"), 1)
            pe.wait_ge(S("ng_wlo"), 1)
            project(pe, acc, hi, lo, T).then_inc(S("ng_logit"), 1)

        @block.vector
        def _(dve):
            dve.wait_ge(S("ng_cwT"), 1)
            dve.tensor_copy(T.cw[:, :, :], cps[:, :, :]).then_inc(S("ng_cw"), 1)
            dve.wait_ge(S("ng_logit"), 1)
            dve.wait_ge(S("ng_small_in"), 48)
            for b, (s, m) in enumerate(SPANS):
                dve.tensor_scalar(mx[:, s:s + m], acc[A0:A0 + NH, b, 0:m], dt[:, 0:1], 0.0, ALU.add, ALU.max)\
                   .then_inc(S("ng_max"), 1)
            for b, (s, m) in enumerate(SPANS):
                dve.tensor_scalar(ax[:, s:s + m], acc[A0:A0 + NH, b, 0:m], dt[:, 0:1], 0.0, ALU.add, ALU.min)\
                   .then_inc(S("ng_min"), 1)
            dve.wait_ge(S("ng_max"), 3)
            dve.wait_ge(S("ng_min"), 3)
            dve.tensor_tensor(ax[:, :], mx[:, :], ax[:, :], ALU.subtract).then_inc(S("ng_abs"), 1)
            dve.wait_ge(S("ng_ebeta"), 3)
            dve.tensor_scalar(be[:, :], be[:, :], 1.0, None, ALU.add).then_inc(S("ng_beta"), 1)
            dve.wait_ge(S("ng_beta"), 1)
            dve.reciprocal(be[:, :], be[:, :]).then_inc(S("ng_beta"), 3)
            dve.wait_ge(S("ng_ln"), 1)
            dve.wait_ge(S("ng_max"), 3)
            dve.wait_ge(S("ng_ea"), 1)
            dve.tensor_tensor(mx[:, :], mx[:, :], ax[:, :], ALU.add).then_inc(S("ng_sp"), 1)
            dve.wait_ge(S("ng_sp"), 1)
            dve.tensor_scalar(mx[:, :], mx[:, :], ea[:, 0:1], -1.0, ALU.mult, ALU.mult).then_inc(S("ng_sp"), 1)
            dve.wait_ge(S("ng_sp"), 2)
            dve.tensor_tensor_scan(g[:, :], cm[:, :], mx[:, :], 0.0, ALU.mult, ALU.add).then_inc(S("ng_g"), 1)


def gdn_qk(nc, S, T, w_in):
    n = NH
    with ExitStack() as ctx:
        q = Proj(nc, S, T, ctx, "nq", w_in, lambda i, j: j * NQK + i * P)

        def sb(name, shape):
            return ctx.enter_context(nc.sbuf_tensor(name, shape, F32))
        xs = sb("nq_xs", [P, CONV - 1 + L])
        cv = sb("nq_cv", [P, L])
        xT = [sb(f"nq_x{j}", [P, L]) for j in range(2)]
        tok = [sb(f"nq_tok{j}", [P, NT, P]) for j in range(2)]
        sq = sb("nq_sq", [P, NT, P])
        ss = [sb(f"nq_ss{j}", [P, NT]) for j in range(2)]
        xn = [sb(f"nq_xn{j}", [P, L]) for j in range(2)]
        block = ctx.enter_context(nc.Block())

        @block.sync
        def _(sp):
            def store_tok(i):
                wait(sp, q.sem("norm1"), i + 1)
                store_tokens(sp, T.gdn_k, tok[1], i * P, NQK, q.sem("tok_out"))

            def store(i, j):
                wait(sp, q.sem(f"evn{j}"), i * 3 + 3)
                sp.dma_start(T.gdn_qk[j, ds(i), :, PAD:TP].rearrange("a p n -> p (a n)"), xn[j][:, :])\
                  .then_inc(q.sem(f"out{j}"), 16)
            for j in range(2):
                q.load(sp, 0, j)
            for j in range(2):
                q.load(sp, 1, j)
            with sp.Fori(0, n - 2) as i:
                for j in range(2):
                    q.load(sp, i + 2, j)
                store_tok(i)
                for j in range(2):
                    store(i, j)
            for i in range(n - 2, n):
                store_tok(i)
                for j in range(2):
                    store(i, j)
            sp.wait_ge(q.sem("tok_out"), 32 * n)
            for j in range(2):
                sp.wait_ge(q.sem(f"out{j}"), 16 * n)

        @block.scalar
        def _(act):
            def copy(i, j):
                wait(act, q.sem(f"mm{j}"), i + 1)
                if j == 0:
                    wait(act, q.sem("conv1"), i * CONV)
                else:
                    wait(act, q.sem("conv0"), i * CONV + CONV)
                for b, (s, m) in enumerate(SPANS):
                    act.activation(xs[:, CONV - 1 + s:CONV - 1 + s + m], q.acc[j][:, b, 0:m], ACT.Copy)\
                       .then_inc(q.sem(f"free{j}"), 1)

            def silu(i, j):
                wait(act, q.sem(f"conv{j}"), i * CONV + CONV)
                wait(act, q.sem(f"tr{j}"), i * 3)
                act.activation(xT[j][:, :], cv[:, :], ACT.Silu).then_inc(q.sem(f"silu{j}"), 1)

            def square(i, j):
                wait(act, q.sem(f"ev{j}"), i * 3 + 3)
                if j == 0:
                    wait(act, q.sem("ss1"), i)
                else:
                    wait(act, q.sem("ss0"), i + 1)
                act.activation(sq[:, :, :], tok[j][:, :, :], ACT.Square).then_inc(q.sem(f"sq{j}"), 1)

            def back(i, j):
                wait(act, q.sem(f"out{j}"), i * 16)
                for b in range(3):
                    wait(act, q.sem(f"trn{j}"), i * 3 + b + 1)
                    if b < 2:
                        s = NMETA + 4 * b * P
                        act.activation(xn[j][:, s:s + 4 * P], (q.trA, q.trB)[b][:, :, :].rearrange("p a b -> p (a b)"),
                                       ACT.Copy).then_inc(q.sem(f"evn{j}"), 1)
                    else:
                        act.activation(xn[j][:, 0:NMETA], q.trA[:, 0, 0:NMETA], ACT.Copy).then_inc(q.sem(f"evn{j}"), 1)

            def body(i, first, last):
                copy(i, 0)
                if not last:
                    q.split_hi(act, i + 1, 0)
                if not first:
                    square(i - 1, 1)
                    back(i - 1, 0)
                silu(i, 0)
                copy(i, 1)
                if not last:
                    q.split_hi(act, i + 1, 1)
                square(i, 0)
                if not first:
                    back(i - 1, 1)
                silu(i, 1)
            for j in range(2):
                q.split_hi(act, 0, j)
            body(0, True, False)
            with act.Fori(1, n - 1) as i:
                body(i, False, False)
            body(n - 1, False, True)
            square(n - 1, 1)
            back(n - 1, 0)
            back(n - 1, 1)

        @block.gpsimd
        def _(pool):
            def norm(i, j):
                waits_apart(pool, T.pool_carrier,
                            (q.sem(f"ss{j}"), i + 1))
                pool.tensor_scalar(ss[j][:, :], ss[j][:, :], EPS, (float(NDK), 1.0)[j], ALU.add, ALU.mult)\
                    .then_inc(q.sem(f"sum{j}"), 1)
                wait(pool, q.sem(f"sum{j}"), i + 1)
                pool.tensor_tensor(ss[j][:, :], ss[j][:, :], bc(T.minus_half[:, 0:1], [P, NT]), ALU.pow)\
                    .then_inc(q.sem(f"rs{j}"), 1)
                wait(pool, q.sem(f"rs{j}"), i + 1)
                pool.tensor_tensor(tok[j][:, :, :], tok[j][:, :, :],
                                   bc(ss[j][:, :].rearrange("p (t o) -> p t o", o=1), [P, NT, P]), ALU.mult)\
                    .then_inc(q.sem(f"norm{j}"), 1)

            def body(i, first, last):
                if not last:
                    q.split_lo(pool, i + 1, 0)
                if not first:
                    norm(i - 1, 1)
                if not last:
                    q.split_lo(pool, i + 1, 1)
                norm(i, 0)
            for j in range(2):
                pool.memset(tok[j][:, :, :], 0.0).then_inc(q.sem("tok_zero"), 1)
            for j in range(2):
                q.split_lo(pool, 0, j)
            body(0, True, False)
            with pool.Fori(1, n - 1) as i:
                body(i, False, False)
            body(n - 1, False, True)
            norm(n - 1, 1)

        @block.tensor
        def _(pe):
            def tr(i, j):
                wait(pe, q.sem(f"silu{j}"), i + 1)
                if j == 1:
                    wait(pe, q.sem("ev0"), i * 3 + 3)
                    wait(pe, q.sem("evn1"), i * 3)
                else:
                    wait(pe, q.sem("ev1"), i * 3)
                    wait(pe, q.sem("evn0"), i * 3)
                for b in range(3):
                    if b == 2:
                        wait(pe, q.sem(f"ev{j}"), i * 3 + 1)
                    transpose_out(pe, q, xT[j], b, T.eye, q.sem(f"tr{j}"))

            def back(i, j):
                wait(pe, q.sem(f"norm{j}"), i + 1)
                yield_to = q.sem("ev1") if j == 0 else q.sem("ev0")
                wait(pe, yield_to, i * 3 + 3 if j == 0 else (i * 3 + 6 if not isinstance(i, int) else min(i * 3 + 6, 3 * n)))
                if j == 1:
                    wait(pe, q.sem("evn0"), i * 3 + 3)
                for b in range(3):
                    if b == 2:
                        waits_apart(pe, T.pe_carrier,
                                    (q.sem(f"evn{j}"), i * 3 + 1))
                    bankd = (q.trA, q.trB, q.trA)[b]
                    if b < 2:
                        for c in range(4):
                            mm = pe.transpose(bankd[:, c, :], tok[j][:, 1 + 4 * b + c, :], T.eye)
                    else:
                        mm = pe.transpose(bankd[:, 0, 0:NMETA], tok[j][0:NMETA, 0, :],
                                          T.k[0:NMETA, K_EYE:K_EYE + NMETA])
                    mm.then_inc(q.sem(f"trn{j}"), 1)
            q.mm(pe, 0, 0, 3)
            q.mm(pe, 0, 1, 3)
            tr(0, 0)
            with pe.Fori(1, n) as i:
                q.mm(pe, i, 0, 3)
                tr(i - 1, 1)
                back(i - 1, 0)
                q.mm(pe, i, 1, 3)
                tr(i, 0)
                back(i - 1, 1)
            tr(n - 1, 1)
            back(n - 1, 0)
            back(n - 1, 1)

        @block.vector
        def _(dve):
            dve.memset(xs[:, 0:CONV - 1], 0.0).then_inc(q.sem("xs_zero"), 1)
            dve.wait_ge(q.sem("xs_zero"), 1)
            dve.wait_ge(q.sem("tok_zero"), 2)

            def ev(i, j):
                if j == 1:
                    wait(dve, q.sem("tok_out"), i * 32)
                wait(dve, q.sem(f"trn{j}"), i * 3)
                for b in range(3):
                    wait(dve, q.sem(f"tr{j}"), i * 3 + b + 1)
                    evacuate_out(dve, dve.tensor_copy, q, tok[j], b, q.sem(f"ev{j}"))
                wait(dve, q.sem(f"sq{j}"), i + 1)
                wait(dve, q.sem(f"norm{j}"), i)
                dve.tensor_reduce(ss[j][:, :], sq[:, :, :], AX.X, ALU.add).then_inc(q.sem(f"ss{j}"), 1)

            def conv(i, j):
                wait(dve, q.sem(f"free{j}"), i * 3 + 3)
                if j == 0:
                    wait(dve, q.sem("silu1"), i)
                else:
                    wait(dve, q.sem("silu0"), i + 1)
                convolve(dve, cv, xs, T.cw, j * NH, i, q.sem(f"conv{j}"))
            conv(0, 0)
            ev(0, 0)
            conv(0, 1)
            with dve.Fori(1, n) as i:
                ev(i - 1, 1)
                conv(i, 0)
                ev(i, 0)
                conv(i, 1)
            ev(n - 1, 1)


class Chunk:

    def __init__(self, c, j, n):
        self.c, self.m, self.j, self.n = c, c - 1, j, n


def over_chunks(eng, chunk, tail):
    chunk(Chunk(1, 1, 0), None, False)
    chunk(Chunk(2, 0, 0), 1, False)
    chunk(Chunk(3, 1, 1), 1, False)
    with eng.Fori(2, NT) as t:
        chunk(Chunk(t * 2, 0, t - 1), t, True)
        chunk(Chunk(t * 2 + 1, 1, t), t, True)
    tail()


def gdn_scan(nc, S, T, w_out, out_norm, out):
    KO = NV // P
    R = [slice(0, C), slice(C, P)]
    with ExitStack() as ctx:
        def sb(name, shape, dt=F32):
            return ctx.enter_context(nc.sbuf_tensor("ns_" + name, shape, dt))

        def ps(name, shape):
            return ctx.enter_context(nc.psum_tensor("ns_" + name, shape, F32))
        whi = sb("whi", [P, KO, D], F32R)
        wlo = sb("wlo", [P, KO, D], F32R)
        kq = sb("kq", [P, NH, 2, C])
        kqd = sb("kqd", [P, NH, 2, C])
        kt = sb("kt", [P, HP, NDK])
        v = sb("v", [P, HP, NDV])
        og = sb("og", [P, HP, NDV])
        gb = sb("gb", [P, NH, 2, C])
        gp = sb("gp", [P, HP, 2, C])
        tg = kqd[:, 0:HP, :, :]
        gbc = sb("gbc", [P, HP, 2])
        St = sb("s", [P, NH, NDV])
        er = gb[:, :, 0, :]
        d1 = sb("d1", [P, HP, C])
        dn = sb("dn", [P, HP, C])
        dx = sb("dx", [P, HP, C])
        mtf = sb("mtf", [P, HP, C])
        M = sb("m", [P, HP, C])
        low = [mtf] + [sb(f"low{n}", [P, HP, C]) for n in range(1, 1 + len(LEVELS))]
        U = sb("u", [P, HP, C])
        Ti = sb("ti", [P, HP, C])
        Pm = sb("pm", [P, HP, C])
        at = sb("at", [P, HP, C])
        kdl = sb("kdl", [P, HP])
        kdec = kt
        vn = sb("vn", [P, HP, NDV])
        oT_hi = sb("othi", [P, KO, P], F32R)
        oT_lo = sb("otlo", [P, KO, P], F32R)
        h = sb("h", [P, D])
        nw = sb("nw", [P, D])
        junk = sb("junk", [P, NDV])
        ss = sb("ss", [P, HP])
        ss2 = sb("ss2", [P, 1])
        pX = [ps(f"px{p}", [P, HP, NDV]) for p in range(2)]
        p4 = ps("p4", [P, 512])
        p56 = ps("p56", [P, 2, 512])
        pY = ps("py", [P, 512])
        pKK = p4[:, 0:HP * C].rearrange("p (h c) -> p h c", c=C)
        pQK = p4[:, HP * C:2 * HP * C].rearrange("p (h c) -> p h c", c=C)
        pUP = p56[:, 0, 0:HP * C].rearrange("p (h c) -> p h c", c=C)
        pPT = p56[:, 1, 0:HP * C].rearrange("p (h c) -> p h c", c=C)
        pV = p56[:, :, :].rearrange("p b (h v) -> p (b h) v", v=NDV)
        pS = [p4[:, :].rearrange("p (h v) -> p h v", v=NDV), p56[:, 0, :].rearrange("p (h v) -> p h v", v=NDV)]
        pT = [pX[0][:, 2 * b:2 * b + 2, :].rearrange("p a (d x c) -> p (a d x) c", d=2, c=C) for b in range(2)]
        w_load, w_hi, w_lo = split_w_out(nc, S, T, "ns", w_out, KO, whi, wlo,
                                         [vn[:, :, :].rearrange("p h v -> p (h v)"), h[:, :]])
        block = ctx.enter_context(nc.Block())
        LV = len(LEVELS)

        def eye_p(shape):
            return bc(T.k[:, K_EYEP:K_EYEP + C].rearrange("p (o c) -> p o c", o=1), shape)

        def mask(col):
            return bc(T.k[:, col:col + C].rearrange("p (o c) -> p o c", o=1), [P, HP, C])

        def outputs_after(t, ch):
            return 1 if ch.j == 0 else LV - 2

        @block.sync
        def _(sp):
            sp.dma_start(nw[:, :], bc(out_norm, [P, D])).then_inc(S("ns_nw_in"), 16)

            def tokens(dst, src, ch, width, swap, sem):
                for p in range(2):
                    rows = R[1 - p] if swap else R[p]
                    sp.dma_start(dst[rows, :, :],
                                 src[ds(ch.c * C, C), :].rearrange("t (h p d) -> t h p d", p=2, d=width)[:, :, p, :])\
                      .then_inc(sem, 16)

            def loads(ch, before_z=None):
                m = ch.m
                wait(sp, S("ns_mtf"), m * 2)
                wait(sp, S("ns_kdl"), m)
                wait(sp, S("ns_d1"), m)
                wait(sp, S("ns_tg"), m)
                for p in range(2):
                    src = T.gb[ds(ch.c)].rearrange("o (h p) w c -> o h p w c", p=2)[:, :, p]
                    sp.dma_start(gp[R[p], :, :, :], bc(src, [C, HP, 2, C])).then_inc(S("ns_in_g"), 16)
                wait(sp, S("ns_kqd"), m * 3)
                wait(sp, S("ns_g"), m)
                for w in range(2):
                    for p in range(2):
                        src = T.gdn_qk[w].rearrange("(h p) d n -> d h p n", p=2)[:, :, p, ds(ch.c * C, C)]
                        slot = 1 - w if p == 0 else w
                        sp.dma_start(kq[:, p::2, slot, :], src).then_inc(S("ns_in_kq"), 16)
                if not (isinstance(m, int) and m == 0):
                    wait(sp, S("ns_v"), m)
                tokens(v, T.gdn_v, ch, NDV, False, S("ns_in_v"))
                wait(sp, S("ns_su"), m * 8)
                sp.dma_start(gb[:, :, :, :], bc(T.gb[ds(ch.c)], [P, NH, 2, C])).then_inc(S("ns_in_gb"), 16)
                wait(sp, S("ns_ds"), m * 2)
                tokens(kt, T.gdn_k, ch, NDK, False, S("ns_in_kt"))
                if before_z is not None:
                    before_z()
                wait(sp, S("ns_oT"), m * 2 - 2)
                wait(sp, S("ns_og"), m * 8)
                tokens(og, T.gdn_z, ch, NDV, True, S("ns_in_z"))

            def load_h(t):
                sp.dma_start(h[:, :], T.h1[ds(t * P, P), :]).then_inc(S("ns_in_h"), 16)

            def store_out(t):
                wait(sp, S("ns_final"), t)
                sp.dma_start(out[ds((t - 1) * P, P), :], h[:, :]).then_inc(S("ns_out"), 16)
                wait(sp, S("ns_out"), t * 16)
            loads(Chunk(1, 1, 0))
            w_load(sp)
            loads(Chunk(2, 0, 0))
            loads(Chunk(3, 1, 1))

            def first_h():
                sp.wait_ge(S("ns_wlo"), KO)
                load_h(1)
            loads(Chunk(4, 0, 1), first_h)
            loads(Chunk(5, 1, 2))
            with sp.Fori(3, NT) as t:
                def turn():
                    store_out(t - 2)
                    load_h(t - 1)
                loads(Chunk(t * 2, 0, t - 1), turn)
                loads(Chunk(t * 2 + 1, 1, t))
            store_out(NT - 2)
            load_h(NT - 1)
            store_out(NT - 1)

        @block.tensor
        def _(pe):
            pe.wait_ge(S("ns_init"), 1)

            def pairs():
                for hp in range(HP):
                    for p in range(2):
                        yield hp, p, R[p]

            def fill(stream, k):
                for _ in range(k):
                    if stream:
                        stream.pop(0)()

            def out_stream(t, half):
                steps = []
                n = 3 * KO
                for kk in range(KO):
                    hp, d, x = kk // 4, kk // 2 % 2, kk % 2
                    row = (2 * hp + 1 - x) * 2 + d
                    for o, w in ((oT_hi, whi), (oT_hi, wlo), (oT_lo, whi)):
                        def step(i=len(steps), o=o, w=w, kk=kk, row=row):
                            if i == 0:
                                wait(pe, S("ns_otlo"), t * 4)
                                wait(pe, S("ns_yd"), t * 2 - 2 + half)
                            mm = pe.matmul(pY[:, :], o[:, kk, :], w[:, row, half * 512:half * 512 + 512],
                                           start=(i == 0), stop=(i == n - 1))
                            if i == n - 1:
                                mm.then_inc(S("ns_y"), 1)
                        steps.append(step)
                return steps

            def outputs(m):
                wait(pe, S("ns_og"), m * 8 + 8)
                for b in range(2):
                    for a in range(2):
                        for d in range(2):
                            i0 = (a * 2 + d) * 2
                            mm = pe.transpose(pT[b][:, i0:i0 + 2, :], og[:, 2 * b + a, d * P:(d + 1) * P], T.eye)
                    mm.then_inc(S("ns_oT"), 1)

            def chunk(ch, t, has_prev):
                m, j = ch.m, ch.j
                if t is None:
                    pe.wait_ge(S("ns_wlo"), KO)
                stream = out_stream(t - 1, j) if has_prev else []
                give = (lambda: fill(stream, 4)) if j else (lambda: None)
                wait(pe, S("ns_in_kq"), m * 64 + 64)
                wait(pe, S("ns_su"), m * 8)
                for hp, p, r in pairs():
                    kk_, qq_ = (0, 1) if p == 0 else (1, 0)
                    hd = 2 * hp + p
                    pe.matmul(pKK[r, hp, :], kq[:, hd, kk_, :], kq[:, hd, kk_, :], start=True, stop=True)
                    mm = pe.matmul(pQK[r, hp, :], kq[:, hd, kk_, :], kq[:, hd, qq_, :], start=True, stop=True)
                mm.then_inc(S("ns_g"), 1)
                give()
                for l in range(LV):
                    waits_apart(pe, T.pe_carrier,
                                (S("ns_u"), m * (LV + 1) + l + 1),
                                (S("ns_low"), m * LV + l + 1),
                                (S("ns_at"), (m + 1) if l == 0 else 0))
                    for hp, p, r in pairs():
                        mm = pe.matmul(pKK[r, hp, :], low[l + 1][r, hp, :], U[r, hp, :], start=True, stop=True)
                    mm.then_inc(S("ns_p"), 1)
                    give()
                    waits_apart(pe, T.pe_carrier,
                                (S("ns_pm"), m * LV + l + 1),
                                (S("ns_t"), m * LV + l + 1))
                    for hp, p, r in pairs():
                        mm = pe.matmul(pUP[r, hp, :], Ti[r, hp, :], Pm[r, hp, :], start=True, stop=True)
                    mm.then_inc(S("ns_up"), 1)
                    if l < LV - 1:
                        for hp, p, r in pairs():
                            mm = pe.matmul(pPT[r, hp, :], Pm[r, hp, :], Ti[r, hp, :], start=True, stop=True)
                        mm.then_inc(S("ns_pt"), 1)
                    give()
                    if l == outputs_after(t, ch) and t is not None:
                        if j:
                            fill(stream, len(stream))
                            outputs(m - 1)
                        elif has_prev:
                            outputs(m - 1)
                            give = lambda: fill(stream, 5)
                wait(pe, S("ns_kqd"), m * 3 + 3)
                wait(pe, S("ns_og"), m * 8)
                if t is not None and (j or has_prev):
                    wait(pe, S("ns_otlo"), m * 2 - (2 if True else 0))
                for hp, p, r in pairs():
                    hd = 2 * hp + p
                    mm = pe.matmul(pX[p][:, hp, :], kqd[:, hd, :, :].rearrange("p w c -> p (w c)"), St[:, hd, :],
                                   start=(hp % 2 == 0), stop=False, skip_group_check=True)
                mm.then_inc(S("ns_x"), 1)
                give()
                waits_apart(pe, T.pe_carrier,
                            (S("ns_r"), m * 2 + 2),
                            (S("ns_u"), m * (LV + 1) + LV + 1))
                for hp, p, r in pairs():
                    mm = pe.matmul(pV[r, hp, :], U[r, hp, :], v[r, hp, :], start=True, stop=True)
                mm.then_inc(S("ns_v"), 1)
                give()
                waits_apart(pe, T.pe_carrier,
                            (S("ns_vn"), m + 1))
                for hp, p, r in pairs():
                    mm = pe.matmul(pX[p][R[1 - p], hp, :], at[r, hp, :], vn[r, hp, :], start=False, stop=True,
                                   skip_group_check=True)
                mm.then_inc(S("ns_o"), 1)
                give()
                wait(pe, S("ns_kdec"), m + 1)
                for rnd in range(2):
                    if rnd:
                        wait(pe, S("ns_su"), m * 8 + 4)
                    for a in range(2):
                        for p in range(2):
                            hp = 2 * rnd + a
                            mm = pe.matmul(pS[p][:, a, :], kdec[R[p], hp, :], vn[R[p], hp, :], start=True, stop=True)
                    mm.then_inc(S("ns_ds"), 1)
                    give()
                fill(stream, len(stream))

            def tail():
                outputs(2 * NT - 2)
                for half in range(2):
                    s = out_stream(NT - 1, half)
                    fill(s, len(s))
            over_chunks(pe, chunk, tail)

        @block.scalar
        def _(act):
            w_hi(act)

            def high(m, half):
                for b in range(2):
                    wait(act, S("ns_oT"), (m - 1) * 2 + b + 1)
                    act.activation(oT_hi[:, 8 * b:8 * b + 8, half * C:half * C + C], pT[b], ACT.Copy)\
                       .then_inc(S("ns_othi"), 1)

            def chunk(ch, t, has_prev):
                m, j = ch.m, ch.j
                wait(act, S("ns_dn"), m + 1)
                act.activation(dn[:, :, :], dn[:, :, :], ACT.Exp).then_inc(S("ns_edn"), 1)
                wait(act, S("ns_dx"), m + 1)
                act.activation(dx[:, :, :], dx[:, :, :], ACT.Exp, scale=-1.0).then_inc(S("ns_edx"), 1)
                wait(act, S("ns_kdl"), m + 1)
                act.activation(kdl[:, :], kdl[:, :], ACT.Exp).then_inc(S("ns_ekdl"), 1)
                wait(act, S("ns_in_gb"), m * 16 + 16)
                act.activation(er[:, :, :], gb[:, :, 0, :], ACT.Exp).then_inc(S("ns_er"), 1)
                for l in range(LV):
                    wait(act, S("ns_p"), m * LV + l + 1)
                    if l:
                        wait(act, S("ns_pt"), m * (LV - 1) + l)
                    else:
                        wait(act, S("ns_up"), m * LV)
                    act.activation(Pm[:, :, :], pKK, ACT.Copy).then_inc(S("ns_pm"), 1)
                    if l == outputs_after(t, ch) and t is not None and (j or has_prev):
                        high(m - 1, 1 - j)
                wait(act, S("ns_v"), m + 1)
                wait(act, S("ns_ds"), m * 2)
                if t is None:
                    act.wait_ge(S("ns_wlo"), KO)
                act.activation(vn[:, :, :], pV, ACT.Copy).then_inc(S("ns_vn"), 1)
                wait(act, S("ns_o"), m + 1)
                wait(act, S("ns_rs"), m * 2)
                for n, (hp, p) in enumerate((hp, p) for hp in range(HP) for p in range(2)):
                    r = R[1 - p]
                    act.activation(junk[r, :], pX[p][r, hp, :], ACT.Square, accum_out=ss[r, hp:hp + 1])\
                       .then_inc(S("ns_ss"), 1)
                    wait(act, S("ns_ss"), m * 8 + n + 1)
                if j and has_prev:
                    norm2(t - 1)

            def norm2(t):
                wait(act, S("ns_yd"), t * 2)
                wait(act, S("ns_ds"), t * 4 + 6)
                act.activation(vn[:, :, :].rearrange("p a b -> p (a b)"), h[:, :], ACT.Square, accum_out=ss2[:, :])\
                   .then_inc(S("ns_ss2"), 1)

            def tail():
                high(2 * NT - 2, 1)
                wait(act, S("ns_yd"), 2 * NT - 2)
                act.activation(vn[:, :, :].rearrange("p a b -> p (a b)"), h[:, :], ACT.Square, accum_out=ss2[:, :])\
                   .then_inc(S("ns_ss2"), 1)
            over_chunks(act, chunk, tail)

        @block.vector
        def _(dve):
            dve.memset(St[:, :, :], 0.0).then_inc(S("ns_init"), 1)
            dve.wait_ge(S("ns_init"), 1)
            dve.wait_ge(S("ns_nw_in"), 16)

            def lo(m, half):
                for b in range(2):
                    wait(dve, S("ns_othi"), (m - 1) * 2 + b + 1)
                    dve.tensor_tensor(oT_lo[:, 8 * b:8 * b + 8, half * C:half * C + C], pT[b],
                                      oT_hi[:, 8 * b:8 * b + 8, half * C:half * C + C].bitcast(F32), ALU.subtract)\
                       .then_inc(S("ns_otlo"), 1)

            def residual(t, half):
                wait(dve, S("ns_y"), t * 2 - 1 + half)
                wait(dve, S("ns_in_h"), t * 16)
                c = slice(half * 512, half * 512 + 512)
                dve.tensor_tensor(h[:, c], pY[:, :], h[:, c], ALU.add).then_inc(S("ns_yd"), 1)

            def final(t):
                wait(dve, S("ns_rs2"), t)
                wait(dve, S("ns_yd"), t * 2)
                dve.scalar_tensor_tensor(h[:, :], h[:, :], ss2[:, 0:1], nw[:, :], ALU.mult, ALU.mult)\
                   .then_inc(S("ns_final"), 1)

            def chunk(ch, t, has_prev):
                m, j = ch.m, ch.j
                wait(dve, S("ns_tg"), m + 1)
                wait(dve, S("ns_vb"), m)
                dve.tensor_reduce(gbc[:, :, :], tg, AX.X, ALU.add).then_inc(S("ns_gbc"), 1)
                wait(dve, S("ns_gbc"), m + 1)
                wait(dve, S("ns_in_g"), m * 32 + 32)
                wait(dve, S("ns_dx"), m)
                dve.tensor_tensor(d1[:, :, :], gp[:, :, 0, :], bc(gbc[:, :, 0:1], [P, HP, C]), ALU.subtract)\
                   .then_inc(S("ns_d1"), 1)
                wait(dve, S("ns_kdec"), m)
                dve.tensor_tensor(kdl[:, :], gp[:, :, 0, C - 1], gbc[:, :, 0], ALU.subtract).then_inc(S("ns_kdl"), 1)
                wait(dve, S("ns_d1"), m + 1)
                wait(dve, S("ns_at"), m)
                dve.tensor_scalar(dn[:, :, :], d1[:, :, :], 0.0, None, ALU.min).then_inc(S("ns_dn"), 1)
                wait(dve, S("ns_m"), m)
                dve.tensor_scalar(dx[:, :, :], d1[:, :, :], 0.0, None, ALU.max).then_inc(S("ns_dx"), 1)
                wait(dve, S("ns_g"), m + 1)
                wait(dve, S("ns_dxb"), m + 1)
                wait(dve, S("ns_low"), m * LV)
                dve.tensor_tensor(M[:, :, :], pKK, dx[:, :, :], ALU.mult).then_inc(S("ns_m"), 1)
                wait(dve, S("ns_mtf"), m * 2 + 2)
                dve.tensor_tensor(d1[:, :, :], pKK, mtf[:, :, :], ALU.mult).then_inc(S("ns_mt"), 1)
                wait(dve, S("ns_mt"), m + 1)
                wait(dve, S("ns_v"), m)
                dve.tensor_tensor(U[:, :, :], eye_p([P, HP, C]), d1[:, :, :], ALU.subtract).then_inc(S("ns_u"), 1)
                wait(dve, S("ns_dnm"), m + 1)
                wait(dve, S("ns_o"), m)
                dve.tensor_tensor(at[:, :, :], pQK, dn[:, :, :], ALU.mult).then_inc(S("ns_at"), 1)
                for l in range(LV):
                    wait(dve, S("ns_up"), m * LV + l + 1)
                    wait(dve, S("ns_u"), m * (LV + 1) + l + 1)
                    dve.tensor_tensor(U[:, :, :], U[:, :, :], pUP, ALU.subtract).then_inc(S("ns_u"), 1)
                    if l < LV - 1:
                        wait(dve, S("ns_pt"), m * (LV - 1) + l + 1)
                        wait(dve, S("ns_t"), m * LV + l + 1)
                        dve.tensor_tensor(Ti[:, :, :], Ti[:, :, :], pPT, ALU.subtract).then_inc(S("ns_t"), 1)
                    if l == outputs_after(t, ch) and t is not None and (j or has_prev):
                        if j and has_prev:
                            residual(t - 1, 1)
                        lo(m - 1, 1 - j)
                for p in range(2):
                    wait(dve, S("ns_vb"), m + 1)
                    wait(dve, S("ns_x"), m + 1)
                    dve.tensor_tensor(v[R[p], :, :], v[R[p], :, :], pX[p][R[p], :, :], ALU.subtract)\
                       .then_inc(S("ns_r"), 1)
                for rnd in range(2):
                    wait(dve, S("ns_ds"), m * 2 + rnd + 1)
                    for a in range(2):
                        for p in range(2):
                            hd = 2 * (2 * rnd + a) + p
                            wait(dve, S("ns_er"), m + 1)
                            dve.scalar_tensor_tensor(St[:, hd, :], St[:, hd, :], er[:, hd, C - 1:C], pS[p][:, a, :],
                                                     ALU.mult, ALU.add).then_inc(S("ns_su"), 1)
                wait(dve, S("ns_rs"), m * 2 + 2)
                wait(dve, S("ns_in_z"), m * 32 + 32)
                for hp in range(HP):
                    for p in range(2):
                        r = R[1 - p]
                        dve.scalar_tensor_tensor(og[r, hp, :], pX[p][r, hp, :], ss[r, hp:hp + 1], og[r, hp, :],
                                                 ALU.mult, ALU.mult).then_inc(S("ns_og"), 1)
                if has_prev and j == 0:
                    residual(t - 1, 0)
                if has_prev and j:
                    final(t - 1)

            def tail():
                lo(2 * NT - 2, 1)
                residual(NT - 1, 0)
                residual(NT - 1, 1)
                final(NT - 1)
            over_chunks(dve, chunk, tail)

        @block.gpsimd
        def _(pool):
            w_lo(pool)

            def mult(dst, a, b, sem):
                pool.tensor_tensor(dst, a, b, ALU.mult).then_inc(S(sem), 1)

            def chunk(ch, t, has_prev):
                m, j = ch.m, ch.j
                wait(pool, S("ns_in_g"), m * 32 + 32)
                wait(pool, S("ns_gbc"), m)
                wait(pool, S("ns_x"), m)
                mult(tg.rearrange("p h w c -> p (h w) c"), gp[:, :, :, :].rearrange("p h w c -> p (h w) c"),
                     eye_p([P, 2 * HP, C]), "ns_tg")
                wait(pool, S("ns_edn"), m + 1)
                wait(pool, S("ns_t"), m * LV)
                mult(mtf[:, :, :], dn[:, :, :], gp[:, :, 1, :], "ns_mtf")
                wait(pool, S("ns_mtf"), m * 2 + 1)
                mult(mtf[:, :, :], mtf[:, :, :], mask(K_LOW1T), "ns_mtf")
                mult(dn[:, :, :], dn[:, :, :], mask(K_CAUSP), "ns_dnm")
                wait(pool, S("ns_edx"), m + 1)
                wait(pool, S("ns_gbc"), m + 1)
                mult(dx[:, :, :], dx[:, :, :], bc(gbc[:, :, 1:2], [P, HP, C]), "ns_dxb")
                wait(pool, S("ns_m"), m + 1)
                wait(pool, S("ns_mt"), m + 1)
                wait(pool, S("ns_p"), m * LV)
                mult(low[0][:, :, :], M[:, :, :], mask(K_LOW), "ns_low1")
                wait(pool, S("ns_low1"), m + 1)
                wait(pool, S("ns_up"), m * LV)
                pool.tensor_tensor(Ti[:, :, :], eye_p([P, HP, C]), low[0][:, :, :], ALU.subtract)\
                    .then_inc(S("ns_t"), 1)
                for l in range(LV):
                    mult(low[l + 1][:, :, :], M[:, :, :], mask(K_LOW + (l + 1) * C), "ns_low")
                wait(pool, S("ns_er"), m + 1)
                wait(pool, S("ns_in_kq"), m * 64 + 64)
                wait(pool, S("ns_gbc"), m + 1)
                mult(kqd[:, :, :, :], kq[:, :, :, :], bc(gb[:, :, 0:1, :], [P, NH, 2, C]), "ns_kqd")
                wait(pool, S("ns_kqd"), m * 3 + 1)
                for p in range(2):
                    mult(kqd[:, p::2, p, :], kqd[:, p::2, p, :], gb[:, p::2, 1, :], "ns_kqd")
                wait(pool, S("ns_in_v"), m * 32 + 32)
                mult(v[:, :, :], v[:, :, :], bc(gbc[:, :, 1:2], [P, HP, NDV]), "ns_vb")
                wait(pool, S("ns_ekdl"), m + 1)
                wait(pool, S("ns_in_kt"), m * 32 + 32)
                mult(kdec[:, :, :], kt[:, :, :], bc(kdl[:, :].rearrange("p (h o) -> p h o", o=1), [P, HP, NDK]),
                     "ns_kdec")
                waits_apart(pool, T.pool_carrier,
                            (S("ns_ss"), m * 8 + 8),
                            (S("ns_og"), m * 8))
                rsqrt(ss, NDV, m, "ns_rs")
                if j and has_prev:
                    norm2(t - 1)

            def rsqrt(x, width, i, sem):
                pool.tensor_scalar(x[:, :], x[:, :], 1.0 / width, EPS, ALU.mult, ALU.add).then_inc(S(sem), 1)
                wait(pool, S(sem), i * 2 + 1)
                pool.tensor_tensor(x[:, :], x[:, :], bc(T.minus_half[:, 0:1], list(x.shape)), ALU.pow)\
                    .then_inc(S(sem), 1)

            def norm2(t):
                waits_apart(pool, T.pool_carrier,
                            (S("ns_ss2"), t))
                pool.tensor_scalar(ss2[:, :], ss2[:, :], 1.0 / D, EPS, ALU.mult, ALU.add).then_inc(S("ns_mean2"), 1)
                wait(pool, S("ns_mean2"), t)
                pool.tensor_tensor(ss2[:, :], ss2[:, :], T.minus_half[:, 0:1], ALU.pow).then_inc(S("ns_rs2"), 1)

            def tail():
                norm2(NT - 1)
            over_chunks(pool, chunk, tail)


class Tensors:
    pass


def build(nc, a, out):
    T = Tensors()
    with ExitStack() as ctx:
        S = Sems(nc)

        def sb(name, shape, dt=F32, where=ctx):
            return where.enter_context(nc.sbuf_tensor(name, shape, dt))

        def dram(name, shape):
            return nc.dram_tensor(name, shape, F32).ap()
        T.k_dram, T.starts_dram = a["k"], a["starts"]
        T.gla_qk = dram("gla_qk", [GH, 2, P, TP])
        T.gla_ko = dram("gla_ko", [TP, GQK])
        T.gla_v = dram("gla_v", [TP, GV])
        T.gla_z = dram("gla_z", [TP, GV])
        T.h1 = dram("h1", [TP, D])
        T.gdn_qk = dram("gdn_qk", [2, NH, P, TP])
        T.gdn_k = dram("gdn_k", [TP, NQK])
        T.gdn_v = dram("gdn_v", [TP, NV])
        T.gdn_z = dram("gdn_z", [TP, NV])
        T.gb = dram("gdn_gb", [2 * NT, NH, 2, C])
        T.k = sb("consts", [P, K_END])
        T.eye = T.k[:, K_EYE:K_EYE + P]
        T.causal = T.k[:, K_CAUSAL:K_CAUSAL + P].rearrange("p (o c) -> p o c", o=1)
        T.minus_half = sb("minus_half", [P, 1])
        zero_w = sb("zero_weights", [P, 32], mybir.dt.bfloat16)
        spare = [sb(f"carrier{n}", [P, 2]) for n in range(2)]
        with nc.Block() as block:
            @block.vector
            def _(dve):
                dve.memset(zero_w[:, :], 0.0)
                for x in spare:
                    dve.memset(x[:, :], 0.0)
        T.pe_carrier = lambda: nc.tensor.ldweights(zero_w[:, :], tile_position=(0, 0))
        T.dve_carrier = lambda: nc.vector.tensor_copy(spare[0][:, 0:1], spare[0][:, 1:2])
        T.pool_carrier = lambda: nc.gpsimd.tensor_tensor(spare[1][:, 0:1], spare[1][:, 1:2], spare[1][:, 1:2], ALU.add)
        T.cw = sb("conv_taps", [P, CONV, (2 * NQK + NV) // P])
        T.hnw = sb("gla_hn", [P, GV // P])
        T.hnw2 = sb("gdn_hn", [P, NV // P])
        with ExitStack() as hctx:
            T.hn_hi = sb("hn_hi", [P, KT, TP], F32R, hctx)
            T.hn_lo = sb("hn_lo", [P, KT, TP], F32R, hctx)
            with ExitStack() as zctx:
                T.zeros = sb("zeros", [P, NV], F32, zctx)

                def pads():
                    found = [(d[0:PAD, :], T.zeros[0:PAD, 0:d.shape[1]])
                             for d in (T.gla_ko, T.gla_v, T.gla_z, T.gdn_k, T.gdn_v, T.gdn_z)]
                    found += [(T.gla_qk[g, :, :, 0:PAD].rearrange("w p n -> p w n"),
                               T.zeros[:, 0:2 * PAD].rearrange("p (w n) -> p w n", w=2)) for g in range(GH)]
                    found += [(T.gdn_qk[w, :, :, 0:PAD].rearrange("h p n -> p h n"),
                               T.zeros[:, 0:NH * PAD].rearrange("p (h n) -> p h n", h=NH)) for w in range(2)]
                    found += [(T.gb[c].rearrange("h w c -> h (w c)"), T.zeros[0:NH, 0:2 * C]) for c in range(2)]
                    return found
                T.pads = pads
                embed(nc, S, T, a["x"], a["meta"], a["gla_norm"])
            with ExitStack() as gctx:
                T.dec = sb("gla_dec", [P, GH, 2 * NT], F32, gctx)
                with ExitStack() as ectx:
                    T.Eb = sb("gla_eb", [P, GH, L], F32, ectx)
                    T.Enb = sb("gla_enb", [P, GH, L], F32, ectx)
                    T.Eout = sb("gla_eout", [P, GH, L], F32, ectx)
                    gla_gate(nc, S, T, a["gla_w_in"], a["gla_w_gk"], a["gla_b_gk"], a["gla_head_norm"])
                    gla_qk(nc, S, T, a["gla_w_in"])
                project_vz(nc, S, T, "av", a["gla_w_in"], 2 * GQK, 2 * GQK + GV, GV // P, T.gla_v, T.gla_z, T.hnw)
                gla_scan(nc, S, T, a["gla_w_out"], a["x"], a["meta"], a["gdn_norm"])
                S.give_back()
            gdn_gate(nc, S, T, a["gdn_w_in"], a["gdn_a_log"], a["gdn_dt_bias"], a["gdn_conv_w"], a["gdn_head_norm"])
            gdn_qk(nc, S, T, a["gdn_w_in"])
            project_vz(nc, S, T, "nv", a["gdn_w_in"], 2 * NQK, 2 * NQK + NV, NV // P, T.gdn_v, T.gdn_z, T.hnw2,
                       conv=2 * NQK // P)
        gdn_scan(nc, S, T, a["gdn_w_out"], a["final_norm"], out)


def kernel(x, meta_tokens, gla_norm, gla_w_in, gla_w_gk, gla_b_gk, gla_head_norm, gla_w_out, gdn_norm, gdn_w_in,
           gdn_conv_w, gdn_a_log, gdn_dt_bias, gdn_head_norm, gdn_w_out, final_norm):
    import concourse.bacc as bacc
    from concourse.bass_utils import run_bass_kernel_spmd

    def by_channel(w, width):
        return np.tile(w.reshape(-1, P).T, (1, width // w.size))

    arrays = {
        "x": x[0], "meta": meta_tokens, "gla_norm": gla_norm, "gla_w_in": gla_w_in[0], "gla_w_gk": gla_w_gk[0],
        "gla_b_gk": gla_b_gk[0].reshape(GH, P).T, "gla_head_norm": by_channel(gla_head_norm[0], GV), "gla_w_out": gla_w_out[0], "gdn_norm": gdn_norm,
        "gdn_w_in": gdn_w_in[0], "gdn_conv_w": gdn_conv_w[0], "gdn_a_log": gdn_a_log[0],
        "gdn_dt_bias": gdn_dt_bias[0], "gdn_head_norm": by_channel(gdn_head_norm[0], NV), "gdn_w_out": gdn_w_out[0],
        "final_norm": final_norm.reshape(1, D), "k": constants(), "starts": chunk_starts(),
    }
    arrays = {name: np.ascontiguousarray(v) for name, v in arrays.items()}
    nc = bacc.Bacc("TRN2", target_bir_lowering=False, num_devices=1)
    a = {name: nc.dram_tensor("in_" + name, v.shape, mybir.dt.from_np(v.dtype), kind="ExternalInput").ap()
         for name, v in arrays.items()}
    out = nc.dram_tensor("out", [SEQ, D], F32, kind="ExternalOutput").ap()
    build(nc, a, out)
    r = run_bass_kernel_spmd(nc, [{"in_" + name: v for name, v in arrays.items()}], core_ids=[0])
    return r.results[0]["out"].reshape(1, SEQ, D)
```

```python
from contextlib import ExitStack

import numpy as np
import concourse.bass as bass
from concourse import mybir
from concourse.alu_op_type import AluOpType as ALU

F32 = mybir.dt.float32
F32R = mybir.dt.float32r
I32 = mybir.dt.int32
ACT = mybir.ActivationFunctionType
AX = mybir.AxisListType

P = 128
D = 1024
KT = D // P
SEQ = 1024
NMETA = 16
C = 64
PAD = P - NMETA
TP = P + SEQ
NT = TP // P
L = NMETA + SEQ
EPS = 1e-6
SPANS = [(0, 352), (352, 344), (696, 344)]
GH, GDK, GDV = 4, 128, 256
GRANK = 16
GQK, GV = GH * GDK, GH * GDV
NH, NDK, NDV = 8, 128, 256
NQK, NV = NH * NDK, NH * NDV
HP = NH // 2
CONV = 4
LEVELS = [2, 4, 8, 16, 32]

K_EYE, K_CAUSAL, K_EYEP, K_CAUSP, K_LOW1T, K_LOW = 0, 128, 256, 320, 384, 448
K_END = K_LOW + (1 + len(LEVELS)) * C


def constants():
    k = np.zeros((P, K_END), np.float32)
    j, i = np.meshgrid(np.arange(P), np.arange(P), indexing="ij")
    k[:, K_EYE:K_EYE + P] = j == i
    k[:, K_CAUSAL:K_CAUSAL + P] = (j // C == i // C) & (j <= i)
    r, c = np.meshgrid(np.arange(P) % C, np.arange(C), indexing="ij")
    k[:, K_EYEP:K_EYEP + C] = r == c
    k[:, K_CAUSP:K_CAUSP + C] = r <= c

    def below(a, b, size):
        return (a // size % 2 == 1) & (a // size - b // size == 1)
    k[:, K_LOW1T:K_LOW1T + C] = below(c, r, 1)
    for n, size in enumerate([1] + LEVELS):
        k[:, K_LOW + n * C:K_LOW + (n + 1) * C] = below(r, c, size)
    return k


def chunk_starts():
    m = np.ones((P, L), np.float32)
    m[:, 0] = 0
    m[:, NMETA::C] = 0
    return m


class Sems:

    def __init__(self, nc):
        self.nc, self.made = nc, {}

    def __call__(self, name):
        if name not in self.made:
            self.made[name] = self.nc.alloc_semaphore(name=name)
        return self.made[name]

    def give_back(self):
        self.nc.all_engine_barrier()
        self.nc.clear_and_free_semaphores(list(self.made.values()))
        self.nc.all_engine_barrier()
        self.made = {}


def wait(eng, sem, value):
    if isinstance(value, int) and value <= 0:
        return
    eng.wait_ge(sem, value)


def waits_apart(eng, carrier, *waits):
    for s, v in waits:
        wait(eng, s, v)
    carrier()


def ds(i, n=1):
    return bass.ds(i, n)


def bc(ap, shape):
    return ap.broadcast_to(shape)


def embed(nc, S, T, x, meta, norm_w):
    with ExitStack() as ctx:
        def sb(name, shape, dt=F32):
            return ctx.enter_context(nc.sbuf_tensor(name, shape, dt))
        X = [sb(f"em_x{j}", [P, D]) for j in range(2)]
        hn = [sb(f"em_hn{j}", [P, D]) for j in range(2)]
        junk = sb("em_junk", [P, D])
        ss = [sb(f"em_ss{j}", [P, 1]) for j in range(2)]
        rs = [sb(f"em_rs{j}", [P, 1]) for j in range(2)]
        nw = sb("em_nw", [P, D])
        tr = [ctx.enter_context(nc.psum_tensor(f"em_tr{j}{b}", [P, 4, P], F32)) for j in range(2) for b in range(2)]
        block = ctx.enter_context(nc.Block())
        x_in = [S("em_x_in0"), S("em_x_in1")]

        def over_tiles(eng, one):
            one(0, 0, 0)
            with eng.Fori(0, (NT - 1) // 2) as i:
                one(i * 2 + 1, 1, i)
                one(i * 2 + 2, 0, i + 1)

        @block.sync
        def _(sp):
            sp.dma_start(T.k[:, :], T.k_dram).then_inc(S("k_in"), 16)
            sp.dma_start(nw[:, :], bc(norm_w, [P, D])).then_inc(S("em_nw_in"), 16)
            wait(sp, S("em_x_zero"), 1)
            sp.dma_start(X[0][PAD:P, :], meta).then_inc(x_in[0], 16)

            def load(t, j, n):
                if isinstance(t, int) and t == 0:
                    return
                wait(sp, S("em_hn_done"), t - 1)
                sp.dma_start(X[j][:, :], x[ds((t - 1) * P, P), :]).then_inc(x_in[j], 16)
            over_tiles(sp, load)
            sp.wait_ge(S("em_zero"), 1)
            for dst, src in T.pads():
                sp.dma_start(dst, src).then_inc(S("pads_out"), 16)
            wait(sp, S("pads_out"), 16 * len(T.pads()))

        @block.scalar
        def _(act):
            def one(t, j, n):
                wait(act, x_in[j], n * 16 + 16)
                wait(act, S("em_ss"), t)
                wait(act, S("em_mean"), t - 1 if isinstance(t, int) else t - 1)
                act.activation(junk[:, :], X[j][:, :], ACT.Square, accum_out=ss[j][:, :]).then_inc(S("em_ss"), 1)
                for b in range(2):
                    wait(act, S("em_tr"), t * 2 + b + 1)
                    act.activation(T.hn_hi[:, 4 * b:4 * b + 4, ds(t * P, P)], tr[2 * j + b][:, :, :],
                                   ACT.Copy).then_inc(S("em_hi"), 1)
            over_tiles(act, one)

        @block.gpsimd
        def _(pool):
            pool.memset(T.zeros[:, :], 0.0).then_inc(S("em_zero"), 1)
            pool.memset(T.minus_half[:, :], -0.5).then_inc(S("em_half"), 1)
            pool.wait_ge(S("em_half"), 1)

            def one(t, j, n):
                waits_apart(pool, T.pool_carrier,
                            (S("em_ss"), t + 1),
                            (S("em_hn_done"), t - 1))
                pool.tensor_scalar(rs[j][:, :], ss[j][:, :], 1.0 / D, EPS, ALU.mult, ALU.add).then_inc(S("em_mean"), 1)
                wait(pool, S("em_mean"), t + 1)
                pool.tensor_tensor(rs[j][:, :], rs[j][:, :], T.minus_half[:, 0:1], ALU.pow).then_inc(S("em_rs"), 1)
            over_tiles(pool, one)

        @block.vector
        def _(dve):
            dve.memset(X[0][:, :], 0.0).then_inc(S("em_x_zero"), 1)
            dve.wait_ge(S("em_nw_in"), 16)

            def one(t, j, n):
                wait(dve, S("em_rs"), t + 1)
                wait(dve, x_in[j], n * 16 + 16)
                wait(dve, S("em_tr"), t * 2 - 2 if not isinstance(t, int) else 2 * t - 2)
                dve.scalar_tensor_tensor(hn[j][:, :], X[j][:, :], rs[j][:, 0:1], nw[:, :],
                                         ALU.mult, ALU.mult).then_inc(S("em_hn_done"), 1)
                for b in range(2):
                    wait(dve, S("em_hi"), t * 2 + b + 1)
                    dve.tensor_tensor(T.hn_lo[:, 4 * b:4 * b + 4, ds(t * P, P)], tr[2 * j + b][:, :, :],
                                      T.hn_hi[:, 4 * b:4 * b + 4, ds(t * P, P)].bitcast(F32),
                                      ALU.subtract).then_inc(S("em_lo"), 1)
            over_tiles(dve, one)

        @block.tensor
        def _(pe):
            pe.wait_ge(S("k_in"), 16)

            def one(t, j, n):
                wait(pe, S("em_hn_done"), t + 1)
                wait(pe, S("em_lo"), t * 2 - 2 if not isinstance(t, int) else 2 * t - 2)
                for b in range(2):
                    for c in range(4):
                        kt = 4 * b + c
                        mm = pe.transpose(tr[2 * j + b][:, c, :], hn[j][:, kt * P:(kt + 1) * P], T.eye)
                    mm.then_inc(S("em_tr"), 1)
            over_tiles(pe, one)


def project(pe, acc, w_hi, w_lo, T):
    for kt in range(KT):
        for n, (w, h) in enumerate(((w_hi, T.hn_hi), (w_hi, T.hn_lo), (w_lo, T.hn_hi))):
            for b, (s, m) in enumerate(SPANS):
                mm = pe.matmul(acc[:, b, 0:m], w[:, kt, :], h[:, kt, PAD + s:PAD + s + m],
                               start=(kt == 0 and n == 0), stop=(kt == KT - 1 and n == 2))
    return mm


class Proj:

    def __init__(self, nc, S, T, ctx, tag, w, col):
        self.S, self.T, self.tag, self.col = S, T, tag, col
        self.w = w.rearrange("(k p) n -> p k n", p=P)
        self.st = [ctx.enter_context(nc.sbuf_tensor(f"{tag}_w{j}", [P, KT, P], F32)) for j in range(2)]
        self.hi = [ctx.enter_context(nc.sbuf_tensor(f"{tag}_whi{j}", [P, KT, P], F32R)) for j in range(2)]
        self.lo = [ctx.enter_context(nc.sbuf_tensor(f"{tag}_wlo{j}", [P, KT, P], F32R)) for j in range(2)]
        self.acc = [ctx.enter_context(nc.psum_tensor(f"{tag}_acc{j}", [P, 3, 512], F32)) for j in range(2)]
        self.trA = ctx.enter_context(nc.psum_tensor(f"{tag}_trA", [P, 4, P], F32))
        self.trB = ctx.enter_context(nc.psum_tensor(f"{tag}_trB", [P, 4, P], F32))

    def sem(self, name):
        return self.S(f"{self.tag}_{name}")

    def load(self, sp, i, j):
        wait(sp, self.sem(f"whi{j}"), i)
        wait(sp, self.sem(f"wlo{j}"), i)
        sp.dma_start(self.st[j][:, :, :], self.w[:, :, ds(self.col(i, j), P)]).then_inc(self.sem(f"w_in{j}"), 16)

    def split_hi(self, act, i, j):
        wait(act, self.sem(f"w_in{j}"), i * 16 + 16)
        wait(act, self.sem(f"mm{j}"), i)
        act.activation(self.hi[j][:, :, :], self.st[j][:, :, :], ACT.Copy).then_inc(self.sem(f"whi{j}"), 1)

    def split_lo(self, pool, i, j):
        wait(pool, self.sem(f"whi{j}"), i + 1)
        wait(pool, self.sem(f"mm{j}"), i)
        wait(pool, self.sem(f"w_in{j}"), i * 16 + 16)
        pool.tensor_tensor(self.lo[j][:, :, :], self.st[j][:, :, :], self.hi[j][:, :, :].bitcast(F32),
                           ALU.subtract).then_inc(self.sem(f"wlo{j}"), 1)

    def mm(self, pe, i, j, free):
        wait(pe, self.sem(f"whi{j}"), i + 1)
        wait(pe, self.sem(f"wlo{j}"), i + 1)
        wait(pe, self.sem(f"free{j}"), i * free)
        project(pe, self.acc[j], self.hi[j], self.lo[j], self.T).then_inc(self.sem(f"mm{j}"), 1)

    def banks(self):
        return ((0, self.trA), (1, self.trB))


def transpose_out(pe, q, src, b, eye, done):
    if b < 2:
        bank = (q.trA, q.trB)[b]
        for c in range(4):
            s = NMETA + (4 * b + c) * P
            mm = pe.transpose(bank[:, c, :], src[:, s:s + P], eye)
    else:
        mm = pe.transpose(q.trA[0:NMETA, 0, :], src[:, 0:NMETA], eye)
    mm.then_inc(done, 1)


def evacuate_out(eng, copy, q, dst, b, done):
    if b < 2:
        copy(dst[:, 1 + 4 * b:5 + 4 * b, :], (q.trA, q.trB)[b][:, :, :]).then_inc(done, 1)
    else:
        copy(dst[0:NMETA, 0, :], q.trA[0:NMETA, 0, :]).then_inc(done, 1)


def store_tokens(sp, dst, tok, col, width, done):
    sp.dma_start(dst[PAD:P, ds(col, P)], tok[0:NMETA, 0, :]).then_inc(done, 16)
    sp.dma_start(dst[P:TP, ds(col, P)].rearrange("(t p) c -> p t c", p=P), tok[:, 1:NT, :]).then_inc(done, 16)


def gla_gate(nc, S, T, w_in, w_gk, b_gk, head_norm):
    with ExitStack() as ctx:
        def sb(name, shape, dt=F32):
            return ctx.enter_context(nc.sbuf_tensor(name, shape, dt))
        st = sb("gg_w", [P, KT, P])
        hi = sb("gg_whi", [P, KT, P], F32R)
        lo = sb("gg_wlo", [P, KT, P], F32R)
        gl = sb("gg_low", [GRANK, L])
        wg = sb("gg_wgk", [GRANK, GQK])
        bg = sb("gg_b", [P, GH])
        cm = sb("gg_starts", [P, L])
        ax = [sb(f"gg_ax{j}", [P, L]) for j in range(2)]
        mn = [sb(f"gg_mn{j}", [P, L]) for j in range(2)]
        bt = [sb(f"gg_bt{j}", [P, L]) for j in range(2)]
        acc = [ctx.enter_context(nc.psum_tensor(f"gg_acc{j}", [P, 3, 512], F32)) for j in range(2)]
        block = ctx.enter_context(nc.Block())
        c0 = 2 * GQK + 2 * GV

        @block.sync
        def _(sp):
            sp.wait_ge(S("gg_zero"), 1)
            sp.dma_start(st[:, :, 0:GRANK], w_in.rearrange("(k p) n -> p k n", p=P)[:, :, c0:c0 + GRANK])\
              .then_inc(S("gg_w_in"), 16)
            sp.dma_start(wg[:, :], w_gk).then_inc(S("gg_small_in"), 16)
            sp.dma_start(bg[:, :], b_gk).then_inc(S("gg_small_in"), 16)
            sp.dma_start(cm[:, :], T.starts_dram).then_inc(S("gg_small_in"), 16)
            sp.dma_start(T.hnw[:, :], head_norm).then_inc(S("gg_hnw_in"), 16)
            sp.wait_ge(S("gg_hnw_in"), 16)

        @block.scalar
        def _(act):
            act.wait_ge(S("gg_w_in"), 16)
            act.activation(hi[:, :, :], st[:, :, :], ACT.Copy).then_inc(S("gg_whi"), 1)
            act.wait_ge(S("gg_low"), 1)
            for b, (s, m) in enumerate(SPANS):
                act.activation(gl[:, s:s + m], acc[0][0:GRANK, b, 0:m], ACT.Copy).then_inc(S("gg_low_out"), 1)

            def logs(h):
                j = h % 2
                act.wait_ge(S("gg_abs"), h + 1)
                act.activation(ax[j][:, :], ax[j][:, :], ACT.Exp, scale=-1.0).then_inc(S("gg_e"), 1)
                act.wait_ge(S("gg_e"), h + 1)
                act.activation(ax[j][:, :], ax[j][:, :], ACT.Ln, bias=1.0).then_inc(S("gg_ln"), 1)

            def exps(h):
                j = h % 2
                act.wait_ge(S("gg_cum"), h + 1)
                act.activation(T.Eb[:, h, :], bt[j][:, :], ACT.Exp, scale=1.0 / 16).then_inc(S("gg_exps"), 1)
                act.activation(T.Enb[:, h, :], bt[j][:, :], ACT.Exp, scale=-1.0 / 16).then_inc(S("gg_exps"), 1)
                act.activation(T.dec[:, h, 2:], bt[j][:, NMETA + C - 1::C], ACT.Exp, scale=1.0 / 16)\
                   .then_inc(S("gg_exps"), 1)
                act.activation(T.dec[:, h, 1:2], bt[j][:, NMETA - 1:NMETA], ACT.Exp, scale=1.0 / 16)\
                   .then_inc(S("gg_exps"), 1)
                act.wait_ge(S("gg_left"), 2 * (h + 1))
                act.activation(T.Eout[:, h, :], ax[j][:, :], ACT.Exp, scale=1.0 / 16).then_inc(S("gg_exps"), 1)
            for h in range(GH):
                logs(h)
                if h:
                    exps(h - 1)
            exps(GH - 1)
            act.wait_ge(S("gg_exps"), 5 * GH)

        @block.gpsimd
        def _(pool):
            pool.memset(st[:, :, :], 0.0).then_inc(S("gg_zero"), 1)
            pool.memset(T.dec[:, :, 0:1], 1.0).then_inc(S("gg_dec0"), 1)
            pool.wait_ge(S("gg_whi"), 1)
            pool.tensor_tensor(lo[:, :, :], st[:, :, :], hi[:, :, :].bitcast(F32), ALU.subtract)\
                .then_inc(S("gg_wlo"), 1)

        @block.tensor
        def _(pe):
            pe.wait_ge(S("gg_wlo"), 1)
            project(pe, acc[0], hi, lo, T).then_inc(S("gg_low"), 1)
            pe.wait_ge(S("gg_low_out"), 3)
            pe.wait_ge(S("gg_small_in"), 48)
            for h in range(GH):
                if h >= 2:
                    pe.wait_ge(S("gg_min"), 3 * (h - 1))
                for b, (s, m) in enumerate(SPANS):
                    mm = pe.matmul(acc[h % 2][:, b, 0:m], wg[:, h * P:(h + 1) * P], gl[:, s:s + m],
                                   start=True, stop=True)
                mm.then_inc(S("gg_logit"), 1)

        @block.vector
        def _(dve):
            def take(h):
                j = h % 2
                dve.wait_ge(S("gg_logit"), h + 1)
                if h >= 2:
                    dve.wait_ge(S("gg_exps"), 5 * (h - 1))
                for b, (s, m) in enumerate(SPANS):
                    dve.tensor_scalar(ax[j][:, s:s + m], acc[j][:, b, 0:m], bg[:, h:h + 1], 0.0, ALU.add, ALU.max)\
                       .then_inc(S("gg_max"), 1)
                for b, (s, m) in enumerate(SPANS):
                    dve.tensor_scalar(mn[j][:, s:s + m], acc[j][:, b, 0:m], bg[:, h:h + 1], 0.0, ALU.add, ALU.min)\
                       .then_inc(S("gg_min"), 1)
                dve.wait_ge(S("gg_max"), 3 * (h + 1))
                dve.wait_ge(S("gg_min"), 3 * (h + 1))
                dve.tensor_tensor(ax[j][:, :], ax[j][:, :], mn[j][:, :], ALU.subtract).then_inc(S("gg_abs"), 1)

            def cumulate(h):
                j = h % 2
                dve.wait_ge(S("gg_ln"), h + 1)
                dve.wait_ge(S("gg_min"), 3 * (h + 1))
                dve.tensor_tensor(mn[j][:, :], mn[j][:, :], ax[j][:, :], ALU.subtract).then_inc(S("gg_log"), 1)
                dve.wait_ge(S("gg_log"), h + 1)
                dve.tensor_tensor_scan(bt[j][:, :], cm[:, :], mn[j][:, :], 0.0, ALU.mult, ALU.add)\
                   .then_inc(S("gg_cum"), 1)
                dve.wait_ge(S("gg_cum"), h + 1)
                dve.tensor_tensor(ax[j][:, 0:NMETA], bc(bt[j][:, NMETA - 1:NMETA], [P, NMETA]), bt[j][:, 0:NMETA],
                                  ALU.subtract).then_inc(S("gg_left"), 1)
                real = bt[j][:, NMETA:].rearrange("p (c t) -> p c t", t=C)
                dve.tensor_tensor(ax[j][:, NMETA:].rearrange("p (c t) -> p c t", t=C),
                                  bc(real[:, :, C - 1:C], [P, SEQ // C, C]), real, ALU.subtract)\
                   .then_inc(S("gg_left"), 1)
            take(0)
            for h in range(GH):
                if h + 1 < GH and h < 1:
                    take(h + 1)
                cumulate(h)
                if h + 2 < GH:
                    take(h + 2)


def gla_qk(nc, S, T, w_in):
    n = GH
    with ExitStack() as ctx:
        q = Proj(nc, S, T, ctx, "aq", w_in, lambda i, j: j * GQK + i * P)
        qT = ctx.enter_context(nc.sbuf_tensor("aq_q", [P, L], F32))
        kT = ctx.enter_context(nc.sbuf_tensor("aq_k", [P, L], F32))
        oT = ctx.enter_context(nc.sbuf_tensor("aq_kout", [P, L], F32))
        tok = ctx.enter_context(nc.sbuf_tensor("aq_tok", [P, NT, P], F32))
        block = ctx.enter_context(nc.Block())

        @block.sync
        def _(sp):
            def store(i):
                wait(sp, q.sem("free0"), i * 3 + 3)
                sp.dma_start(T.gla_qk[ds(i), 0, :, PAD:TP].rearrange("a p n -> p (a n)"), qT[:, :])\
                  .then_inc(q.sem("q_out"), 16)
                wait(sp, q.sem("free1"), i * 6 + 6)
                sp.dma_start(T.gla_qk[ds(i), 1, :, PAD:TP].rearrange("a p n -> p (a n)"), kT[:, :])\
                  .then_inc(q.sem("k_out"), 16)
                wait(sp, q.sem("ev"), i * 3 + 3)
                store_tokens(sp, T.gla_ko, tok, i * P, GQK, q.sem("tok_out"))
            for j in range(2):
                q.load(sp, 0, j)
            for j in range(2):
                q.load(sp, 1, j)
            with sp.Fori(0, n - 2) as i:
                for j in range(2):
                    q.load(sp, i + 2, j)
                store(i)
            store(n - 2)
            store(n - 1)
            sp.wait_ge(q.sem("q_out"), 16 * n)
            sp.wait_ge(q.sem("k_out"), 16 * n)
            sp.wait_ge(q.sem("tok_out"), 32 * n)

        @block.scalar
        def _(act):
            for j in range(2):
                q.split_hi(act, 0, j)
            with act.Fori(1, n) as i:
                for j in range(2):
                    q.split_hi(act, i, j)

        @block.gpsimd
        def _(pool):
            for j in range(2):
                q.split_lo(pool, 0, j)
            with pool.Fori(1, n) as i:
                for j in range(2):
                    q.split_lo(pool, i, j)

        @block.tensor
        def _(pe):
            def tr(i):
                wait(pe, q.sem("free1"), i * 6 + 6)
                for b in range(3):
                    wait(pe, q.sem("ev"), i * 3 if b == 0 else i * 3 + b - 1)
                    transpose_out(pe, q, oT, b, T.eye, q.sem("tr"))
            q.mm(pe, 0, 0, 3)
            q.mm(pe, 0, 1, 6)
            with pe.Fori(1, n) as i:
                q.mm(pe, i, 0, 3)
                tr(i - 1)
                q.mm(pe, i, 1, 6)
            tr(n - 1)

        @block.vector
        def _(dve):
            def ev(i):
                wait(dve, q.sem("tok_out"), i * 32)
                for b in range(3):
                    wait(dve, q.sem("tr"), i * 3 + b + 1)
                    evacuate_out(dve, dve.tensor_copy, q, tok, b, q.sem("ev"))

            def epi_q(i):
                wait(dve, q.sem("mm0"), i + 1)
                wait(dve, q.sem("q_out"), i * 16)
                for b, (s, m) in enumerate(SPANS):
                    dve.scalar_tensor_tensor(qT[:, s:s + m], q.acc[0][:, b, 0:m], float(GDK) ** -0.5,
                                             T.Eb[:, ds(i), s:s + m].rearrange("p a n -> p (a n)"),
                                             ALU.mult, ALU.mult).then_inc(q.sem("free0"), 1)

            def epi_k(i):
                wait(dve, q.sem("mm1"), i + 1)
                wait(dve, q.sem("k_out"), i * 16)
                wait(dve, q.sem("tr"), i * 3)
                for dst, gate in ((kT, T.Enb), (oT, T.Eout)):
                    for b, (s, m) in enumerate(SPANS):
                        dve.tensor_tensor(dst[:, s:s + m], q.acc[1][:, b, 0:m],
                                          gate[:, ds(i), s:s + m].rearrange("p a n -> p (a n)"), ALU.mult)\
                           .then_inc(q.sem("free1"), 1)
            epi_q(0)
            epi_k(0)
            with dve.Fori(1, n) as i:
                epi_q(i)
                ev(i - 1)
                epi_k(i)
            ev(n - 1)


def project_vz(nc, S, T, tag, w_in, col_v, col_z, n, v_out, z_out, hnw, conv=None):
    with ExitStack() as ctx:
        q = Proj(nc, S, T, ctx, tag, w_in, lambda i, j: (col_v, col_z)[j] + i * P)
        xT = [ctx.enter_context(nc.sbuf_tensor(f"{tag}_x{j}", [P, L], F32)) for j in range(2)]
        tok = [ctx.enter_context(nc.sbuf_tensor(f"{tag}_tok{j}", [P, NT, P], F32)) for j in range(2)]
        if conv is not None:
            xs = ctx.enter_context(nc.sbuf_tensor(f"{tag}_xs", [P, CONV - 1 + L], F32))
            cv = ctx.enter_context(nc.sbuf_tensor(f"{tag}_cv", [P, L], F32))
        block = ctx.enter_context(nc.Block())

        @block.sync
        def _(sp):
            def store(i, j):
                wait(sp, q.sem(f"ev{j}"), i * 3 + 3)
                store_tokens(sp, (v_out, z_out)[j], tok[j], i * P, n * P, q.sem(f"tok_out{j}"))
            for j in range(2):
                q.load(sp, 0, j)
            for j in range(2):
                q.load(sp, 1, j)
            with sp.Fori(0, n - 2) as i:
                for j in range(2):
                    q.load(sp, i + 2, j)
                for j in range(2):
                    store(i, j)
            for i in range(n - 2, n):
                for j in range(2):
                    store(i, j)
            for j in range(2):
                sp.wait_ge(q.sem(f"tok_out{j}"), 32 * n)

        @block.scalar
        def _(act):
            def epi_v(i, before=None):
                wait(act, q.sem("mm0"), i + 1)
                dst, at = (xT[0], 0) if conv is None else (xs, CONV - 1)
                if conv is None:
                    wait(act, q.sem("tr0"), i * 3)
                else:
                    wait(act, q.sem("conv"), i * CONV)
                for b, (s, m) in enumerate(SPANS):
                    act.activation(dst[:, at + s:at + s + m], q.acc[0][:, b, 0:m], ACT.Copy)\
                       .then_inc(q.sem("free0"), 1)

            def silu_v(i):
                if conv is not None:
                    wait(act, q.sem("conv"), i * CONV + CONV)
                    wait(act, q.sem("tr0"), i * 3)
                    act.activation(xT[0][:, :], cv[:, :], ACT.Silu).then_inc(q.sem("v"), 1)

            def epi_z(i):
                wait(act, q.sem("mm1"), i + 1)
                wait(act, q.sem("tr1"), i * 3)
                for b, (s, m) in enumerate(SPANS):
                    act.activation(xT[1][:, s:s + m], q.acc[1][:, b, 0:m], ACT.Silu).then_inc(q.sem("free1"), 1)
            for j in range(2):
                q.split_hi(act, 0, j)
            with act.Fori(0, n - 1) as i:
                epi_v(i)
                q.split_hi(act, i + 1, 0)
                silu_v(i)
                epi_z(i)
                q.split_hi(act, i + 1, 1)
            epi_v(n - 1)
            silu_v(n - 1)
            epi_z(n - 1)

        @block.gpsimd
        def _(pool):
            for j in range(2):
                q.split_lo(pool, 0, j)
            with pool.Fori(1, n) as i:
                for j in range(2):
                    q.split_lo(pool, i, j)

        @block.tensor
        def _(pe):
            def tr(i, j):
                if j == 0:
                    wait(pe, q.sem("free0") if conv is None else q.sem("v"), i * 3 + 3 if conv is None else i + 1)
                    wait(pe, q.sem("ev1"), i * 3)
                else:
                    wait(pe, q.sem("zw"), i + 1)
                    wait(pe, q.sem("ev0"), i * 3 + 3)
                for b in range(3):
                    wait(pe, q.sem(f"ev{j}"), i * 3 if b == 0 else i * 3 + b - 1)
                    transpose_out(pe, q, xT[j], b, T.eye, q.sem(f"tr{j}"))
            q.mm(pe, 0, 0, 3)
            q.mm(pe, 0, 1, 3)
            tr(0, 0)
            with pe.Fori(1, n) as i:
                q.mm(pe, i, 0, 3)
                tr(i - 1, 1)
                q.mm(pe, i, 1, 3)
                tr(i, 0)
            tr(n - 1, 1)

        @block.vector
        def _(dve):
            if conv is not None:
                dve.memset(xs[:, 0:CONV - 1], 0.0).then_inc(q.sem("xs_zero"), 1)
                dve.wait_ge(q.sem("xs_zero"), 1)

            def ev(i, j):
                wait(dve, q.sem(f"tok_out{j}"), i * 32)
                for b in range(3):
                    wait(dve, q.sem(f"tr{j}"), i * 3 + b + 1)
                    evacuate_out(dve, dve.tensor_copy, q, tok[j], b, q.sem(f"ev{j}"))

            def epi(i):
                if conv is not None:
                    wait(dve, q.sem("free0"), i * 3 + 3)
                    wait(dve, q.sem("v"), i)
                    convolve(dve, cv, xs, T.cw, conv, i, q.sem("conv"))

            def weigh(i):
                wait(dve, q.sem("free1"), i * 3 + 3)
                dve.tensor_scalar(xT[1][:, :], xT[1][:, :], hnw[:, ds(i)], None, ALU.mult).then_inc(q.sem("zw"), 1)
            epi(0)
            ev(0, 0)
            weigh(0)
            with dve.Fori(1, n) as i:
                ev(i - 1, 1)
                epi(i)
                ev(i, 0)
                weigh(i)
            ev(n - 1, 1)


def convolve(dve, cv, xs, cw, tile0, i, done):
    def w(tap):
        return cw[:, tap, ds(i + tile0)]
    dve.tensor_scalar(cv[:, :], xs[:, 0:L], w(0), None, ALU.mult).then_inc(done, 1)
    for tap in range(1, CONV):
        wait(dve, done, i * CONV + tap)
        dve.scalar_tensor_tensor(cv[:, :], xs[:, tap:tap + L], w(tap), cv[:, :], ALU.mult, ALU.add).then_inc(done, 1)


class Step:

    def __init__(self, t, j, n):
        self.t, self.j, self.n = t, j, n

    def back(self):
        return Step(self.t - 1, 1 - self.j, self.n if self.j else self.n - 1)


def over_steps(eng, body, tail):
    body(Step(0, 0, 0), False, False)
    body(Step(1, 1, 0), True, False)
    with eng.Fori(0, (NT - 3) // 2) as i:
        body(Step(i * 2 + 2, 0, i + 1), True, True)
        body(Step(i * 2 + 3, 1, i + 1), True, True)
    last = NT - 1
    body(Step(last, 0, last // 2), True, True)
    tail(Step(last, 0, last // 2))


def split_w_out(nc, S, T, tag, w_out, kts, whi, wlo, stage):
    w = w_out.rearrange("(k p) n -> p k n", p=P)

    def load(sp):
        for k in range(kts):
            wait(sp, S(f"{tag}_wlo"), k - 1)
            wait(sp, S(f"{tag}_whi"), k - 1)
            sp.dma_start(stage[k % 2], w[:, k, :]).then_inc(S(f"{tag}_w_in{k % 2}"), 16)

    def hi(act):
        for k in range(kts):
            act.wait_ge(S(f"{tag}_w_in{k % 2}"), 16 * (k // 2 + 1))
            act.activation(whi[:, k, :], stage[k % 2], ACT.Copy).then_inc(S(f"{tag}_whi"), 1)

    def lo(pool):
        for k in range(kts):
            pool.wait_ge(S(f"{tag}_w_in{k % 2}"), 16 * (k // 2 + 1))
            pool.wait_ge(S(f"{tag}_whi"), k + 1)
            pool.tensor_tensor(wlo[:, k, :], stage[k % 2], whi[:, k, :].bitcast(F32), ALU.subtract)\
                .then_inc(S(f"{tag}_wlo"), 1)
    return load, hi, lo


def gla_scan(nc, S, T, w_out, x, meta, next_norm):
    with ExitStack() as ctx:
        def sb(name, shape, dt=F32):
            return ctx.enter_context(nc.sbuf_tensor(name, shape, dt))

        def ps(name, shape):
            return ctx.enter_context(nc.psum_tensor(name, shape, F32))
        whi = sb("as_whi", [P, KT, D], F32R)
        wlo = sb("as_wlo", [P, KT, D], F32R)
        qk = [sb(f"as_qk{j}", [P, GH, 2, P]) for j in range(2)]
        ko = [sb(f"as_ko{j}", [P, GH, P]) for j in range(2)]
        v = [sb(f"as_v{j}", [P, GH, GDV]) for j in range(2)]
        z = [sb(f"as_z{j}", [P, GH, GDV]) for j in range(2)]
        hres = [sb(f"as_res{j}", [P, D]) for j in range(2)]
        St = [sb(f"as_s{j}", [P, GH, GDV]) for j in range(2)]
        decs = sb("as_dec", [P, GH, 2])
        at = sb("as_at", [P, GH, P])
        og = sb("as_og", [P, GH, GDV])
        oT_hi = sb("as_othi", [P, KT, P], F32R)
        oT_lo = sb("as_otlo", [P, KT, P], F32R)
        hn = sb("as_hn", [P, D])
        junk = sb("as_junk", [P, GDV])
        nw = sb("as_nw", [P, D])
        ss = sb("as_ss", [P, GH])
        rs = sb("as_rs", [P, GH])
        ss2 = sb("as_ss2", [P, 1])
        rs2 = sb("as_rs2", [P, 1])
        pA = ps("as_pA", [P, GH, P])
        pO = ps("as_pO", [P, GH, GDV])
        pU = ps("as_pU", [P, GH, GDV])
        pT = ps("as_pT", [P, GH, P])
        pY = ps("as_pY", [P, 2, 512])
        bank = [pT, pA]
        w_load, w_hi, w_lo = split_w_out(nc, S, T, "as", w_out, KT, whi, wlo, [og[:, :, :].rearrange("p h v -> p (h v)"), hn[:, :]])
        block = ctx.enter_context(nc.Block())
        NLOAD = 4

        @block.sync
        def _(sp):
            sp.wait_ge(S("as_hzero"), 1)
            sp.dma_start(nw[:, :], bc(next_norm, [P, D])).then_inc(S("as_nw_in"), 16)

            def load(s):
                t, j = s.t, s.j
                sem = S(f"as_in{j}")
                wait(sp, S("as_inter"), t * 2 - 2)
                wait(sp, S("as_og"), t * 4 - 4)
                sp.dma_start(qk[j][:, :, :, :].rearrange("p h w n -> p (h w) n"),
                             T.gla_qk.rearrange("h w p n -> p (h w) n")[:, :, ds(t * P, P)]).then_inc(sem, 16)
                sp.dma_start(ko[j][:, :, :].rearrange("p h d -> p (h d)"), T.gla_ko[ds(t * P, P), :]).then_inc(sem, 16)
                sp.dma_start(v[j][:, :, :].rearrange("p h d -> p (h d)"), T.gla_v[ds(t * P, P), :]).then_inc(sem, 16)
                sp.dma_start(z[j][:, :, :].rearrange("p h d -> p (h d)"), T.gla_z[ds(t * P, P), :]).then_inc(sem, 16)

            def load_residual(s):
                t, j = s.t, s.j
                sem = S(f"as_in_res{j}")
                if isinstance(t, int) and t == 0:
                    sp.dma_start(hres[0][PAD:P, :], meta).then_inc(sem, 16)
                else:
                    wait(sp, S("as_hn"), t - 1)
                    wait(sp, S("as_h1_out"), t * 16 - 16)
                    sp.dma_start(hres[j][:, :], x[ds((t - 1) * P, P), :]).then_inc(sem, 16)

            def store(s):
                wait(sp, S("as_h1"), s.t * 2 + 2)
                sp.dma_start(T.h1[ds(s.t * P, P), :], hres[s.j][:, :]).then_inc(S("as_h1_out"), 16)

            def turn(last, nxt):
                load(nxt)
                store(last)
                load_residual(nxt)
            load(Step(0, 0, 0))
            w_load(sp)
            load(Step(1, 1, 0))
            load_residual(Step(0, 0, 0))
            load_residual(Step(1, 1, 0))
            with sp.Fori(0, (NT - 3) // 2) as i:
                turn(Step(i * 2, 0, i), Step(i * 2 + 2, 0, i + 1))
                turn(Step(i * 2 + 1, 1, i), Step(i * 2 + 3, 1, i + 1))
            turn(Step(NT - 3, 0, (NT - 3) // 2), Step(NT - 1, 0, (NT - 1) // 2))
            for t in range(NT - 2, NT):
                store(Step(t, t % 2, t // 2))
            sp.wait_ge(S("as_h1_out"), 16 * NT)

        @block.tensor
        def _(pe):
            pe.wait_ge(S("as_init"), 2)

            def arrived(s):
                wait(pe, S(f"as_in{s.j}"), s.n * (16 * NLOAD) + 16 * NLOAD)

            def outer(s, ch):
                wait(pe, S("as_su"), s.t * 8 + 4 * ch)
                r = slice(ch * C, ch * C + C)
                for h in range(GH):
                    mm = pe.matmul(pU[:, h, :], ko[s.j][r, h, :], v[s.j][r, h, :], start=True, stop=True)
                mm.then_inc(S("as_u"), 1)

            def inter(s, ch):
                wait(pe, S("as_su"), s.t * 8 + 4 * ch)
                r = slice(ch * C, ch * C + C)
                for h in range(GH):
                    mm = pe.matmul(pO[r, h, :], qk[s.j][:, h, 0, r], St[ch][:, h, :], start=False, stop=True,
                                   skip_group_check=True)
                mm.then_inc(S("as_inter"), 1)

            def transposes(src, name, s, before):
                for b in range(2):
                    wait(pe, *before(b))
                    for c in range(4):
                        kt = 4 * b + c
                        mm = pe.transpose(bank[b][:, c, :], src[:, kt * P:(kt + 1) * P], T.eye)
                    mm.then_inc(S(name), 1)

            def scan(s, has2):
                arrived(s)
                wait(pe, S("as_otlo"), s.t * 2)
                for h in range(GH):
                    mm = pe.matmul(pA[:, h, :], qk[s.j][:, h, 1, :], qk[s.j][:, h, 0, :], start=True, stop=True)
                mm.then_inc(S("as_a"), 1)
                outer(s, 0)
                if has2:
                    norm_out(s.back().back(), s)
                wait(pe, S("as_at"), s.t + 1)
                wait(pe, S("as_og"), s.t * 4)
                for h in range(GH):
                    mm = pe.matmul(pO[:, h, :], at[:, h, :], v[s.j][:, h, :], start=(h % 2 == 0), stop=False,
                                   skip_group_check=True)
                inter(s, 0)
                outer(s, 1)
                inter(s, 1)

            def norm_out(s2, s):
                wait(pe, S("as_hn"), s2.t + 1)
                ogs = hn[:, :]
                for b in range(2):
                    if b == 1 and s is not None:
                        wait(pe, S("as_at"), s.t + 1)
                    if b == 0:
                        wait(pe, S("as_otlo"), s2.t * 2 + 4 if s is not None else NT * 2)
                    if s is None:
                        wait(pe, S("as_hnlo"), s2.t * 2 + b - 1 if b else s2.t * 2)
                    for c in range(4):
                        kt = 4 * b + c
                        mm = pe.transpose(bank[b][:, c, :], ogs[:, kt * P:(kt + 1) * P], T.eye)
                    mm.then_inc(S("as_hnT"), 1)

            def out_project(s):
                wait(pe, S("as_otlo"), s.t * 2 + 2)
                wait(pe, S("as_h1"), s.t * 2)
                for n in range(2):
                    k = 0
                    for kt in range(KT):
                        for o, w in ((oT_hi, whi), (oT_hi, wlo), (oT_lo, whi)):
                            mm = pe.matmul(pY[:, n, :], o[:, kt, :], w[:, kt, n * 512:(n + 1) * 512],
                                           start=(k == 0), stop=(k == 3 * KT - 1))
                            k += 1
                    mm.then_inc(S("as_y"), 1)

            def outputs(s, has2):
                wait(pe, S("as_og"), s.t * 4 + 4)
                if has2:
                    wait(pe, S("as_hnlo"), s.t * 2 - 2)
                for b in range(2):
                    if b == 1:
                        wait(pe, S("as_at"), s.t + 1)
                    for c in range(4):
                        kt = 4 * b + c
                        mm = pe.transpose(bank[b][:, c, :], og[:, kt // 2, (kt % 2) * P:(kt % 2 + 1) * P], T.eye)
                    mm.then_inc(S("as_oT"), 1)

            def body(s, has1, has2):
                scan(s, has2)
                if has1:
                    if not has2:
                        pe.wait_ge(S("as_wlo"), KT)
                    out_project(s.back())
                outputs(s, has2)

            def tail(s):
                norm_out(s.back(), None)
                out_project(s)
                norm_out(s, None)
            over_steps(pe, body, tail)

        @block.vector
        def _(dve):
            dve.memset(at[:, :, :], 0.0).then_inc(S("as_init"), 1)
            dve.memset(St[0][:, :, :], 0.0).then_inc(S("as_init"), 1)
            dve.memset(hres[0][:, :], 0.0).then_inc(S("as_hzero"), 1)
            dve.wait_ge(S("as_init"), 2)
            dve.wait_ge(S("as_nw_in"), 16)

            def update(s, ch):
                wait(dve, S("as_u"), s.t * 2 + ch + 1)
                if ch:
                    wait(dve, S("as_inter"), s.t * 2 + 1)
                    wait(dve, S("as_su"), s.t * 8 + 4)
                else:
                    wait(dve, S("as_inter"), s.t * 2)
                    wait(dve, S("as_dec"), s.t + 1)
                    wait(dve, S("as_su"), s.t * 8)
                for h in range(GH):
                    dve.scalar_tensor_tensor(St[1 - ch][:, h, :], St[ch][:, h, :], decs[:, h, ch:ch + 1],
                                             pU[:, h, :], ALU.mult, ALU.add).then_inc(S("as_su"), 1)

            def low(dst, hi, t, name, pre):
                for b in range(2):
                    wait(dve, S(f"as_{pre}hi"), t * 2 + b + 1)
                    dve.tensor_tensor(dst(b), bank[b][:, :, :], hi(b).bitcast(F32), ALU.subtract)\
                       .then_inc(S(f"as_{pre}lo"), 1)

            def norm_low(s):
                low(lambda b: T.hn_lo[:, 4 * b:4 * b + 4, ds(s.t * P, P)],
                    lambda b: T.hn_hi[:, 4 * b:4 * b + 4, ds(s.t * P, P)], s.t, "hn", "hn")

            def residual(s):
                wait(dve, S(f"as_in_res{s.j}"), s.n * 16 + 16)
                for n in range(2):
                    wait(dve, S("as_y"), s.t * 2 + n + 1)
                    dve.tensor_tensor(hres[s.j][:, n * 512:(n + 1) * 512], pY[:, n, :],
                                      hres[s.j][:, n * 512:(n + 1) * 512], ALU.add).then_inc(S("as_h1"), 1)

            def normed(s):
                wait(dve, S("as_rs2"), s.t + 1)
                wait(dve, S("as_h1"), s.t * 2 + 2)
                wait(dve, S("as_hnT"), s.t * 2)
                dve.scalar_tensor_tensor(hn[:, :], hres[s.j][:, :], rs2[:, 0:1], nw[:, :], ALU.mult, ALU.mult)\
                   .then_inc(S("as_hn"), 1)

            def body(s, has1, has2):
                wait(dve, S("as_su"), s.t * 8)
                dve.tensor_copy(decs[:, :, :], T.dec[:, :, ds(s.t * 2, 2)]).then_inc(S("as_dec"), 1)
                waits_apart(dve, T.dve_carrier,
                            (S("as_a"), s.t + 1),
                            (S("as_inter"), s.t * 2))
                dve.copy_predicated(at[:, :, :], bc(T.causal.bitcast(I32), [P, GH, P]), pA[:, :, :])\
                   .then_inc(S("as_at"), 1)
                update(s, 0)
                if has2:
                    norm_low(s.back().back())
                update(s, 1)
                wait(dve, S("as_rs"), s.t + 1)
                wait(dve, S("as_in%d" % s.j), s.n * (16 * NLOAD) + 16 * NLOAD)
                wait(dve, S("as_oT"), s.t * 2)
                if not has1:
                    dve.wait_ge(S("as_wlo"), KT)
                for h in range(GH):
                    dve.scalar_tensor_tensor(og[:, h, :], pO[:, h, :], rs[:, h:h + 1], z[s.j][:, h, :],
                                             ALU.mult, ALU.mult).then_inc(S("as_og"), 1)
                if has1:
                    residual(s.back())
                low(lambda b: oT_lo[:, 4 * b:4 * b + 4, :], lambda b: oT_hi[:, 4 * b:4 * b + 4, :], s.t, "ot", "ot")
                if has1:
                    normed(s.back())

            def tail(s):
                norm_low(s.back())
                residual(s)
                normed(s)
                norm_low(s)
            over_steps(dve, body, tail)

        @block.scalar
        def _(act):
            w_hi(act)

            def high(dst, s, name):
                for b in range(2):
                    wait(act, S(name), s.t * 2 + b + 1)
                    act.activation(dst(b), bank[b][:, :, :], ACT.Copy)\
                       .then_inc(S("as_othi" if name == "as_oT" else "as_hnhi"), 1)

            def norm_high(s):
                high(lambda b: T.hn_hi[:, 4 * b:4 * b + 4, ds(s.t * P, P)], s, "as_hnT")

            def squares2(s):
                wait(act, S("as_h1"), s.t * 2 + 2)
                wait(act, S("as_mean2"), s.t)
                wait(act, S("as_hnT"), s.t * 2)
                act.activation(hn[:, :], hres[s.j][:, :], ACT.Square, accum_out=ss2[:, :]).then_inc(S("as_ss2"), 1)

            def body(s, has1, has2):
                if has2:
                    norm_high(s.back().back())
                wait(act, S("as_inter"), s.t * 2 + 2)
                wait(act, S("as_mean"), s.t)
                for h in range(GH):
                    wait(act, S("as_ss"), s.t * 4 + h)
                    act.activation(junk[:, :], pO[:, h, :], ACT.Square, accum_out=ss[:, h:h + 1])\
                       .then_inc(S("as_ss"), 1)
                wait(act, S("as_y"), s.t * 2)
                high(lambda b: oT_hi[:, 4 * b:4 * b + 4, :], s, "as_oT")
                if has1:
                    squares2(s.back())

            def tail(s):
                norm_high(s.back())
                squares2(s)
                norm_high(s)
            over_steps(act, body, tail)

        @block.gpsimd
        def _(pool):
            w_lo(pool)

            def rsqrt(dst, src, width, t, ready, mean, out, used):
                waits_apart(pool, T.pool_carrier,
                            ready,
                            used)
                pool.tensor_scalar(dst[:, :], src[:, :], 1.0 / width, EPS, ALU.mult, ALU.add).then_inc(S(mean), 1)
                wait(pool, S(mean), t + 1)
                pool.tensor_tensor(dst[:, :], dst[:, :], bc(T.minus_half[:, 0:1], list(dst.shape)), ALU.pow)\
                    .then_inc(S(out), 1)

            def rs_h1(s):
                rsqrt(rs2, ss2, D, s.t, (S("as_ss2"), s.t + 1), "as_mean2", "as_rs2", (S("as_hn"), s.t))

            def body(s, has1, has2):
                rsqrt(rs, ss, GDV, s.t, (S("as_ss"), s.t * 4 + 4), "as_mean", "as_rs", (S("as_og"), s.t * 4))
                if has1:
                    rs_h1(s.back())

            def tail(s):
                rs_h1(s)
            over_steps(pool, body, tail)


def gdn_gate(nc, S, T, w_in, a_log, dt_bias, conv_w, head_norm):
    with ExitStack() as ctx:
        def sb(name, shape, dt=F32):
            return ctx.enter_context(nc.sbuf_tensor(name, shape, dt))
        st = sb("ng_w", [P, KT, P])
        hi = sb("ng_whi", [P, KT, P], F32R)
        lo = sb("ng_wlo", [P, KT, P], F32R)
        al = sb("ng_alog", [NH, 1])
        ea = sb("ng_ea", [NH, 1])
        dt = sb("ng_dt", [NH, 1])
        cm = sb("ng_starts", [NH, L])
        ax = sb("ng_ax", [NH, L])
        mx = sb("ng_mx", [NH, L])
        g = sb("ng_g", [NH, L])
        be = sb("ng_beta", [NH, L])
        NCT = (2 * NQK + NV) // P
        cwn = sb("ng_cw", [NCT, CONV, P])
        acc = ctx.enter_context(nc.psum_tensor("ng_acc", [P, 3, 512], F32))
        cps = ctx.enter_context(nc.psum_tensor("ng_cps", [P, CONV, NCT], F32))
        block = ctx.enter_context(nc.Block())
        c0 = 2 * NQK + 2 * NV
        A0 = 32
        wv = w_in.rearrange("(k p) n -> p k n", p=P)

        @block.sync
        def _(sp):
            sp.wait_ge(S("ng_zero"), 1)
            sp.dma_start(st[:, :, 0:NH], wv[:, :, c0:c0 + NH]).then_inc(S("ng_w_in"), 16)
            sp.dma_start(st[:, :, A0:A0 + NH], wv[:, :, c0 + NH:c0 + 2 * NH]).then_inc(S("ng_w_in"), 16)
            sp.dma_start(al[:, :], a_log.rearrange("(h o) -> h o", o=1)).then_inc(S("ng_small_in"), 16)
            sp.dma_start(dt[:, :], dt_bias.rearrange("(h o) -> h o", o=1)).then_inc(S("ng_small_in"), 16)
            sp.dma_start(cm[:, :], T.starts_dram[0:NH, :]).then_inc(S("ng_small_in"), 16)
            sp.dma_start(cwn[:, :, :], conv_w.rearrange("k (t p) -> t k p", p=P)).then_inc(S("ng_cw_in"), 16)
            sp.dma_start(T.hnw2[:, :], head_norm).then_inc(S("ng_hnw_in"), 16)
            sp.wait_ge(S("ng_g"), 1)
            sp.wait_ge(S("ng_beta"), 4)
            for w, src in ((0, g), (1, be)):
                sp.dma_start(T.gb[2:, :, w, :].rearrange("c h t -> h c t"),
                             src[:, NMETA:].rearrange("h (c t) -> h c t", t=C)).then_inc(S("ng_out"), 16)
                sp.dma_start(T.gb[1, :, w, C - NMETA:C], src[:, 0:NMETA]).then_inc(S("ng_out"), 16)
            sp.wait_ge(S("ng_out"), 64)
            sp.wait_ge(S("ng_hnw_in"), 16)

        @block.scalar
        def _(act):
            act.wait_ge(S("ng_w_in"), 32)
            act.activation(hi[:, :, :], st[:, :, :], ACT.Copy).then_inc(S("ng_whi"), 1)
            act.wait_ge(S("ng_small_in"), 48)
            act.activation(ea[:, :], al[:, :], ACT.Exp).then_inc(S("ng_ea"), 1)
            act.wait_ge(S("ng_logit"), 1)
            act.wait_ge(S("ng_abs"), 1)
            for b, (s, m) in enumerate(SPANS):
                act.activation(be[:, s:s + m], acc[0:NH, b, 0:m], ACT.Exp, scale=-1.0).then_inc(S("ng_ebeta"), 1)
            act.activation(ax[:, :], ax[:, :], ACT.Exp, scale=-1.0).then_inc(S("ng_e"), 1)
            act.wait_ge(S("ng_e"), 1)
            act.activation(ax[:, :], ax[:, :], ACT.Ln, bias=1.0).then_inc(S("ng_ln"), 1)

        @block.gpsimd
        def _(pool):
            pool.memset(st[:, :, :], 0.0).then_inc(S("ng_zero"), 1)
            pool.wait_ge(S("ng_whi"), 1)
            pool.tensor_tensor(lo[:, :, :], st[:, :, :], hi[:, :, :].bitcast(F32), ALU.subtract)\
                .then_inc(S("ng_wlo"), 1)

        @block.tensor
        def _(pe):
            pe.wait_ge(S("ng_cw_in"), 16)
            for k in range(CONV):
                mm = pe.transpose(cps[:, k, :], cwn[:, k, :], T.k[0:NCT, K_EYE:K_EYE + NCT])
            mm.then_inc(S("ng_cwT"), 1)
            pe.wait_ge(S("ng_wlo"), 1)
            project(pe, acc, hi, lo, T).then_inc(S("ng_logit"), 1)

        @block.vector
        def _(dve):
            dve.wait_ge(S("ng_cwT"), 1)
            dve.tensor_copy(T.cw[:, :, :], cps[:, :, :]).then_inc(S("ng_cw"), 1)
            dve.wait_ge(S("ng_logit"), 1)
            dve.wait_ge(S("ng_small_in"), 48)
            for b, (s, m) in enumerate(SPANS):
                dve.tensor_scalar(mx[:, s:s + m], acc[A0:A0 + NH, b, 0:m], dt[:, 0:1], 0.0, ALU.add, ALU.max)\
                   .then_inc(S("ng_max"), 1)
            for b, (s, m) in enumerate(SPANS):
                dve.tensor_scalar(ax[:, s:s + m], acc[A0:A0 + NH, b, 0:m], dt[:, 0:1], 0.0, ALU.add, ALU.min)\
                   .then_inc(S("ng_min"), 1)
            dve.wait_ge(S("ng_max"), 3)
            dve.wait_ge(S("ng_min"), 3)
            dve.tensor_tensor(ax[:, :], mx[:, :], ax[:, :], ALU.subtract).then_inc(S("ng_abs"), 1)
            dve.wait_ge(S("ng_ebeta"), 3)
            dve.tensor_scalar(be[:, :], be[:, :], 1.0, None, ALU.add).then_inc(S("ng_beta"), 1)
            dve.wait_ge(S("ng_beta"), 1)
            dve.reciprocal(be[:, :], be[:, :]).then_inc(S("ng_beta"), 3)
            dve.wait_ge(S("ng_ln"), 1)
            dve.wait_ge(S("ng_max"), 3)
            dve.wait_ge(S("ng_ea"), 1)
            dve.tensor_tensor(mx[:, :], mx[:, :], ax[:, :], ALU.add).then_inc(S("ng_sp"), 1)
            dve.wait_ge(S("ng_sp"), 1)
            dve.tensor_scalar(mx[:, :], mx[:, :], ea[:, 0:1], -1.0, ALU.mult, ALU.mult).then_inc(S("ng_sp"), 1)
            dve.wait_ge(S("ng_sp"), 2)
            dve.tensor_tensor_scan(g[:, :], cm[:, :], mx[:, :], 0.0, ALU.mult, ALU.add).then_inc(S("ng_g"), 1)


def gdn_qk(nc, S, T, w_in):
    n = NH
    with ExitStack() as ctx:
        q = Proj(nc, S, T, ctx, "nq", w_in, lambda i, j: j * NQK + i * P)

        def sb(name, shape):
            return ctx.enter_context(nc.sbuf_tensor(name, shape, F32))
        xs = sb("nq_xs", [P, CONV - 1 + L])
        cv = sb("nq_cv", [P, L])
        xT = [sb(f"nq_x{j}", [P, L]) for j in range(2)]
        tok = [sb(f"nq_tok{j}", [P, NT, P]) for j in range(2)]
        sq = sb("nq_sq", [P, NT, P])
        ss = [sb(f"nq_ss{j}", [P, NT]) for j in range(2)]
        xn = [sb(f"nq_xn{j}", [P, L]) for j in range(2)]
        block = ctx.enter_context(nc.Block())

        @block.sync
        def _(sp):
            def store_tok(i):
                wait(sp, q.sem("norm1"), i + 1)
                store_tokens(sp, T.gdn_k, tok[1], i * P, NQK, q.sem("tok_out"))

            def store(i, j):
                wait(sp, q.sem(f"evn{j}"), i * 3 + 3)
                sp.dma_start(T.gdn_qk[j, ds(i), :, PAD:TP].rearrange("a p n -> p (a n)"), xn[j][:, :])\
                  .then_inc(q.sem(f"out{j}"), 16)
            for j in range(2):
                q.load(sp, 0, j)
            for j in range(2):
                q.load(sp, 1, j)
            with sp.Fori(0, n - 2) as i:
                for j in range(2):
                    q.load(sp, i + 2, j)
                store_tok(i)
                for j in range(2):
                    store(i, j)
            for i in range(n - 2, n):
                store_tok(i)
                for j in range(2):
                    store(i, j)
            sp.wait_ge(q.sem("tok_out"), 32 * n)
            for j in range(2):
                sp.wait_ge(q.sem(f"out{j}"), 16 * n)

        @block.scalar
        def _(act):
            def copy(i, j):
                wait(act, q.sem(f"mm{j}"), i + 1)
                if j == 0:
                    wait(act, q.sem("conv1"), i * CONV)
                else:
                    wait(act, q.sem("conv0"), i * CONV + CONV)
                for b, (s, m) in enumerate(SPANS):
                    act.activation(xs[:, CONV - 1 + s:CONV - 1 + s + m], q.acc[j][:, b, 0:m], ACT.Copy)\
                       .then_inc(q.sem(f"free{j}"), 1)

            def silu(i, j):
                wait(act, q.sem(f"conv{j}"), i * CONV + CONV)
                wait(act, q.sem(f"tr{j}"), i * 3)
                act.activation(xT[j][:, :], cv[:, :], ACT.Silu).then_inc(q.sem(f"silu{j}"), 1)

            def square(i, j):
                wait(act, q.sem(f"ev{j}"), i * 3 + 3)
                if j == 0:
                    wait(act, q.sem("ss1"), i)
                else:
                    wait(act, q.sem("ss0"), i + 1)
                act.activation(sq[:, :, :], tok[j][:, :, :], ACT.Square).then_inc(q.sem(f"sq{j}"), 1)

            def back(i, j):
                wait(act, q.sem(f"out{j}"), i * 16)
                for b in range(3):
                    wait(act, q.sem(f"trn{j}"), i * 3 + b + 1)
                    if b < 2:
                        s = NMETA + 4 * b * P
                        act.activation(xn[j][:, s:s + 4 * P], (q.trA, q.trB)[b][:, :, :].rearrange("p a b -> p (a b)"),
                                       ACT.Copy).then_inc(q.sem(f"evn{j}"), 1)
                    else:
                        act.activation(xn[j][:, 0:NMETA], q.trA[:, 0, 0:NMETA], ACT.Copy).then_inc(q.sem(f"evn{j}"), 1)

            def body(i, first, last):
                copy(i, 0)
                if not last:
                    q.split_hi(act, i + 1, 0)
                if not first:
                    square(i - 1, 1)
                    back(i - 1, 0)
                silu(i, 0)
                copy(i, 1)
                if not last:
                    q.split_hi(act, i + 1, 1)
                square(i, 0)
                if not first:
                    back(i - 1, 1)
                silu(i, 1)
            for j in range(2):
                q.split_hi(act, 0, j)
            body(0, True, False)
            with act.Fori(1, n - 1) as i:
                body(i, False, False)
            body(n - 1, False, True)
            square(n - 1, 1)
            back(n - 1, 0)
            back(n - 1, 1)

        @block.gpsimd
        def _(pool):
            def norm(i, j):
                waits_apart(pool, T.pool_carrier,
                            (q.sem(f"ss{j}"), i + 1))
                pool.tensor_scalar(ss[j][:, :], ss[j][:, :], EPS, (float(NDK), 1.0)[j], ALU.add, ALU.mult)\
                    .then_inc(q.sem(f"sum{j}"), 1)
                wait(pool, q.sem(f"sum{j}"), i + 1)
                pool.tensor_tensor(ss[j][:, :], ss[j][:, :], bc(T.minus_half[:, 0:1], [P, NT]), ALU.pow)\
                    .then_inc(q.sem(f"rs{j}"), 1)
                wait(pool, q.sem(f"rs{j}"), i + 1)
                pool.tensor_tensor(tok[j][:, :, :], tok[j][:, :, :],
                                   bc(ss[j][:, :].rearrange("p (t o) -> p t o", o=1), [P, NT, P]), ALU.mult)\
                    .then_inc(q.sem(f"norm{j}"), 1)

            def body(i, first, last):
                if not last:
                    q.split_lo(pool, i + 1, 0)
                if not first:
                    norm(i - 1, 1)
                if not last:
                    q.split_lo(pool, i + 1, 1)
                norm(i, 0)
            for j in range(2):
                pool.memset(tok[j][:, :, :], 0.0).then_inc(q.sem("tok_zero"), 1)
            for j in range(2):
                q.split_lo(pool, 0, j)
            body(0, True, False)
            with pool.Fori(1, n - 1) as i:
                body(i, False, False)
            body(n - 1, False, True)
            norm(n - 1, 1)

        @block.tensor
        def _(pe):
            def tr(i, j):
                wait(pe, q.sem(f"silu{j}"), i + 1)
                if j == 1:
                    wait(pe, q.sem("ev0"), i * 3 + 3)
                    wait(pe, q.sem("evn1"), i * 3)
                else:
                    wait(pe, q.sem("ev1"), i * 3)
                    wait(pe, q.sem("evn0"), i * 3)
                for b in range(3):
                    if b == 2:
                        wait(pe, q.sem(f"ev{j}"), i * 3 + 1)
                    transpose_out(pe, q, xT[j], b, T.eye, q.sem(f"tr{j}"))

            def back(i, j):
                wait(pe, q.sem(f"norm{j}"), i + 1)
                yield_to = q.sem("ev1") if j == 0 else q.sem("ev0")
                wait(pe, yield_to, i * 3 + 3 if j == 0 else (i * 3 + 6 if not isinstance(i, int) else min(i * 3 + 6, 3 * n)))
                if j == 1:
                    wait(pe, q.sem("evn0"), i * 3 + 3)
                for b in range(3):
                    if b == 2:
                        waits_apart(pe, T.pe_carrier,
                                    (q.sem(f"evn{j}"), i * 3 + 1))
                    bankd = (q.trA, q.trB, q.trA)[b]
                    if b < 2:
                        for c in range(4):
                            mm = pe.transpose(bankd[:, c, :], tok[j][:, 1 + 4 * b + c, :], T.eye)
                    else:
                        mm = pe.transpose(bankd[:, 0, 0:NMETA], tok[j][0:NMETA, 0, :],
                                          T.k[0:NMETA, K_EYE:K_EYE + NMETA])
                    mm.then_inc(q.sem(f"trn{j}"), 1)
            q.mm(pe, 0, 0, 3)
            q.mm(pe, 0, 1, 3)
            tr(0, 0)
            with pe.Fori(1, n) as i:
                q.mm(pe, i, 0, 3)
                tr(i - 1, 1)
                back(i - 1, 0)
                q.mm(pe, i, 1, 3)
                tr(i, 0)
                back(i - 1, 1)
            tr(n - 1, 1)
            back(n - 1, 0)
            back(n - 1, 1)

        @block.vector
        def _(dve):
            dve.memset(xs[:, 0:CONV - 1], 0.0).then_inc(q.sem("xs_zero"), 1)
            dve.wait_ge(q.sem("xs_zero"), 1)
            dve.wait_ge(q.sem("tok_zero"), 2)

            def ev(i, j):
                if j == 1:
                    wait(dve, q.sem("tok_out"), i * 32)
                wait(dve, q.sem(f"trn{j}"), i * 3)
                for b in range(3):
                    wait(dve, q.sem(f"tr{j}"), i * 3 + b + 1)
                    evacuate_out(dve, dve.tensor_copy, q, tok[j], b, q.sem(f"ev{j}"))
                wait(dve, q.sem(f"sq{j}"), i + 1)
                wait(dve, q.sem(f"norm{j}"), i)
                dve.tensor_reduce(ss[j][:, :], sq[:, :, :], AX.X, ALU.add).then_inc(q.sem(f"ss{j}"), 1)

            def conv(i, j):
                wait(dve, q.sem(f"free{j}"), i * 3 + 3)
                if j == 0:
                    wait(dve, q.sem("silu1"), i)
                else:
                    wait(dve, q.sem("silu0"), i + 1)
                convolve(dve, cv, xs, T.cw, j * NH, i, q.sem(f"conv{j}"))
            conv(0, 0)
            ev(0, 0)
            conv(0, 1)
            with dve.Fori(1, n) as i:
                ev(i - 1, 1)
                conv(i, 0)
                ev(i, 0)
                conv(i, 1)
            ev(n - 1, 1)


class Chunk:

    def __init__(self, c, j):
        self.c, self.m, self.j, self.par = c, c - 1, j, 1 - j

    def ahead(self, k):
        return Chunk(self.c + k, (self.j + k) % 2)


def over_chunks(eng, chunk, tail):
    chunk(Chunk(1, 1), None, False, 2)
    chunk(Chunk(2, 0), 1, False, 2)
    chunk(Chunk(3, 1), 1, False, 2)
    with eng.Fori(2, NT - 1) as t:
        chunk(Chunk(t * 2, 0), t, True, 2)
        chunk(Chunk(t * 2 + 1, 1), t, True, 2)
    chunk(Chunk(2 * NT - 2, 0), NT - 1, True, 1)
    chunk(Chunk(2 * NT - 1, 1), NT - 1, True, 0)
    tail()


def gdn_scan(nc, S, T, w_out, out_norm, out):
    KO = NV // P
    LV = len(LEVELS)
    R = [slice(0, C), slice(C, P)]
    with ExitStack() as ctx:
        def sb(name, shape, dt=F32):
            return ctx.enter_context(nc.sbuf_tensor("ns_" + name, shape, dt))

        def ps(name, shape):
            return ctx.enter_context(nc.psum_tensor("ns_" + name, shape, F32))
        whi = sb("whi", [P, KO, D], F32R)
        wlo = sb("wlo", [P, KO, D], F32R)
        kq = sb("kq", [P, NH, 2, C])
        kqd = sb("kqd", [P, NH, 2, C])
        kt = sb("kt", [P, HP, NDK])
        v = sb("v", [P, HP, NDV])
        og = sb("og", [P, HP, NDV])
        gb = sb("gb", [P, NH, 2, C])
        gp = sb("gp", [P, HP, 2, C])
        gbc = sb("gbc", [P, HP, 2])
        St = sb("s", [P, NH, NDV])
        er = gb[:, :, 0, :]
        dec = [sb(f"dec{n}", [P, NH]) for n in range(2)]
        d1 = sb("d1", [P, HP, C])
        junk = d1[:, :, :].rearrange("p h c -> p (h c)")
        dn = [sb(f"dn{n}", [P, HP, C]) for n in range(2)]
        dx = sb("dx", [P, HP, C])
        mm2 = sb("mm2", [P, 2, HP, C])
        M, mtf = mm2[:, 0], mm2[:, 1]
        tg = mm2[:, :, :, :].rearrange("p a h c -> p (a h) c")
        low = [mtf] + [sb(f"low{n}", [P, HP, C])[:, :, :] for n in range(1, 1 + LV)]
        U = [sb(f"u{n}", [P, HP, C]) for n in range(2)]
        Ti = sb("ti", [P, HP, C])
        Pm = sb("pm", [P, HP, C])
        kdl = sb("kdl", [P, HP])
        kdec = kt
        vn = sb("vn", [P, HP, NDV])
        with nc.sbuf_tensor("ns_stage", [P, 4, D], F32) as early:
            pass
        oT_hi = sb("othi", [P, KO, P], F32R)
        oT_lo = sb("otlo", [P, KO, P], F32R)
        h = sb("h", [P, D])
        nw = sb("nw", [P, D])
        ss = sb("ss", [P, HP])
        ss2 = sb("ss2", [P, 1])
        pX = [ps(f"px{p}", [P, HP, NDV]) for p in range(2)]
        p4 = ps("p4", [P, 512])
        p56 = ps("p56", [P, 2, 512])
        pY = ps("py", [P, 512])
        pKK = p4[:, 0:HP * C].rearrange("p (h c) -> p h c", c=C)
        pQK = p4[:, HP * C:2 * HP * C].rearrange("p (h c) -> p h c", c=C)
        pP, pUP, pPT = pKK, pQK, pKK
        pS = [p56[:, p, :].rearrange("p (h v) -> p h v", v=NDV) for p in range(2)]
        pT = [p56[:, b, :].rearrange("p (x c) -> p x c", c=C) for b in range(2)]
        block = ctx.enter_context(nc.Block())

        w = w_out.rearrange("(k p) n -> p k n", p=P)
        stage = [early[:, b, :] for b in range(4)] + [h[:, :], nw[:, :]]
        NS = len(stage)
        parts = [range(0, NS), range(NS, NS + 5), range(NS + 5, KO)]

        def w_load(sp, part):
            for k in parts[part]:
                wait(sp, S("ns_wlo"), k - NS + 1)
                wait(sp, S("ns_whi"), k - NS + 1)
                sp.dma_start(stage[k % NS], w[:, k, :]).then_inc(S(f"ns_w_in{k % NS}"), 16)

        def w_hi(act, part):
            for k in parts[part]:
                act.wait_ge(S(f"ns_w_in{k % NS}"), 16 * (k // NS + 1))
                act.activation(whi[:, k, :], stage[k % NS], ACT.Copy).then_inc(S("ns_whi"), 1)

        def w_lo(pool, part):
            for k in parts[part]:
                pool.wait_ge(S(f"ns_w_in{k % NS}"), 16 * (k // NS + 1))
                pool.wait_ge(S("ns_whi"), k + 1)
                pool.tensor_tensor(wlo[:, k, :], stage[k % NS], whi[:, k, :].bitcast(F32), ALU.subtract)\
                    .then_inc(S("ns_wlo"), 1)

        def part_of(t, ch):
            return 1 if t is None else 2 if isinstance(t, int) and t == 1 and ch.j == 0 else None

        def eye_p(shape):
            return bc(T.k[:, K_EYEP:K_EYEP + C].rearrange("p (o c) -> p o c", o=1), shape)

        def mask(col):
            return bc(T.k[:, col:col + C].rearrange("p (o c) -> p o c", o=1), [P, HP, C])

        def transposed(t, ch, has_prev):
            return t is not None and (ch.j == 1 or has_prev)

        @block.sync
        def _(sp):
            def tokens(dst, src, ch, width, swap, sem):
                for p in range(2):
                    rows = R[1 - p] if swap else R[p]
                    sp.dma_start(dst[rows, :, :],
                                 src[ds(ch.c * C, C), :].rearrange("t (h p d) -> t h p d", p=2, d=width)[:, :, p, :])\
                      .then_inc(sem, 16)

            def load_gp(ch):
                m = ch.m
                wait(sp, S("ns_mtf"), m * 2)
                wait(sp, S("ns_kdl"), m)
                wait(sp, S("ns_d1"), m)
                wait(sp, S("ns_tg"), m)
                for p in range(2):
                    src = T.gb[ds(ch.c)].rearrange("o (h p) w c -> o h p w c", p=2)[:, :, p]
                    sp.dma_start(gp[R[p], :, :, :], bc(src, [C, HP, 2, C])).then_inc(S("ns_in_g"), 16)

            def load_kq(ch):
                m = ch.m
                wait(sp, S("ns_kqd"), m * 3)
                wait(sp, S("ns_g"), m)
                for w_ in range(2):
                    for p in range(2):
                        src = T.gdn_qk[w_].rearrange("(h p) d n -> d h p n", p=2)[:, :, p, ds(ch.c * C, C)]
                        slot = 1 - w_ if p == 0 else w_
                        sp.dma_start(kq[:, p::2, slot, :], src).then_inc(S("ns_in_kq"), 16)
                wait(sp, S("ns_dec"), m)
                sp.dma_start(gb[:, :, :, :], bc(T.gb[ds(ch.c)], [P, NH, 2, C])).then_inc(S("ns_in_gb"), 16)

            def load_v(ch):
                wait(sp, S("ns_v"), ch.m)
                tokens(v, T.gdn_v, ch, NDV, False, S("ns_in_v"))

            def load_kt(ch):
                wait(sp, S("ns_ds"), ch.m * 2)
                tokens(kt, T.gdn_k, ch, NDK, False, S("ns_in_kt"))

            def load_z(ch, m):
                if isinstance(m, int) and m == 1:
                    sp.wait_ge(S("ns_og"), 8)
                wait(sp, S("ns_oT"), m * 2 - 2)
                tokens(og, T.gdn_z, ch, NDV, True, S("ns_in_z"))

            def load_h(t):
                sp.dma_start(h[:, :], T.h1[ds(t * P, P), :]).then_inc(S("ns_in_h"), 16)

            def store_out(t):
                wait(sp, S("ns_final"), t)
                sp.dma_start(out[ds((t - 1) * P, P), :], h[:, :]).then_inc(S("ns_out"), 16)
                wait(sp, S("ns_out"), t * 16)

            def chunk(ch, left):
                if ch.j == 0:
                    load_z(ch, ch.m)
                if left > 1:
                    load_gp(ch.ahead(2))
                if left > 0:
                    load_v(ch.ahead(1))
                if ch.j == 1:
                    load_z(ch, ch.m)
                if left > 1:
                    load_kq(ch.ahead(2))
                if left > 0:
                    load_kt(ch.ahead(1))

            first = Chunk(1, 1)
            load_gp(first)
            load_kq(first)
            load_v(first)
            load_kt(first)
            w_load(sp, 0)
            load_gp(first.ahead(1))
            load_kq(first.ahead(1))
            chunk(first, 2)
            w_load(sp, 1)
            chunk(Chunk(2, 0), 2)
            w_load(sp, 2)
            chunk(Chunk(3, 1), 2)
            sp.wait_ge(S("ns_wlo"), KO)
            sp.dma_start(nw[:, :], bc(out_norm, [P, D])).then_inc(S("ns_nw_in"), 16)
            load_h(1)
            chunk(Chunk(4, 0), 2)
            chunk(Chunk(5, 1), 2)
            with sp.Fori(3, NT - 1) as t:
                store_out(t - 2)
                load_h(t - 1)
                chunk(Chunk(t * 2, 0), 2)
                chunk(Chunk(t * 2 + 1, 1), 2)
            store_out(NT - 3)
            load_h(NT - 2)
            chunk(Chunk(2 * NT - 2, 0), 1)
            chunk(Chunk(2 * NT - 1, 1), 0)
            store_out(NT - 2)
            load_h(NT - 1)
            store_out(NT - 1)

        @block.tensor
        def _(pe):
            def pairs():
                for hp in range(HP):
                    for p in range(2):
                        yield hp, p, R[p]

            def out_stream(t):
                steps = []
                n = 3 * KO
                for half in range(2):
                    for kk in range(KO):
                        hp, d, x = kk // 4, kk // 2 % 2, kk % 2
                        row = (2 * hp + 1 - x) * 2 + d
                        for e, (o, w_) in enumerate(((oT_hi, whi), (oT_hi, wlo), (oT_lo, whi))):
                            def step(i=3 * kk + e, o=o, w_=w_, kk=kk, row=row, half=half):
                                if i == 0:
                                    if half == 0:
                                        wait(pe, S("ns_otlo"), t * 4)
                                    wait(pe, S("ns_yd"), t * 2 - 2 + half)
                                mm = pe.matmul(pY[:, :], o[:, kk, :], w_[:, row, half * 512:half * 512 + 512],
                                               start=(i == 0), stop=(i == n - 1))
                                if i == n - 1:
                                    mm.then_inc(S("ns_y"), 1)
                            steps.append(step)
                return steps

            def outputs(m):
                wait(pe, S("ns_su"), m * 8 + 8)
                wait(pe, S("ns_og"), m * 8 + 8)
                for b in range(2):
                    for a in range(2):
                        for d in range(2):
                            i0 = (a * 2 + d) * 2
                            mm = pe.transpose(pT[b][:, i0:i0 + 2, :], og[:, 2 * b + a, d * P:(d + 1) * P], T.eye)
                    mm.then_inc(S("ns_oT"), 1)

            def scores(ch):
                m = ch.m
                wait(pe, S("ns_in_kq"), m * 64 + 64)
                wait(pe, S("ns_u"), m * (LV + 1))
                for hp, p, r in pairs():
                    kk_, qq_ = (0, 1) if p == 0 else (1, 0)
                    hd = 2 * hp + p
                    pe.matmul(pKK[r, hp, :], kq[:, hd, kk_, :], kq[:, hd, kk_, :], start=True, stop=True)
                    mm = pe.matmul(pQK[r, hp, :], kq[:, hd, kk_, :], kq[:, hd, qq_, :], start=True, stop=True)
                mm.then_inc(S("ns_g"), 1)

            def level_p(ch, l):
                m = ch.m
                waits_apart(pe, T.pe_carrier,
                            (S("ns_u"), m * (LV + 1) + l + 1),
                            (S("ns_low"), m * LV + l + 1),
                            (S("ns_at"), (m + 1) if l == 0 else 0),
                            (S("ns_t"), m * LV + l + 1))
                for hp, p, r in pairs():
                    mm = pe.matmul(pP[r, hp, :], low[l + 1][r, hp, :], U[ch.par][r, hp, :], start=True, stop=True)
                mm.then_inc(S("ns_p"), 1)

            def level_u(ch, l):
                m = ch.m
                waits_apart(pe, T.pe_carrier,
                            (S("ns_pm"), m * LV + l + 1))
                for hp, p, r in pairs():
                    mm = pe.matmul(pUP[r, hp, :], Ti[r, hp, :], Pm[r, hp, :], start=True, stop=True)
                mm.then_inc(S("ns_up"), 1)
                if l < LV - 1:
                    for hp, p, r in pairs():
                        mm = pe.matmul(pPT[r, hp, :], Pm[r, hp, :], Ti[r, hp, :], start=True, stop=True)
                    mm.then_inc(S("ns_pt"), 1)

            def chunk(ch, t, has_prev, left):
                m, j = ch.m, ch.j
                nxt = ch.ahead(1)
                stream = []
                if has_prev:
                    stream = out_stream(t - 1)
                    stream = stream[64:] if j else stream[:64]

                def fill(k):
                    for _ in range(k):
                        if stream:
                            stream.pop(0)()
                wait(pe, S("ns_kqd"), m * 3 + 3)
                wait(pe, S("ns_su"), m * 8)
                wait(pe, S("ns_og"), m * 8)
                for hp, p, r in pairs():
                    hd = 2 * hp + p
                    mm = pe.matmul(pX[p][:, hp, :], kqd[:, hd, :, :].rearrange("p w c -> p (w c)"), St[:, hd, :],
                                   start=(hp % 2 == 0), stop=False, skip_group_check=True)
                mm.then_inc(S("ns_x"), 1)
                if j == 0 and transposed(t, ch, has_prev):
                    outputs(m - 1)
                if j:
                    fill(8)
                if left > 0:
                    scores(nxt)
                waits_apart(pe, T.pe_carrier,
                            (S("ns_r"), m * 2 + 2),
                            (S("ns_u"), m * (LV + 1) + LV + 1))
                for hp, p, r in pairs():
                    mm = pe.matmul(pX[p][r, hp, :], U[ch.par][r, hp, :], v[r, hp, :],
                                   start=(hp % 2 == 0), stop=True, skip_group_check=True)
                mm.then_inc(S("ns_v"), 1)
                fill(8)
                waits_apart(pe, T.pe_carrier,
                            (S("ns_vn0"), m + 1),
                            (S("ns_vn1"), m + 1),
                            (S("ns_at"), m + 1))
                for hp, p, r in pairs():
                    mm = pe.matmul(pX[p][R[1 - p], hp, :], dn[ch.par][r, hp, :], vn[r, hp, :], start=False, stop=True,
                                   skip_group_check=True)
                mm.then_inc(S("ns_o"), 1)
                if j:
                    fill(len(stream))
                    if transposed(t, ch, has_prev):
                        outputs(m - 1)
                else:
                    fill(8)
                for rnd in range(2):
                    if rnd:
                        wait(pe, S("ns_su"), m * 8 + 4)
                    else:
                        waits_apart(pe, T.pe_carrier,
                                    (S("ns_kdec"), m + 1),
                                    (S("ns_otlo"), m * 2 - 2 if transposed(t, ch, has_prev) else 0))
                    for a in range(2):
                        for p in range(2):
                            hp = 2 * rnd + a
                            mm = pe.matmul(pS[p][:, a, :], kdec[R[p], hp, :], vn[R[p], hp, :], start=True, stop=True)
                    mm.then_inc(S("ns_ds"), 1)
                    if rnd == 0 and left > 0:
                        level_p(nxt, 0)
                    if rnd == 0:
                        fill(4)
                if left > 0:
                    level_u(nxt, 0)
                    for l in range(1, LV):
                        k = 4 if l == 3 else 6
                        fill(k)
                        level_p(nxt, l)
                        fill(k)
                        level_u(nxt, l)
                fill(len(stream))

            def tail():
                outputs(2 * NT - 2)
                for step in out_stream(NT - 1):
                    step()
            first = Chunk(1, 1)
            pe.wait_ge(S("ns_init"), 1)
            scores(first)
            for l in range(LV):
                level_p(first, l)
                level_u(first, l)
            over_chunks(pe, chunk, tail)

        @block.scalar
        def _(act):
            def high(m, half):
                for b in range(2):
                    wait(act, S("ns_oT"), (m - 1) * 2 + b + 1)
                    act.activation(oT_hi[:, 8 * b:8 * b + 8, half * C:half * C + C], pT[b], ACT.Copy)\
                       .then_inc(S("ns_othi"), 1)

            def decays(ch):
                m = ch.m
                wait(act, S("ns_in_gb"), m * 16 + 16)
                wait(act, S("ns_su"), (m - 1) * 8)
                act.activation(dec[ch.par][:, :], gb[:, :, 0, C - 1], ACT.Exp).then_inc(S("ns_dec"), 1)
                wait(act, S("ns_dec"), m + 1)
                act.activation(er[:, :, :], gb[:, :, 0, :], ACT.Exp).then_inc(S("ns_er"), 1)
                wait(act, S("ns_kdl"), m + 1)
                act.activation(kdl[:, :], kdl[:, :], ACT.Exp).then_inc(S("ns_ekdl"), 1)
                wait(act, S("ns_dn"), m + 1)
                act.activation(dn[ch.par][:, :, :], dn[ch.par][:, :, :], ACT.Exp).then_inc(S("ns_edn"), 1)
                wait(act, S("ns_dx"), m + 1)
                act.activation(dx[:, :, :], dx[:, :, :], ACT.Exp, scale=-1.0).then_inc(S("ns_edx"), 1)

            def level(ch, l):
                m = ch.m
                wait(act, S("ns_p"), m * LV + l + 1)
                if l:
                    wait(act, S("ns_pt"), m * (LV - 1) + l)
                else:
                    wait(act, S("ns_up"), m * LV)
                act.activation(Pm[:, :, :], pP, ACT.Copy).then_inc(S("ns_pm"), 1)

            def chunk(ch, t, has_prev, left):
                m, j = ch.m, ch.j
                nxt = ch.ahead(1)
                if left > 0:
                    decays(nxt)
                if j == 0 and transposed(t, ch, has_prev):
                    high(m - 1, 1)
                wait(act, S("ns_v"), m + 1)
                wait(act, S("ns_ds"), m * 2)
                act.activation(vn[R[0], :, :], pX[0][R[0], :, :], ACT.Copy).then_inc(S("ns_vn0"), 1)
                wait(act, S("ns_o"), m + 1)
                wait(act, S("ns_rs"), m * 2)
                if left > 0:
                    wait(act, S("ns_u"), (m + 1) * (LV + 1) + 1)
                for n, (hp, p) in enumerate((hp, p) for hp in range(HP) for p in range(2)):
                    r = R[1 - p]
                    act.activation(junk[r, :], pX[p][r, hp, :], ACT.Square, accum_out=ss[r, hp:hp + 1])\
                       .then_inc(S("ns_ss"), 1)
                    wait(act, S("ns_ss"), m * 8 + n + 1)
                if j == 1 and transposed(t, ch, has_prev):
                    if not has_prev:
                        act.wait_ge(S("ns_wlo"), KO)
                    high(m - 1, 0)
                if left > 0:
                    for l in range(LV):
                        level(nxt, l)
                if part_of(t, ch):
                    w_hi(act, part_of(t, ch))
                if j and has_prev:
                    norm2(t - 1)

            def norm2(t):
                wait(act, S("ns_yd"), t * 2)
                wait(act, S("ns_ds"), t * 4 + 6)
                act.activation(vn[:, :, :].rearrange("p a b -> p (a b)"), h[:, :], ACT.Square, accum_out=ss2[:, :])\
                   .then_inc(S("ns_ss2"), 1)

            def tail():
                high(2 * NT - 2, 1)
                wait(act, S("ns_yd"), 2 * NT - 2)
                act.activation(vn[:, :, :].rearrange("p a b -> p (a b)"), h[:, :], ACT.Square, accum_out=ss2[:, :])\
                   .then_inc(S("ns_ss2"), 1)
            first = Chunk(1, 1)
            decays(first)
            for l in range(LV):
                level(first, l)
            w_hi(act, 0)
            over_chunks(act, chunk, tail)

        @block.vector
        def _(dve):
            dve.memset(St[:, :, :], 0.0).then_inc(S("ns_init"), 1)

            def lo(m, half):
                for b in range(2):
                    wait(dve, S("ns_othi"), (m - 1) * 2 + b + 1)
                    dve.tensor_tensor(oT_lo[:, 8 * b:8 * b + 8, half * C:half * C + C], pT[b],
                                      oT_hi[:, 8 * b:8 * b + 8, half * C:half * C + C].bitcast(F32), ALU.subtract)\
                       .then_inc(S("ns_otlo"), 1)

            def residual(t, half):
                wait(dve, S("ns_y"), t * 2 - 1 + half)
                wait(dve, S("ns_in_h"), t * 16)
                c = slice(half * 512, half * 512 + 512)
                dve.tensor_tensor(h[:, c], pY[:, :], h[:, c], ALU.add).then_inc(S("ns_yd"), 1)

            def final(t):
                dve.wait_ge(S("ns_nw_in"), 16)
                wait(dve, S("ns_rs2"), t)
                wait(dve, S("ns_yd"), t * 2)
                dve.scalar_tensor_tensor(h[:, :], h[:, :], ss2[:, 0:1], nw[:, :], ALU.mult, ALU.mult)\
                   .then_inc(S("ns_final"), 1)

            def differences(ch):
                m = ch.m
                wait(dve, S("ns_tg"), m + 1)
                wait(dve, S("ns_vb"), m)
                dve.tensor_reduce(gbc[:, :, :].rearrange("p h w -> p (h w)"), tg, AX.X, ALU.add).then_inc(S("ns_gbc"), 1)
                wait(dve, S("ns_gbc"), m + 1)
                wait(dve, S("ns_in_g"), m * 32 + 32)
                wait(dve, S("ns_dx"), m)
                wait(dve, S("ns_ss"), (m - 1) * 8)
                dve.tensor_tensor(d1[:, :, :], gp[:, :, 0, :], bc(gbc[:, :, 0:1], [P, HP, C]), ALU.subtract)\
                   .then_inc(S("ns_d1"), 1)
                wait(dve, S("ns_kdec"), m)
                dve.tensor_tensor(kdl[:, :], gp[:, :, 0, C - 1], gbc[:, :, 0], ALU.subtract).then_inc(S("ns_kdl"), 1)
                wait(dve, S("ns_d1"), m + 1)
                wait(dve, S("ns_o"), m - 1)
                dve.tensor_scalar(dn[ch.par][:, :, :], d1[:, :, :], 0.0, None, ALU.min).then_inc(S("ns_dn"), 1)
                wait(dve, S("ns_m"), m)
                dve.tensor_scalar(dx[:, :, :], d1[:, :, :], 0.0, None, ALU.max).then_inc(S("ns_dx"), 1)

            def first_inverse(ch):
                m = ch.m
                wait(dve, S("ns_g"), m + 1)
                wait(dve, S("ns_dxb"), m + 1)
                wait(dve, S("ns_low"), m * LV)
                dve.tensor_tensor(M, pKK, dx[:, :, :], ALU.mult).then_inc(S("ns_m"), 1)
                wait(dve, S("ns_mtf"), m * 2 + 2)
                dve.tensor_tensor(d1[:, :, :], pKK, mtf, ALU.mult).then_inc(S("ns_mt"), 1)
                wait(dve, S("ns_mt"), m + 1)
                wait(dve, S("ns_v"), m - 1)
                dve.tensor_tensor(U[ch.par][:, :, :], eye_p([P, HP, C]), d1[:, :, :], ALU.subtract)\
                   .then_inc(S("ns_u"), 1)
                wait(dve, S("ns_dnm"), m + 1)
                dve.tensor_tensor(dn[ch.par][:, :, :], pQK, dn[ch.par][:, :, :], ALU.mult).then_inc(S("ns_at"), 1)

            def level(ch, l):
                m = ch.m
                wait(dve, S("ns_up"), m * LV + l + 1)
                wait(dve, S("ns_u"), m * (LV + 1) + l + 1)
                if l < LV - 1:
                    wait(dve, S("ns_pt"), m * (LV - 1) + l + 1)
                dve.tensor_tensor(U[ch.par][:, :, :], U[ch.par][:, :, :], pUP, ALU.subtract).then_inc(S("ns_u"), 1)
                if l < LV - 1:
                    wait(dve, S("ns_t"), m * LV + l + 1)
                    dve.tensor_tensor(Ti[:, :, :], Ti[:, :, :], pPT, ALU.subtract).then_inc(S("ns_t"), 1)

            def chunk(ch, t, has_prev, left):
                m, j = ch.m, ch.j
                nxt = ch.ahead(1)
                if left > 0:
                    differences(nxt)
                for p in range(2):
                    wait(dve, S("ns_vb"), m + 1)
                    wait(dve, S("ns_x"), m + 1)
                    dve.tensor_tensor(v[R[p], :, :], v[R[p], :, :], pX[p][R[p], :, :], ALU.subtract)\
                       .then_inc(S("ns_r"), 1)
                if j == 0 and transposed(t, ch, has_prev):
                    lo(m - 1, 1)
                wait(dve, S("ns_v"), m + 1)
                wait(dve, S("ns_ds"), m * 2)
                dve.tensor_copy(vn[R[1], :, :], pX[1][R[1], :, :]).then_inc(S("ns_vn1"), 1)
                if left > 0:
                    first_inverse(nxt)
                if j and has_prev:
                    residual(t - 1, 1)
                if j and transposed(t, ch, has_prev):
                    if not has_prev:
                        dve.wait_ge(S("ns_wlo"), KO)
                    lo(m - 1, 0)
                for rnd in range(2):
                    wait(dve, S("ns_ds"), m * 2 + rnd + 1)
                    for a in range(2):
                        for p in range(2):
                            hd = 2 * (2 * rnd + a) + p
                            wait(dve, S("ns_dec"), m + 1)
                            dve.scalar_tensor_tensor(St[:, hd, :], St[:, hd, :], dec[ch.par][:, hd:hd + 1],
                                                     pS[p][:, a, :], ALU.mult, ALU.add).then_inc(S("ns_su"), 1)
                if left > 0:
                    level(nxt, 0)
                wait(dve, S("ns_rs"), m * 2 + 2)
                wait(dve, S("ns_in_z"), m * 32 + 32)
                for hp in range(HP):
                    for p in range(2):
                        r = R[1 - p]
                        dve.scalar_tensor_tensor(og[r, hp, :], pX[p][r, hp, :], ss[r, hp:hp + 1], og[r, hp, :],
                                                 ALU.mult, ALU.mult).then_inc(S("ns_og"), 1)
                    if hp == 1 and left > 0:
                        level(nxt, 1)
                if left > 0:
                    level(nxt, 2)
                if has_prev and j == 0:
                    residual(t - 1, 0)
                if left > 0:
                    level(nxt, 3)
                    level(nxt, 4)
                if has_prev and j:
                    final(t - 1)

            def tail():
                lo(2 * NT - 2, 1)
                residual(NT - 1, 0)
                residual(NT - 1, 1)
                final(NT - 1)
            first = Chunk(1, 1)
            dve.wait_ge(S("ns_init"), 1)
            differences(first)
            first_inverse(first)
            for l in range(LV):
                level(first, l)
            over_chunks(dve, chunk, tail)

        @block.gpsimd
        def _(pool):
            def mult(dst, a, b, sem):
                pool.tensor_tensor(dst, a, b, ALU.mult).then_inc(S(sem), 1)

            def prepare(ch):
                m = ch.m
                dn_ = dn[ch.par]
                wait(pool, S("ns_in_g"), m * 32 + 32)
                wait(pool, S("ns_gbc"), m)
                wait(pool, S("ns_low"), m * LV)
                wait(pool, S("ns_t"), m * LV)
                mult(tg, gp[:, :, :, :].rearrange("p h w c -> p (h w) c"), eye_p([P, 2 * HP, C]), "ns_tg")
                wait(pool, S("ns_gbc"), m + 1)
                wait(pool, S("ns_edn"), m + 1)
                mult(mtf, dn_[:, :, :], gp[:, :, 1, :], "ns_mtf")
                wait(pool, S("ns_mtf"), m * 2 + 1)
                mult(mtf, mtf, mask(K_LOW1T), "ns_mtf")
                wait(pool, S("ns_edx"), m + 1)
                mult(dx[:, :, :], dx[:, :, :], bc(gbc[:, :, 1:2], [P, HP, C]), "ns_dxb")
                mult(dn_[:, :, :], dn_[:, :, :], mask(K_CAUSP), "ns_dnm")
                wait(pool, S("ns_m"), m + 1)
                wait(pool, S("ns_mt"), m + 1)
                wait(pool, S("ns_p"), m * LV)
                mult(low[0], M, mask(K_LOW), "ns_low1")
                mult(low[1], M, mask(K_LOW + C), "ns_low")
                wait(pool, S("ns_low1"), m + 1)
                wait(pool, S("ns_up"), m * LV)
                pool.tensor_tensor(Ti[:, :, :], eye_p([P, HP, C]), low[0], ALU.subtract).then_inc(S("ns_t"), 1)
                for l in range(1, LV):
                    mult(low[l + 1], M, mask(K_LOW + (l + 1) * C), "ns_low")

            def decayed(ch):
                m = ch.m
                wait(pool, S("ns_er"), m + 1)
                wait(pool, S("ns_in_kq"), m * 64 + 64)
                wait(pool, S("ns_x"), m)
                mult(kqd[:, :, :, :], kq[:, :, :, :], bc(gb[:, :, 0:1, :], [P, NH, 2, C]), "ns_kqd")
                wait(pool, S("ns_kqd"), m * 3 + 1)
                for p in range(2):
                    mult(kqd[:, p::2, p, :], kqd[:, p::2, p, :], gb[:, p::2, 1, :], "ns_kqd")

            def weighed(ch):
                m = ch.m
                wait(pool, S("ns_in_v"), m * 32 + 32)
                wait(pool, S("ns_gbc"), m + 1)
                mult(v[:, :, :], v[:, :, :], bc(gbc[:, :, 1:2], [P, HP, NDV]), "ns_vb")
                wait(pool, S("ns_ekdl"), m + 1)
                wait(pool, S("ns_in_kt"), m * 32 + 32)
                mult(kdec[:, :, :], kt[:, :, :], bc(kdl[:, :].rearrange("p (h o) -> p h o", o=1), [P, HP, NDK]),
                     "ns_kdec")

            def chunk(ch, t, has_prev, left):
                m, j = ch.m, ch.j
                nxt = ch.ahead(1)
                if left > 0:
                    prepare(nxt)
                    decayed(nxt)
                waits_apart(pool, T.pool_carrier,
                            (S("ns_ss"), m * 8 + 8),
                            (S("ns_og"), m * 8))
                rsqrt(ss, NDV, m, "ns_rs")
                if left > 0:
                    weighed(nxt)
                if part_of(t, ch):
                    w_lo(pool, part_of(t, ch))
                if j and has_prev:
                    norm2(t - 1)

            def rsqrt(x, width, i, sem):
                pool.tensor_scalar(x[:, :], x[:, :], 1.0 / width, EPS, ALU.mult, ALU.add).then_inc(S(sem), 1)
                wait(pool, S(sem), i * 2 + 1)
                pool.tensor_tensor(x[:, :], x[:, :], bc(T.minus_half[:, 0:1], list(x.shape)), ALU.pow)\
                    .then_inc(S(sem), 1)

            def norm2(t):
                waits_apart(pool, T.pool_carrier,
                            (S("ns_ss2"), t))
                pool.tensor_scalar(ss2[:, :], ss2[:, :], 1.0 / D, EPS, ALU.mult, ALU.add).then_inc(S("ns_mean2"), 1)
                wait(pool, S("ns_mean2"), t)
                pool.tensor_tensor(ss2[:, :], ss2[:, :], T.minus_half[:, 0:1], ALU.pow).then_inc(S("ns_rs2"), 1)

            def tail():
                norm2(NT - 1)
            first = Chunk(1, 1)
            prepare(first)
            decayed(first)
            weighed(first)
            w_lo(pool, 0)
            over_chunks(pool, chunk, tail)


class Tensors:
    pass


def build(nc, a, out):
    T = Tensors()
    with ExitStack() as ctx:
        S = Sems(nc)

        def sb(name, shape, dt=F32, where=ctx):
            return where.enter_context(nc.sbuf_tensor(name, shape, dt))

        def dram(name, shape):
            return nc.dram_tensor(name, shape, F32).ap()
        T.k_dram, T.starts_dram = a["k"], a["starts"]
        T.gla_qk = dram("gla_qk", [GH, 2, P, TP])
        T.gla_ko = dram("gla_ko", [TP, GQK])
        T.gla_v = dram("gla_v", [TP, GV])
        T.gla_z = dram("gla_z", [TP, GV])
        T.h1 = dram("h1", [TP, D])
        T.gdn_qk = dram("gdn_qk", [2, NH, P, TP])
        T.gdn_k = dram("gdn_k", [TP, NQK])
        T.gdn_v = dram("gdn_v", [TP, NV])
        T.gdn_z = dram("gdn_z", [TP, NV])
        T.gb = dram("gdn_gb", [2 * NT, NH, 2, C])
        T.k = sb("consts", [P, K_END])
        T.eye = T.k[:, K_EYE:K_EYE + P]
        T.causal = T.k[:, K_CAUSAL:K_CAUSAL + P].rearrange("p (o c) -> p o c", o=1)
        T.minus_half = sb("minus_half", [P, 1])
        zero_w = sb("zero_weights", [P, 32], mybir.dt.bfloat16)
        spare = [sb(f"carrier{n}", [P, 2]) for n in range(2)]
        with nc.Block() as block:
            @block.vector
            def _(dve):
                dve.memset(zero_w[:, :], 0.0)
                for x in spare:
                    dve.memset(x[:, :], 0.0)
        T.pe_carrier = lambda: nc.tensor.ldweights(zero_w[:, :], tile_position=(0, 0))
        T.dve_carrier = lambda: nc.vector.tensor_copy(spare[0][:, 0:1], spare[0][:, 1:2])
        T.pool_carrier = lambda: nc.gpsimd.tensor_tensor(spare[1][:, 0:1], spare[1][:, 1:2], spare[1][:, 1:2], ALU.add)
        T.cw = sb("conv_taps", [P, CONV, (2 * NQK + NV) // P])
        T.hnw = sb("gla_hn", [P, GV // P])
        T.hnw2 = sb("gdn_hn", [P, NV // P])
        with ExitStack() as hctx:
            T.hn_hi = sb("hn_hi", [P, KT, TP], F32R, hctx)
            T.hn_lo = sb("hn_lo", [P, KT, TP], F32R, hctx)
            with ExitStack() as zctx:
                T.zeros = sb("zeros", [P, NV], F32, zctx)

                def pads():
                    found = [(d[0:PAD, :], T.zeros[0:PAD, 0:d.shape[1]])
                             for d in (T.gla_ko, T.gla_v, T.gla_z, T.gdn_k, T.gdn_v, T.gdn_z)]
                    found += [(T.gla_qk[g, :, :, 0:PAD].rearrange("w p n -> p w n"),
                               T.zeros[:, 0:2 * PAD].rearrange("p (w n) -> p w n", w=2)) for g in range(GH)]
                    found += [(T.gdn_qk[w, :, :, 0:PAD].rearrange("h p n -> p h n"),
                               T.zeros[:, 0:NH * PAD].rearrange("p (h n) -> p h n", h=NH)) for w in range(2)]
                    found += [(T.gb[c].rearrange("h w c -> h (w c)"), T.zeros[0:NH, 0:2 * C]) for c in range(2)]
                    return found
                T.pads = pads
                embed(nc, S, T, a["x"], a["meta"], a["gla_norm"])
            with ExitStack() as gctx:
                T.dec = sb("gla_dec", [P, GH, 2 * NT], F32, gctx)
                with ExitStack() as ectx:
                    T.Eb = sb("gla_eb", [P, GH, L], F32, ectx)
                    T.Enb = sb("gla_enb", [P, GH, L], F32, ectx)
                    T.Eout = sb("gla_eout", [P, GH, L], F32, ectx)
                    gla_gate(nc, S, T, a["gla_w_in"], a["gla_w_gk"], a["gla_b_gk"], a["gla_head_norm"])
                    gla_qk(nc, S, T, a["gla_w_in"])
                project_vz(nc, S, T, "av", a["gla_w_in"], 2 * GQK, 2 * GQK + GV, GV // P, T.gla_v, T.gla_z, T.hnw)
                gla_scan(nc, S, T, a["gla_w_out"], a["x"], a["meta"], a["gdn_norm"])
                S.give_back()
            gdn_gate(nc, S, T, a["gdn_w_in"], a["gdn_a_log"], a["gdn_dt_bias"], a["gdn_conv_w"], a["gdn_head_norm"])
            gdn_qk(nc, S, T, a["gdn_w_in"])
            project_vz(nc, S, T, "nv", a["gdn_w_in"], 2 * NQK, 2 * NQK + NV, NV // P, T.gdn_v, T.gdn_z, T.hnw2,
                       conv=2 * NQK // P)
        gdn_scan(nc, S, T, a["gdn_w_out"], a["final_norm"], out)


def kernel(x, meta_tokens, gla_norm, gla_w_in, gla_w_gk, gla_b_gk, gla_head_norm, gla_w_out, gdn_norm, gdn_w_in,
           gdn_conv_w, gdn_a_log, gdn_dt_bias, gdn_head_norm, gdn_w_out, final_norm):
    import concourse.bacc as bacc
    from concourse.bass_utils import run_bass_kernel_spmd

    def by_channel(w, width):
        return np.tile(w.reshape(-1, P).T, (1, width // w.size))

    arrays = {
        "x": x[0], "meta": meta_tokens, "gla_norm": gla_norm, "gla_w_in": gla_w_in[0], "gla_w_gk": gla_w_gk[0],
        "gla_b_gk": gla_b_gk[0].reshape(GH, P).T, "gla_head_norm": by_channel(gla_head_norm[0], GV), "gla_w_out": gla_w_out[0], "gdn_norm": gdn_norm,
        "gdn_w_in": gdn_w_in[0], "gdn_conv_w": gdn_conv_w[0], "gdn_a_log": gdn_a_log[0],
        "gdn_dt_bias": gdn_dt_bias[0], "gdn_head_norm": by_channel(gdn_head_norm[0], NV), "gdn_w_out": gdn_w_out[0],
        "final_norm": final_norm.reshape(1, D), "k": constants(), "starts": chunk_starts(),
    }
    arrays = {name: np.ascontiguousarray(v) for name, v in arrays.items()}
    nc = bacc.Bacc("TRN2", target_bir_lowering=False, num_devices=1)
    a = {name: nc.dram_tensor("in_" + name, v.shape, mybir.dt.from_np(v.dtype), kind="ExternalInput").ap()
         for name, v in arrays.items()}
    out = nc.dram_tensor("out", [SEQ, D], F32, kind="ExternalOutput").ap()
    build(nc, a, out)
    r = run_bass_kernel_spmd(nc, [{"in_" + name: v for name, v in arrays.items()}], core_ids=[0])
    return r.results[0]["out"].reshape(1, SEQ, D)
```

```python
from contextlib import ExitStack

import numpy as np
import concourse.bass as bass
from concourse import mybir
from concourse.alu_op_type import AluOpType as ALU

F32 = mybir.dt.float32
F32R = mybir.dt.float32r
I32 = mybir.dt.int32
ACT = mybir.ActivationFunctionType
AX = mybir.AxisListType

P = 128
D = 1024
KT = D // P
SEQ = 1024
NMETA = 16
C = 64
PAD = P - NMETA
TP = P + SEQ
NT = TP // P
L = NMETA + SEQ
EPS = 1e-6
SPANS = [(0, 352), (352, 344), (696, 344)]
GH, GDK, GDV = 4, 128, 256
GRANK = 16
GQK, GV = GH * GDK, GH * GDV
NH, NDK, NDV = 8, 128, 256
NQK, NV = NH * NDK, NH * NDV
HP = NH // 2
CONV = 4
LEVELS = [2, 4, 8, 16, 32]

K_EYE, K_CAUSAL, K_EYEP, K_CAUSP, K_LOW1T, K_LOW = 0, 128, 256, 320, 384, 448
K_END = K_LOW + (1 + len(LEVELS)) * C


def constants():
    k = np.zeros((P, K_END), np.float32)
    j, i = np.meshgrid(np.arange(P), np.arange(P), indexing="ij")
    k[:, K_EYE:K_EYE + P] = j == i
    k[:, K_CAUSAL:K_CAUSAL + P] = (j // C == i // C) & (j <= i)
    r, c = np.meshgrid(np.arange(P) % C, np.arange(C), indexing="ij")
    k[:, K_EYEP:K_EYEP + C] = r == c
    k[:, K_CAUSP:K_CAUSP + C] = r <= c

    def below(a, b, size):
        return (a // size % 2 == 1) & (a // size - b // size == 1)
    k[:, K_LOW1T:K_LOW1T + C] = below(c, r, 1)
    for n, size in enumerate([1] + LEVELS):
        k[:, K_LOW + n * C:K_LOW + (n + 1) * C] = below(r, c, size)
    return k


def chunk_starts():
    m = np.ones((P, L), np.float32)
    m[:, 0] = 0
    m[:, NMETA::C] = 0
    return m


class Sems:

    def __init__(self, nc):
        self.nc, self.made = nc, {}

    def __call__(self, name):
        if name not in self.made:
            self.made[name] = self.nc.alloc_semaphore(name=name)
        return self.made[name]

    def give_back(self):
        self.nc.all_engine_barrier()
        self.nc.clear_and_free_semaphores(list(self.made.values()))
        self.nc.all_engine_barrier()
        self.made = {}


def wait(eng, sem, value):
    if isinstance(value, int) and value <= 0:
        return
    eng.wait_ge(sem, value)


def waits_apart(eng, carrier, *waits):
    for s, v in waits:
        wait(eng, s, v)
    carrier()


def ds(i, n=1):
    return bass.ds(i, n)


def bc(ap, shape):
    return ap.broadcast_to(shape)


def embed(nc, S, T, x, meta, norm_w):
    NB = 4
    with ExitStack() as ctx:
        def sb(name, shape, dt=F32):
            return ctx.enter_context(nc.sbuf_tensor(name, shape, dt))
        X = [sb(f"em_x{j}", [P, D]) for j in range(NB)]
        hn = [sb(f"em_hn{j}", [P, D]) for j in range(2)]
        junk = sb("em_junk", [P, D])
        ss = [sb(f"em_ss{j}", [P, 1]) for j in range(NB)]
        rs = [sb(f"em_rs{j}", [P, 1]) for j in range(NB)]
        nw = sb("em_nw", [P, D])
        tr = [ctx.enter_context(nc.psum_tensor(f"em_tr{j}{b}", [P, 4, P], F32)) for j in range(2) for b in range(2)]
        block = ctx.enter_context(nc.Block())
        x_in = [S(f"em_x_in{j}") for j in range(NB)]

        def over_tiles(eng, ahead, after):
            ahead(0, 0, 0)
            with eng.Fori(0, (NT - 1) // NB) as i:
                for r in range(NB):
                    j = (r + 1) % NB
                    ahead(i * NB + r + 1, j, i if j else i + 1)
                    after(i * NB + r, r, i)
            after(NT - 1, (NT - 1) % NB, (NT - 1) // NB)

        def nothing(t, j, n):
            pass

        @block.sync
        def _(sp):
            wait(sp, S("em_x_zero"), 1)
            sp.dma_start(X[0][PAD:P, :], meta).then_inc(x_in[0], 16)
            sp.dma_start(nw[:, :], bc(norm_w, [P, D])).then_inc(S("em_nw_in"), 16)
            for t in range(1, NT):
                if t == 2:
                    sp.dma_start(T.k[:, :], T.k_dram).then_inc(S("k_in"), 16)
                wait(sp, S("em_hn_done"), t - NB + 1)
                sp.dma_start(X[t % NB][:, :], x[(t - 1) * P:t * P, :]).then_inc(x_in[t % NB], 16)
            sp.wait_ge(S("em_zero"), 1)
            for dst, src in T.pads():
                sp.dma_start(dst, src).then_inc(S("pads_out"), 16)
            wait(sp, S("pads_out"), 16 * len(T.pads()))

        @block.scalar
        def _(act):
            def squares(t, j, n):
                wait(act, x_in[j], n * 16 + 16)
                wait(act, S("em_ss"), t)
                act.activation(junk[:, :], X[j][:, :], ACT.Square, accum_out=ss[j][:, :]).then_inc(S("em_ss"), 1)

            def high(t, j, n):
                for b in range(2):
                    wait(act, S("em_tr"), t * 2 + b + 1)
                    act.activation(T.hn_hi[:, 4 * b:4 * b + 4, ds(t * P, P)], tr[2 * (j % 2) + b][:, :, :],
                                   ACT.Copy).then_inc(S("em_hi"), 1)
            over_tiles(act, squares, high)

        @block.gpsimd
        def _(pool):
            pool.memset(T.zeros[:, :], 0.0).then_inc(S("em_zero"), 1)
            pool.memset(T.minus_half[:, :], -0.5).then_inc(S("em_half"), 1)
            pool.wait_ge(S("em_half"), 1)

            def rsqrt(t, j, n):
                waits_apart(pool, T.pool_carrier,
                            (S("em_ss"), t + 1))
                pool.tensor_scalar(rs[j][:, :], ss[j][:, :], 1.0 / D, EPS, ALU.mult, ALU.add).then_inc(S("em_mean"), 1)
                wait(pool, S("em_mean"), t + 1)
                pool.tensor_tensor(rs[j][:, :], rs[j][:, :], T.minus_half[:, 0:1], ALU.pow).then_inc(S("em_rs"), 1)
            over_tiles(pool, rsqrt, nothing)

        @block.vector
        def _(dve):
            dve.memset(X[0][:, :], 0.0).then_inc(S("em_x_zero"), 1)
            dve.wait_ge(S("em_nw_in"), 16)

            def scale(t, j, n):
                wait(dve, S("em_rs"), t + 1)
                wait(dve, x_in[j], n * 16 + 16)
                wait(dve, S("em_tr"), t * 2 - 2)
                dve.scalar_tensor_tensor(hn[j % 2][:, :], X[j][:, :], rs[j][:, 0:1], nw[:, :],
                                         ALU.mult, ALU.mult).then_inc(S("em_hn_done"), 1)

            def low(t, j, n):
                for b in range(2):
                    wait(dve, S("em_hi"), t * 2 + b + 1)
                    dve.tensor_tensor(T.hn_lo[:, 4 * b:4 * b + 4, ds(t * P, P)], tr[2 * (j % 2) + b][:, :, :],
                                      T.hn_hi[:, 4 * b:4 * b + 4, ds(t * P, P)].bitcast(F32),
                                      ALU.subtract).then_inc(S("em_lo"), 1)
            over_tiles(dve, scale, low)

        @block.tensor
        def _(pe):
            pe.wait_ge(S("k_in"), 16)

            def transposes(t, j, n):
                wait(pe, S("em_hn_done"), t + 1)
                for b in range(2):
                    for c in range(4):
                        kt = 4 * b + c
                        mm = pe.transpose(tr[2 * (j % 2) + b][:, c, :], hn[j % 2][:, kt * P:(kt + 1) * P], T.eye)
                    mm.then_inc(S("em_tr"), 1)
            over_tiles(pe, nothing, transposes)


def project(pe, acc, w_hi, w_lo, T):
    for kt in range(KT):
        for n, (w, h) in enumerate(((w_hi, T.hn_hi), (w_hi, T.hn_lo), (w_lo, T.hn_hi))):
            for b, (s, m) in enumerate(SPANS):
                mm = pe.matmul(acc[:, b, 0:m], w[:, kt, :], h[:, kt, PAD + s:PAD + s + m],
                               start=(kt == 0 and n == 0), stop=(kt == KT - 1 and n == 2))
    return mm


class Proj:

    def __init__(self, nc, S, T, ctx, tag, w, col):
        self.S, self.T, self.tag, self.col = S, T, tag, col
        self.w = w.rearrange("(k p) n -> p k n", p=P)
        self.st = [ctx.enter_context(nc.sbuf_tensor(f"{tag}_w{j}", [P, KT, P], F32)) for j in range(2)]
        self.hi = [ctx.enter_context(nc.sbuf_tensor(f"{tag}_whi{j}", [P, KT, P], F32R)) for j in range(2)]
        self.lo = [ctx.enter_context(nc.sbuf_tensor(f"{tag}_wlo{j}", [P, KT, P], F32R)) for j in range(2)]
        self.acc = [ctx.enter_context(nc.psum_tensor(f"{tag}_acc{j}", [P, 3, 512], F32)) for j in range(2)]
        self.trA = ctx.enter_context(nc.psum_tensor(f"{tag}_trA", [P, 4, P], F32))
        self.trB = ctx.enter_context(nc.psum_tensor(f"{tag}_trB", [P, 4, P], F32))

    def sem(self, name):
        return self.S(f"{self.tag}_{name}")

    def load(self, sp, i, j):
        wait(sp, self.sem(f"whi{j}"), i)
        wait(sp, self.sem(f"wlo{j}"), i)
        sp.dma_start(self.st[j][:, :, :], self.w[:, :, ds(self.col(i, j), P)]).then_inc(self.sem(f"w_in{j}"), 16)

    def split_hi(self, act, i, j):
        wait(act, self.sem(f"w_in{j}"), i * 16 + 16)
        wait(act, self.sem(f"mm{j}"), i)
        act.activation(self.hi[j][:, :, :], self.st[j][:, :, :], ACT.Copy).then_inc(self.sem(f"whi{j}"), 1)

    def split_lo(self, pool, i, j):
        wait(pool, self.sem(f"whi{j}"), i + 1)
        wait(pool, self.sem(f"mm{j}"), i)
        wait(pool, self.sem(f"w_in{j}"), i * 16 + 16)
        pool.tensor_tensor(self.lo[j][:, :, :], self.st[j][:, :, :], self.hi[j][:, :, :].bitcast(F32),
                           ALU.subtract).then_inc(self.sem(f"wlo{j}"), 1)

    def mm(self, pe, i, j, free):
        wait(pe, self.sem(f"whi{j}"), i + 1)
        wait(pe, self.sem(f"wlo{j}"), i + 1)
        wait(pe, self.sem(f"free{j}"), i * free)
        project(pe, self.acc[j], self.hi[j], self.lo[j], self.T).then_inc(self.sem(f"mm{j}"), 1)

    def banks(self):
        return ((0, self.trA), (1, self.trB))


def transpose_out(pe, q, src, b, eye, done):
    if b < 2:
        bank = (q.trA, q.trB)[b]
        for c in range(4):
            s = NMETA + (4 * b + c) * P
            mm = pe.transpose(bank[:, c, :], src[:, s:s + P], eye)
    else:
        mm = pe.transpose(q.trA[0:NMETA, 0, :], src[:, 0:NMETA], eye)
    mm.then_inc(done, 1)


def evacuate_out(eng, copy, q, dst, b, done):
    if b < 2:
        copy(dst[:, 1 + 4 * b:5 + 4 * b, :], (q.trA, q.trB)[b][:, :, :]).then_inc(done, 1)
    else:
        copy(dst[0:NMETA, 0, :], q.trA[0:NMETA, 0, :]).then_inc(done, 1)


def store_tokens(sp, dst, tok, col, width, done):
    sp.dma_start(dst[PAD:P, ds(col, P)], tok[0:NMETA, 0, :]).then_inc(done, 16)
    sp.dma_start(dst[P:TP, ds(col, P)].rearrange("(t p) c -> p t c", p=P), tok[:, 1:NT, :]).then_inc(done, 16)


class GlaGate:

    def __init__(self, nc, S, T, ctx, acc, w_in, w_gk, b_gk, head_norm):
        def sb(name, shape, dt=F32):
            return ctx.enter_context(nc.sbuf_tensor(name, shape, dt))
        self.S, self.T, self.acc = S, T, acc
        self.w_in, self.w_gk, self.b_gk, self.head_norm = w_in, w_gk, b_gk, head_norm
        self.st = sb("gg_w", [P, KT, P])
        self.w_hi = sb("gg_whi", [P, KT, P], F32R)
        self.w_lo = sb("gg_wlo", [P, KT, P], F32R)
        self.gl = sb("gg_low", [GRANK, L])
        self.wg = sb("gg_wgk", [GRANK, GQK])
        self.bg = sb("gg_b", [P, GH])
        self.cm = sb("gg_starts", [P, L])
        self.ax = [T.Eout[:, h, :] for h in range(GH)]
        self.mn = [T.Enb[:, h, :] for h in range(GH)]
        self.bt = [T.Eb[:, h, :] for h in range(GH)]

    def load(self, sp):
        S = self.S
        c0 = 2 * GQK + 2 * GV
        sp.wait_ge(S("gg_zero"), 1)
        sp.dma_start(self.st[:, :, 0:GRANK], self.w_in.rearrange("(k p) n -> p k n", p=P)[:, :, c0:c0 + GRANK])\
          .then_inc(S("gg_w_in"), 16)
        sp.dma_start(self.wg[:, :], self.w_gk).then_inc(S("gg_small_in"), 16)
        sp.dma_start(self.bg[:, :], self.b_gk).then_inc(S("gg_small_in"), 16)
        sp.dma_start(self.cm[:, :], self.T.starts_dram).then_inc(S("gg_small_in"), 16)
        sp.dma_start(self.T.hnw[:, :], self.head_norm).then_inc(S("gg_hnw_in"), 16)

    def split_hi(self, act):
        act.wait_ge(self.S("gg_w_in"), 16)
        act.activation(self.w_hi[:, :, :], self.st[:, :, :], ACT.Copy).then_inc(self.S("gg_whi"), 1)

    def split_lo(self, pool):
        S = self.S
        pool.memset(self.st[:, :, :], 0.0).then_inc(S("gg_zero"), 1)
        pool.memset(self.T.dec[:, :, 0:1], 1.0).then_inc(S("gg_dec0"), 1)
        pool.wait_ge(S("gg_whi"), 1)
        pool.tensor_tensor(self.w_lo[:, :, :], self.st[:, :, :], self.w_hi[:, :, :].bitcast(F32), ALU.subtract)\
            .then_inc(S("gg_wlo"), 1)

    def products(self, pe):
        S = self.S
        pe.wait_ge(S("gg_wlo"), 1)
        project(pe, self.acc[0], self.w_hi, self.w_lo, self.T).then_inc(S("gg_low"), 1)
        pe.wait_ge(S("gg_low_out"), 3)
        pe.wait_ge(S("gg_small_in"), 48)
        for h in range(GH):
            if h >= 2:
                pe.wait_ge(S("gg_min"), 3 * (h - 1))
            for b, (s, m) in enumerate(SPANS):
                mm = pe.matmul(self.acc[h % 2][:, b, 0:m], self.wg[:, h * P:(h + 1) * P], self.gl[:, s:s + m],
                               start=True, stop=True)
            mm.then_inc(S("gg_logit"), 1)

    def free(self, pe, j):
        pe.wait_ge(self.S("gg_min"), 3 * (GH - 1 + j))

    def exponentials(self, act):
        S, T = self.S, self.T
        act.wait_ge(S("gg_low"), 1)
        for b, (s, m) in enumerate(SPANS):
            act.activation(self.gl[:, s:s + m], self.acc[0][0:GRANK, b, 0:m], ACT.Copy).then_inc(S("gg_low_out"), 1)
        for h in range(GH):
            act.wait_ge(S("gg_abs"), h + 1)
            act.activation(self.ax[h], self.ax[h], ACT.Exp, scale=-1.0).then_inc(S("gg_e"), 1)
        for h in range(GH):
            act.wait_ge(S("gg_e"), h + 1)
            act.activation(self.ax[h], self.ax[h], ACT.Ln, bias=1.0).then_inc(S("gg_ln"), 1)
        for h in range(GH):
            bt = self.bt[h]
            act.wait_ge(S("gg_cum"), h + 1)
            act.activation(self.mn[h], bt, ACT.Exp, scale=-1.0 / 16).then_inc(S("gg_exps"), 1)
            act.activation(T.dec[:, h, 2:], bt[:, NMETA + C - 1::C], ACT.Exp, scale=1.0 / 16)\
               .then_inc(S("gg_exps"), 1)
            act.activation(T.dec[:, h, 1:2], bt[:, NMETA - 1:NMETA], ACT.Exp, scale=1.0 / 16)\
               .then_inc(S("gg_exps"), 1)
            act.wait_ge(S("gg_left"), 2 * (h + 1))
            act.activation(self.ax[h], self.ax[h], ACT.Exp, scale=1.0 / 16).then_inc(S("gg_exps"), 1)
            act.wait_ge(S("gg_exps"), 5 * h + 3)
            act.activation(bt, bt, ACT.Exp, scale=1.0 / 16).then_inc(S("gg_exps"), 1)

    def logs(self, dve):
        S = self.S
        for h in range(GH):
            dve.wait_ge(S("gg_logit"), h + 1)
            acc, bias = self.acc[h % 2], self.bg[:, h:h + 1]
            for b, (s, m) in enumerate(SPANS):
                dve.tensor_scalar(self.ax[h][:, s:s + m], acc[:, b, 0:m], bias, 0.0, ALU.add, ALU.max)\
                   .then_inc(S("gg_max"), 1)
            for b, (s, m) in enumerate(SPANS):
                dve.tensor_scalar(self.mn[h][:, s:s + m], acc[:, b, 0:m], bias, 0.0, ALU.add, ALU.min)\
                   .then_inc(S("gg_min"), 1)
            dve.wait_ge(S("gg_max"), 3 * (h + 1))
            dve.wait_ge(S("gg_min"), 3 * (h + 1))
            dve.tensor_tensor(self.ax[h], self.ax[h], self.mn[h], ALU.subtract).then_inc(S("gg_abs"), 1)
        for h in range(GH):
            ax, mn, bt = self.ax[h], self.mn[h], self.bt[h]
            dve.wait_ge(S("gg_ln"), h + 1)
            dve.wait_ge(S("gg_min"), 3 * (h + 1))
            dve.tensor_tensor(mn, mn, ax, ALU.subtract).then_inc(S("gg_log"), 1)
            dve.wait_ge(S("gg_log"), h + 1)
            dve.tensor_tensor_scan(bt, self.cm[:, :], mn, 0.0, ALU.mult, ALU.add).then_inc(S("gg_cum"), 1)
            dve.wait_ge(S("gg_cum"), h + 1)
            dve.tensor_tensor(ax[:, 0:NMETA], bc(bt[:, NMETA - 1:NMETA], [P, NMETA]), bt[:, 0:NMETA],
                              ALU.subtract).then_inc(S("gg_left"), 1)
            real = bt[:, NMETA:].rearrange("p (c t) -> p c t", t=C)
            dve.tensor_tensor(ax[:, NMETA:].rearrange("p (c t) -> p c t", t=C),
                              bc(real[:, :, C - 1:C], [P, SEQ // C, C]), real, ALU.subtract)\
               .then_inc(S("gg_left"), 1)


def gla_qk(nc, S, T, w_in):
    n = GH
    with ExitStack() as ctx:
        q = Proj(nc, S, T, ctx, "aq", w_in, lambda i, j: j * GQK + i * P)
        qT = ctx.enter_context(nc.sbuf_tensor("aq_q", [P, L], F32))
        kT = ctx.enter_context(nc.sbuf_tensor("aq_k", [P, L], F32))
        oT = ctx.enter_context(nc.sbuf_tensor("aq_kout", [P, L], F32))
        tok = ctx.enter_context(nc.sbuf_tensor("aq_tok", [P, NT, P], F32))
        block = ctx.enter_context(nc.Block())

        @block.sync
        def _(sp):
            def store(i):
                wait(sp, q.sem("free0"), i * 3 + 3)
                sp.dma_start(T.gla_qk[ds(i), 0, :, PAD:TP].rearrange("a p n -> p (a n)"), qT[:, :])\
                  .then_inc(q.sem("q_out"), 16)
                wait(sp, q.sem("free1"), i * 6 + 6)
                sp.dma_start(T.gla_qk[ds(i), 1, :, PAD:TP].rearrange("a p n -> p (a n)"), kT[:, :])\
                  .then_inc(q.sem("k_out"), 16)
                wait(sp, q.sem("ev"), i * 3 + 3)
                store_tokens(sp, T.gla_ko, tok, i * P, GQK, q.sem("tok_out"))
            for j in range(2):
                q.load(sp, 0, j)
            for j in range(2):
                q.load(sp, 1, j)
            with sp.Fori(0, n - 2) as i:
                for j in range(2):
                    q.load(sp, i + 2, j)
                store(i)
            store(n - 2)
            store(n - 1)
            sp.wait_ge(q.sem("q_out"), 16 * n)
            sp.wait_ge(q.sem("k_out"), 16 * n)
            sp.wait_ge(q.sem("tok_out"), 32 * n)

        @block.scalar
        def _(act):
            for j in range(2):
                q.split_hi(act, 0, j)
            with act.Fori(1, n) as i:
                for j in range(2):
                    q.split_hi(act, i, j)

        @block.gpsimd
        def _(pool):
            for j in range(2):
                q.split_lo(pool, 0, j)
            with pool.Fori(1, n) as i:
                for j in range(2):
                    q.split_lo(pool, i, j)

        @block.tensor
        def _(pe):
            def tr(i):
                wait(pe, q.sem("free1"), i * 6 + 6)
                for b in range(3):
                    wait(pe, q.sem("ev"), i * 3 if b == 0 else i * 3 + b - 1)
                    transpose_out(pe, q, oT, b, T.eye, q.sem("tr"))
            q.mm(pe, 0, 0, 3)
            q.mm(pe, 0, 1, 6)
            with pe.Fori(1, n) as i:
                q.mm(pe, i, 0, 3)
                tr(i - 1)
                q.mm(pe, i, 1, 6)
            tr(n - 1)

        @block.vector
        def _(dve):
            def ev(i):
                wait(dve, q.sem("tok_out"), i * 32)
                for b in range(3):
                    wait(dve, q.sem("tr"), i * 3 + b + 1)
                    evacuate_out(dve, dve.tensor_copy, q, tok, b, q.sem("ev"))

            def epi_q(i):
                wait(dve, q.sem("mm0"), i + 1)
                wait(dve, q.sem("q_out"), i * 16)
                for b, (s, m) in enumerate(SPANS):
                    dve.scalar_tensor_tensor(qT[:, s:s + m], q.acc[0][:, b, 0:m], float(GDK) ** -0.5,
                                             T.Eb[:, ds(i), s:s + m].rearrange("p a n -> p (a n)"),
                                             ALU.mult, ALU.mult).then_inc(q.sem("free0"), 1)

            def epi_k(i):
                wait(dve, q.sem("mm1"), i + 1)
                wait(dve, q.sem("k_out"), i * 16)
                wait(dve, q.sem("tr"), i * 3)
                for dst, gate in ((kT, T.Enb), (oT, T.Eout)):
                    for b, (s, m) in enumerate(SPANS):
                        dve.tensor_tensor(dst[:, s:s + m], q.acc[1][:, b, 0:m],
                                          gate[:, ds(i), s:s + m].rearrange("p a n -> p (a n)"), ALU.mult)\
                           .then_inc(q.sem("free1"), 1)
            epi_q(0)
            epi_k(0)
            with dve.Fori(1, n) as i:
                epi_q(i)
                ev(i - 1)
                epi_k(i)
            ev(n - 1)


def project_vz(nc, S, T, tag, w_in, col_v, col_z, n, v_out, z_out, hnw, conv=None, gate_of=None):
    with ExitStack() as ctx:
        q = Proj(nc, S, T, ctx, tag, w_in, lambda i, j: (col_v, col_z)[j] + i * P)
        xT = [ctx.enter_context(nc.sbuf_tensor(f"{tag}_x{j}", [P, L], F32)) for j in range(2)]
        tok = [ctx.enter_context(nc.sbuf_tensor(f"{tag}_tok{j}", [P, NT, P], F32)) for j in range(2)]
        if conv is not None:
            xs = ctx.enter_context(nc.sbuf_tensor(f"{tag}_xs", [P, CONV - 1 + L], F32))
            cv = ctx.enter_context(nc.sbuf_tensor(f"{tag}_cv", [P, L], F32))
        gate = gate_of(ctx, q.acc) if gate_of else None
        block = ctx.enter_context(nc.Block())

        @block.sync
        def _(sp):
            if gate:
                gate.load(sp)

            def store(i, j):
                wait(sp, q.sem(f"ev{j}"), i * 3 + 3)
                store_tokens(sp, (v_out, z_out)[j], tok[j], i * P, n * P, q.sem(f"tok_out{j}"))
            for j in range(2):
                q.load(sp, 0, j)
            for j in range(2):
                q.load(sp, 1, j)
            with sp.Fori(0, n - 2) as i:
                for j in range(2):
                    q.load(sp, i + 2, j)
                for j in range(2):
                    store(i, j)
            for i in range(n - 2, n):
                for j in range(2):
                    store(i, j)
            for j in range(2):
                sp.wait_ge(q.sem(f"tok_out{j}"), 32 * n)

        @block.scalar
        def _(act):
            def epi_v(i, before=None):
                wait(act, q.sem("mm0"), i + 1)
                dst, at = (xT[0], 0) if conv is None else (xs, CONV - 1)
                if conv is None:
                    wait(act, q.sem("tr0"), i * 3)
                else:
                    wait(act, q.sem("conv"), i * CONV)
                for b, (s, m) in enumerate(SPANS):
                    act.activation(dst[:, at + s:at + s + m], q.acc[0][:, b, 0:m], ACT.Copy)\
                       .then_inc(q.sem("free0"), 1)

            def silu_v(i):
                if conv is not None:
                    wait(act, q.sem("conv"), i * CONV + CONV)
                    wait(act, q.sem("tr0"), i * 3)
                    act.activation(xT[0][:, :], cv[:, :], ACT.Silu).then_inc(q.sem("v"), 1)

            def epi_z(i):
                wait(act, q.sem("mm1"), i + 1)
                wait(act, q.sem("tr1"), i * 3)
                for b, (s, m) in enumerate(SPANS):
                    act.activation(xT[1][:, s:s + m], q.acc[1][:, b, 0:m], ACT.Silu).then_inc(q.sem("free1"), 1)
            if gate:
                gate.split_hi(act)
            for j in range(2):
                q.split_hi(act, 0, j)
            if gate:
                gate.exponentials(act)
            with act.Fori(0, n - 1) as i:
                epi_v(i)
                q.split_hi(act, i + 1, 0)
                silu_v(i)
                epi_z(i)
                q.split_hi(act, i + 1, 1)
            epi_v(n - 1)
            silu_v(n - 1)
            epi_z(n - 1)

        @block.gpsimd
        def _(pool):
            if gate:
                gate.split_lo(pool)
            for j in range(2):
                q.split_lo(pool, 0, j)
            with pool.Fori(1, n) as i:
                for j in range(2):
                    q.split_lo(pool, i, j)

        @block.tensor
        def _(pe):
            def tr(i, j):
                if j == 0:
                    wait(pe, q.sem("free0") if conv is None else q.sem("v"), i * 3 + 3 if conv is None else i + 1)
                    wait(pe, q.sem("ev1"), i * 3)
                else:
                    wait(pe, q.sem("zw"), i + 1)
                    wait(pe, q.sem("ev0"), i * 3 + 3)
                for b in range(3):
                    wait(pe, q.sem(f"ev{j}"), i * 3 if b == 0 else i * 3 + b - 1)
                    transpose_out(pe, q, xT[j], b, T.eye, q.sem(f"tr{j}"))
            if gate:
                gate.products(pe)
            for j in range(2):
                if gate:
                    gate.free(pe, j)
                q.mm(pe, 0, j, 3)
            tr(0, 0)
            with pe.Fori(1, n) as i:
                q.mm(pe, i, 0, 3)
                tr(i - 1, 1)
                q.mm(pe, i, 1, 3)
                tr(i, 0)
            tr(n - 1, 1)

        @block.vector
        def _(dve):
            if gate:
                gate.logs(dve)
                dve.wait_ge(S("gg_hnw_in"), 16)
            if conv is not None:
                dve.memset(xs[:, 0:CONV - 1], 0.0).then_inc(q.sem("xs_zero"), 1)
                dve.wait_ge(q.sem("xs_zero"), 1)

            def ev(i, j):
                wait(dve, q.sem(f"tok_out{j}"), i * 32)
                for b in range(3):
                    wait(dve, q.sem(f"tr{j}"), i * 3 + b + 1)
                    evacuate_out(dve, dve.tensor_copy, q, tok[j], b, q.sem(f"ev{j}"))

            def epi(i):
                if conv is not None:
                    wait(dve, q.sem("free0"), i * 3 + 3)
                    wait(dve, q.sem("v"), i)
                    convolve(dve, cv, xs, T.cw, conv, i, q.sem("conv"))

            def weigh(i):
                wait(dve, q.sem("free1"), i * 3 + 3)
                dve.tensor_scalar(xT[1][:, :], xT[1][:, :], hnw[:, ds(i)], None, ALU.mult).then_inc(q.sem("zw"), 1)
            epi(0)
            ev(0, 0)
            weigh(0)
            with dve.Fori(1, n) as i:
                ev(i - 1, 1)
                epi(i)
                ev(i, 0)
                weigh(i)
            ev(n - 1, 1)


def convolve(dve, cv, xs, cw, tile0, i, done):
    def w(tap):
        return cw[:, tap, ds(i + tile0)]
    dve.tensor_scalar(cv[:, :], xs[:, 0:L], w(0), None, ALU.mult).then_inc(done, 1)
    for tap in range(1, CONV):
        wait(dve, done, i * CONV + tap)
        dve.scalar_tensor_tensor(cv[:, :], xs[:, tap:tap + L], w(tap), cv[:, :], ALU.mult, ALU.add).then_inc(done, 1)


class Step:

    def __init__(self, t, j, n):
        self.t, self.j, self.n = t, j, n

    def back(self):
        return Step(self.t - 1, 1 - self.j, self.n if self.j else self.n - 1)


def over_steps(eng, body, tail):
    body(Step(0, 0, 0), False, False)
    body(Step(1, 1, 0), True, False)
    with eng.Fori(0, (NT - 3) // 2) as i:
        body(Step(i * 2 + 2, 0, i + 1), True, True)
        body(Step(i * 2 + 3, 1, i + 1), True, True)
    last = NT - 1
    body(Step(last, 0, last // 2), True, True)
    tail(Step(last, 0, last // 2))


def split_w_out(nc, S, T, tag, w_out, whi, wlo, stage):
    w = w_out.rearrange("(k p) n -> p k n", p=P)
    NS = len(stage)

    def load(sp, ks):
        for k in ks:
            wait(sp, S(f"{tag}_wlo"), k - NS + 1)
            wait(sp, S(f"{tag}_whi"), k - NS + 1)
            sp.dma_start(stage[k % NS], w[:, k, :]).then_inc(S(f"{tag}_w_in{k % NS}"), 16)

    def hi(act, ks):
        for k in ks:
            act.wait_ge(S(f"{tag}_w_in{k % NS}"), 16 * (k // NS + 1))
            act.activation(whi[:, k, :], stage[k % NS], ACT.Copy).then_inc(S(f"{tag}_whi"), 1)

    def lo(pool, ks):
        for k in ks:
            pool.wait_ge(S(f"{tag}_w_in{k % NS}"), 16 * (k // NS + 1))
            pool.wait_ge(S(f"{tag}_whi"), k + 1)
            pool.tensor_tensor(wlo[:, k, :], stage[k % NS], whi[:, k, :].bitcast(F32), ALU.subtract)\
                .then_inc(S(f"{tag}_wlo"), 1)
    return load, hi, lo


def gla_scan(nc, S, T, w_out, x, meta, next_norm):
    with ExitStack() as ctx:
        def sb(name, shape, dt=F32):
            return ctx.enter_context(nc.sbuf_tensor(name, shape, dt))

        def ps(name, shape):
            return ctx.enter_context(nc.psum_tensor(name, shape, F32))
        whi = sb("as_whi", [P, KT, D], F32R)
        wlo = sb("as_wlo", [P, KT, D], F32R)
        qk = [sb(f"as_qk{j}", [P, GH, 2, P]) for j in range(2)]
        ko = [sb(f"as_ko{j}", [P, GH, P]) for j in range(2)]
        v = [sb(f"as_v{j}", [P, GH, GDV]) for j in range(2)]
        z = [sb(f"as_z{j}", [P, GH, GDV]) for j in range(2)]
        hres = [sb(f"as_res{j}", [P, D]) for j in range(2)]
        St = [sb(f"as_s{j}", [P, GH, GDV]) for j in range(2)]
        decs = sb("as_dec", [P, GH, 2])
        at = sb("as_at", [P, GH, P])
        og = sb("as_og", [P, GH, GDV])
        oT_hi = sb("as_othi", [P, KT, P], F32R)
        oT_lo = sb("as_otlo", [P, KT, P], F32R)
        hn = sb("as_hn", [P, D])
        junk = sb("as_junk", [P, GDV])
        nw = sb("as_nw", [P, D])
        ss = sb("as_ss", [P, GH])
        rs = sb("as_rs", [P, GH])
        ss2 = sb("as_ss2", [P, 1])
        rs2 = sb("as_rs2", [P, 1])
        pA = ps("as_pA", [P, GH, P])
        pO = ps("as_pO", [P, GH, GDV])
        pU = ps("as_pU", [P, GH, GDV])
        pT = ps("as_pT", [P, GH, P])
        pY = ps("as_pY", [P, 2, 512])
        bank = [pT, pA]
        w_load, w_hi, w_lo = split_w_out(nc, S, T, "as", w_out, whi, wlo, [hn[:, :], hres[1][:, :], nw[:, :]])
        block = ctx.enter_context(nc.Block())
        NLOAD = 4
        W_FIRST, W_REST = range(3), range(3, KT)

        @block.sync
        def _(sp):
            def load(s):
                t, j = s.t, s.j
                sem = S(f"as_in{j}")
                wait(sp, S("as_inter"), t * 2 - 2)
                wait(sp, S("as_og"), t * 4 - 4)
                sp.dma_start(qk[j][:, :, :, :].rearrange("p h w n -> p (h w) n"),
                             T.gla_qk.rearrange("h w p n -> p (h w) n")[:, :, ds(t * P, P)]).then_inc(sem, 16)
                sp.dma_start(ko[j][:, :, :].rearrange("p h d -> p (h d)"), T.gla_ko[ds(t * P, P), :]).then_inc(sem, 16)
                sp.dma_start(v[j][:, :, :].rearrange("p h d -> p (h d)"), T.gla_v[ds(t * P, P), :]).then_inc(sem, 16)
                sp.dma_start(z[j][:, :, :].rearrange("p h d -> p (h d)"), T.gla_z[ds(t * P, P), :]).then_inc(sem, 16)

            def load_residual(s):
                t, j = s.t, s.j
                sem = S(f"as_in_res{j}")
                if isinstance(t, int) and t == 0:
                    sp.dma_start(hres[0][PAD:P, :], meta).then_inc(sem, 16)
                else:
                    wait(sp, S("as_hn"), t - 1)
                    wait(sp, S("as_h1_out"), t * 16 - 16)
                    sp.dma_start(hres[j][:, :], x[ds((t - 1) * P, P), :]).then_inc(sem, 16)

            def store(s):
                wait(sp, S("as_h1"), s.t * 2 + 2)
                sp.dma_start(T.h1[ds(s.t * P, P), :], hres[s.j][:, :]).then_inc(S("as_h1_out"), 16)

            def turn(last, nxt):
                load(nxt)
                store(last)
                load_residual(nxt)
            load(Step(0, 0, 0))
            w_load(sp, range(2 * len(W_FIRST)))
            load(Step(1, 1, 0))
            sp.wait_ge(S("as_hzero"), 1)
            load_residual(Step(0, 0, 0))
            w_load(sp, range(2 * len(W_FIRST), KT))
            sp.wait_ge(S("as_wlo"), KT)
            sp.dma_start(nw[:, :], bc(next_norm, [P, D])).then_inc(S("as_nw_in"), 16)
            load_residual(Step(1, 1, 0))
            with sp.Fori(0, (NT - 3) // 2) as i:
                turn(Step(i * 2, 0, i), Step(i * 2 + 2, 0, i + 1))
                turn(Step(i * 2 + 1, 1, i), Step(i * 2 + 3, 1, i + 1))
            turn(Step(NT - 3, 0, (NT - 3) // 2), Step(NT - 1, 0, (NT - 1) // 2))
            for t in range(NT - 2, NT):
                store(Step(t, t % 2, t // 2))
            sp.wait_ge(S("as_h1_out"), 16 * NT)

        @block.tensor
        def _(pe):
            pe.wait_ge(S("as_zero"), 1)

            def arrived(s):
                wait(pe, S(f"as_in{s.j}"), s.n * (16 * NLOAD) + 16 * NLOAD)

            def outer(s, ch):
                wait(pe, S("as_su"), s.t * 8 + 4 * ch)
                r = slice(ch * C, ch * C + C)
                for h in range(GH):
                    mm = pe.matmul(pU[:, h, :], ko[s.j][r, h, :], v[s.j][r, h, :], start=True, stop=True)
                mm.then_inc(S("as_u"), 1)

            def inter(s, ch):
                wait(pe, S("as_su"), s.t * 8 + 4 * ch)
                r = slice(ch * C, ch * C + C)
                for h in range(GH):
                    mm = pe.matmul(pO[r, h, :], qk[s.j][:, h, 0, r], St[ch][:, h, :], start=False, stop=True,
                                   skip_group_check=True)
                mm.then_inc(S("as_inter"), 1)

            def transposes(src, name, s, before):
                for b in range(2):
                    wait(pe, *before(b))
                    for c in range(4):
                        kt = 4 * b + c
                        mm = pe.transpose(bank[b][:, c, :], src[:, kt * P:(kt + 1) * P], T.eye)
                    mm.then_inc(S(name), 1)

            def scan(s, has2):
                arrived(s)
                wait(pe, S("as_otlo"), s.t * 2)
                for h in range(GH):
                    mm = pe.matmul(pA[:, h, :], qk[s.j][:, h, 1, :], qk[s.j][:, h, 0, :], start=True, stop=True)
                mm.then_inc(S("as_a"), 1)
                outer(s, 0)
                if has2:
                    norm_out(s.back().back(), s)
                wait(pe, S("as_at"), s.t + 1)
                wait(pe, S("as_og"), s.t * 4)
                for h in range(GH):
                    mm = pe.matmul(pO[:, h, :], at[:, h, :], v[s.j][:, h, :], start=(h % 2 == 0), stop=False,
                                   skip_group_check=True)
                inter(s, 0)
                outer(s, 1)
                inter(s, 1)

            def norm_out(s2, s):
                wait(pe, S("as_hn"), s2.t + 1)
                ogs = hn[:, :]
                for b in range(2):
                    if b == 1 and s is not None:
                        wait(pe, S("as_at"), s.t + 1)
                    if b == 0:
                        wait(pe, S("as_otlo"), s2.t * 2 + 4 if s is not None else NT * 2)
                    if s is None:
                        wait(pe, S("as_hnlo"), s2.t * 2 + b - 1 if b else s2.t * 2)
                    for c in range(4):
                        kt = 4 * b + c
                        mm = pe.transpose(bank[b][:, c, :], ogs[:, kt * P:(kt + 1) * P], T.eye)
                    mm.then_inc(S("as_hnT"), 1)

            def out_project(s):
                wait(pe, S("as_otlo"), s.t * 2 + 2)
                wait(pe, S("as_h1"), s.t * 2)
                for n in range(2):
                    k = 0
                    for kt in range(KT):
                        for o, w in ((oT_hi, whi), (oT_hi, wlo), (oT_lo, whi)):
                            mm = pe.matmul(pY[:, n, :], o[:, kt, :], w[:, kt, n * 512:(n + 1) * 512],
                                           start=(k == 0), stop=(k == 3 * KT - 1))
                            k += 1
                    mm.then_inc(S("as_y"), 1)

            def outputs(s, has2):
                wait(pe, S("as_og"), s.t * 4 + 4)
                if has2:
                    wait(pe, S("as_hnlo"), s.t * 2 - 2)
                for b in range(2):
                    if b == 1:
                        wait(pe, S("as_at"), s.t + 1)
                    for c in range(4):
                        kt = 4 * b + c
                        mm = pe.transpose(bank[b][:, c, :], og[:, kt // 2, (kt % 2) * P:(kt % 2 + 1) * P], T.eye)
                    mm.then_inc(S("as_oT"), 1)

            def body(s, has1, has2):
                scan(s, has2)
                if has1:
                    if not has2:
                        pe.wait_ge(S("as_wlo"), KT)
                    out_project(s.back())
                outputs(s, has2)

            def tail(s):
                norm_out(s.back(), None)
                out_project(s)
                norm_out(s, None)
            over_steps(pe, body, tail)

        @block.vector
        def _(dve):
            dve.memset(at[:, :, :], 0.0).then_inc(S("as_init"), 1)
            dve.wait_ge(S("as_init"), 1)
            dve.wait_ge(S("as_zero"), 1)

            def update(s, ch):
                wait(dve, S("as_u"), s.t * 2 + ch + 1)
                if ch:
                    wait(dve, S("as_inter"), s.t * 2 + 1)
                    wait(dve, S("as_su"), s.t * 8 + 4)
                else:
                    wait(dve, S("as_inter"), s.t * 2)
                    wait(dve, S("as_dec"), s.t + 1)
                    wait(dve, S("as_su"), s.t * 8)
                for h in range(GH):
                    dve.scalar_tensor_tensor(St[1 - ch][:, h, :], St[ch][:, h, :], decs[:, h, ch:ch + 1],
                                             pU[:, h, :], ALU.mult, ALU.add).then_inc(S("as_su"), 1)

            def low(dst, hi, t, name, pre):
                for b in range(2):
                    wait(dve, S(f"as_{pre}hi"), t * 2 + b + 1)
                    dve.tensor_tensor(dst(b), bank[b][:, :, :], hi(b).bitcast(F32), ALU.subtract)\
                       .then_inc(S(f"as_{pre}lo"), 1)

            def norm_low(s):
                low(lambda b: T.hn_lo[:, 4 * b:4 * b + 4, ds(s.t * P, P)],
                    lambda b: T.hn_hi[:, 4 * b:4 * b + 4, ds(s.t * P, P)], s.t, "hn", "hn")

            def residual(s):
                wait(dve, S(f"as_in_res{s.j}"), s.n * 16 + 16)
                for n in range(2):
                    wait(dve, S("as_y"), s.t * 2 + n + 1)
                    dve.tensor_tensor(hres[s.j][:, n * 512:(n + 1) * 512], pY[:, n, :],
                                      hres[s.j][:, n * 512:(n + 1) * 512], ALU.add).then_inc(S("as_h1"), 1)

            def normed(s):
                wait(dve, S("as_rs2"), s.t + 1)
                wait(dve, S("as_h1"), s.t * 2 + 2)
                wait(dve, S("as_hnT"), s.t * 2)
                dve.wait_ge(S("as_nw_in"), 16)
                dve.scalar_tensor_tensor(hn[:, :], hres[s.j][:, :], rs2[:, 0:1], nw[:, :], ALU.mult, ALU.mult)\
                   .then_inc(S("as_hn"), 1)

            def body(s, has1, has2):
                wait(dve, S("as_su"), s.t * 8)
                dve.tensor_copy(decs[:, :, :], T.dec[:, :, ds(s.t * 2, 2)]).then_inc(S("as_dec"), 1)
                waits_apart(dve, T.dve_carrier,
                            (S("as_a"), s.t + 1),
                            (S("as_inter"), s.t * 2))
                dve.copy_predicated(at[:, :, :], bc(T.causal.bitcast(I32), [P, GH, P]), pA[:, :, :])\
                   .then_inc(S("as_at"), 1)
                update(s, 0)
                if has2:
                    norm_low(s.back().back())
                update(s, 1)
                wait(dve, S("as_rs"), s.t + 1)
                wait(dve, S("as_in%d" % s.j), s.n * (16 * NLOAD) + 16 * NLOAD)
                wait(dve, S("as_oT"), s.t * 2)
                for h in range(GH):
                    dve.scalar_tensor_tensor(og[:, h, :], pO[:, h, :], rs[:, h:h + 1], z[s.j][:, h, :],
                                             ALU.mult, ALU.mult).then_inc(S("as_og"), 1)
                if has1:
                    residual(s.back())
                low(lambda b: oT_lo[:, 4 * b:4 * b + 4, :], lambda b: oT_hi[:, 4 * b:4 * b + 4, :], s.t, "ot", "ot")
                if has1:
                    normed(s.back())

            def tail(s):
                norm_low(s.back())
                residual(s)
                normed(s)
                norm_low(s)
            over_steps(dve, body, tail)

        @block.scalar
        def _(act):
            w_hi(act, W_FIRST)

            def high(dst, s, name):
                for b in range(2):
                    wait(act, S(name), s.t * 2 + b + 1)
                    act.activation(dst(b), bank[b][:, :, :], ACT.Copy)\
                       .then_inc(S("as_othi" if name == "as_oT" else "as_hnhi"), 1)

            def norm_high(s):
                high(lambda b: T.hn_hi[:, 4 * b:4 * b + 4, ds(s.t * P, P)], s, "as_hnT")

            def squares2(s):
                wait(act, S("as_h1"), s.t * 2 + 2)
                wait(act, S("as_mean2"), s.t)
                wait(act, S("as_hnT"), s.t * 2)
                act.activation(hn[:, :], hres[s.j][:, :], ACT.Square, accum_out=ss2[:, :]).then_inc(S("as_ss2"), 1)

            def body(s, has1, has2):
                if has2:
                    norm_high(s.back().back())
                wait(act, S("as_inter"), s.t * 2 + 2)
                wait(act, S("as_mean"), s.t)
                for h in range(GH):
                    wait(act, S("as_ss"), s.t * 4 + h)
                    act.activation(junk[:, :], pO[:, h, :], ACT.Square, accum_out=ss[:, h:h + 1])\
                       .then_inc(S("as_ss"), 1)
                wait(act, S("as_y"), s.t * 2)
                high(lambda b: oT_hi[:, 4 * b:4 * b + 4, :], s, "as_oT")
                if has1:
                    squares2(s.back())
                else:
                    w_hi(act, W_REST)

            def tail(s):
                norm_high(s.back())
                squares2(s)
                norm_high(s)
            over_steps(act, body, tail)

        @block.gpsimd
        def _(pool):
            pool.memset(St[0][:, :, :], 0.0).then_inc(S("as_zero"), 1)
            pool.memset(hres[0][:, :], 0.0).then_inc(S("as_hzero"), 1)

            w_lo(pool, W_FIRST)

            def rsqrt(dst, src, width, t, ready, mean, out, used):
                waits_apart(pool, T.pool_carrier,
                            ready,
                            used)
                pool.tensor_scalar(dst[:, :], src[:, :], 1.0 / width, EPS, ALU.mult, ALU.add).then_inc(S(mean), 1)
                wait(pool, S(mean), t + 1)
                pool.tensor_tensor(dst[:, :], dst[:, :], bc(T.minus_half[:, 0:1], list(dst.shape)), ALU.pow)\
                    .then_inc(S(out), 1)

            def rs_h1(s):
                rsqrt(rs2, ss2, D, s.t, (S("as_ss2"), s.t + 1), "as_mean2", "as_rs2", (S("as_hn"), s.t))

            def body(s, has1, has2):
                rsqrt(rs, ss, GDV, s.t, (S("as_ss"), s.t * 4 + 4), "as_mean", "as_rs", (S("as_og"), s.t * 4))
                if has1:
                    rs_h1(s.back())
                else:
                    w_lo(pool, W_REST)

            def tail(s):
                rs_h1(s)
            over_steps(pool, body, tail)


def gdn_gate(nc, S, T, ctx, acc, cps, w_in, a_log, dt_bias, conv_w, head_norm):
    def sb(name, shape, dt=F32):
        return ctx.enter_context(nc.sbuf_tensor(name, shape, dt))
    st = sb("ng_w", [P, KT, P])
    hi = sb("ng_whi", [P, KT, P], F32R)
    lo = sb("ng_wlo", [P, KT, P], F32R)
    al = sb("ng_alog", [NH, 1])
    ea = sb("ng_ea", [NH, 1])
    dt = sb("ng_dt", [NH, 1])
    cm = sb("ng_starts", [NH, L])
    ax = sb("ng_ax", [NH, L])
    mx = sb("ng_mx", [NH, L])
    g = sb("ng_g", [NH, L])
    be = sb("ng_beta", [NH, L])
    NCT = (2 * NQK + NV) // P
    cwn = sb("ng_cw", [NCT, CONV, P])
    c0 = 2 * NQK + 2 * NV
    A0 = 32
    wv = w_in.rearrange("(k p) n -> p k n", p=P)

    def load(sp):
        sp.wait_ge(S("ng_zero"), 1)
        sp.dma_start(st[:, :, 0:NH], wv[:, :, c0:c0 + NH]).then_inc(S("ng_w_in"), 16)
        sp.dma_start(st[:, :, A0:A0 + NH], wv[:, :, c0 + NH:c0 + 2 * NH]).then_inc(S("ng_w_in"), 16)
        sp.dma_start(al[:, :], a_log.rearrange("(h o) -> h o", o=1)).then_inc(S("ng_small_in"), 16)
        sp.dma_start(dt[:, :], dt_bias.rearrange("(h o) -> h o", o=1)).then_inc(S("ng_small_in"), 16)
        sp.dma_start(cm[:, :], T.starts_dram[0:NH, :]).then_inc(S("ng_small_in"), 16)
        sp.dma_start(cwn[:, :, :], conv_w.rearrange("k (t p) -> t k p", p=P)).then_inc(S("ng_cw_in"), 16)
        sp.dma_start(T.hnw2[:, :], head_norm).then_inc(S("ng_hnw_in"), 16)

    def store(sp):
        sp.wait_ge(S("ng_g"), 1)
        sp.wait_ge(S("ng_beta"), 4)
        for w, src in ((0, g), (1, be)):
            sp.dma_start(T.gb[2:, :, w, :].rearrange("c h t -> h c t"),
                         src[:, NMETA:].rearrange("h (c t) -> h c t", t=C)).then_inc(S("ng_out"), 16)
            sp.dma_start(T.gb[1, :, w, C - NMETA:C], src[:, 0:NMETA]).then_inc(S("ng_out"), 16)
        sp.wait_ge(S("ng_out"), 64)
        sp.wait_ge(S("ng_hnw_in"), 16)

    def split_hi(act):
        act.wait_ge(S("ng_w_in"), 32)
        act.activation(hi[:, :, :], st[:, :, :], ACT.Copy).then_inc(S("ng_whi"), 1)

    def exponentials(act):
        act.wait_ge(S("ng_small_in"), 48)
        act.activation(ea[:, :], al[:, :], ACT.Exp).then_inc(S("ng_ea"), 1)
        act.wait_ge(S("ng_logit"), 1)
        act.wait_ge(S("ng_abs"), 1)
        for b, (s, m) in enumerate(SPANS):
            act.activation(be[:, s:s + m], acc[0:NH, b, 0:m], ACT.Exp, scale=-1.0).then_inc(S("ng_ebeta"), 1)
        act.activation(ax[:, :], ax[:, :], ACT.Exp, scale=-1.0).then_inc(S("ng_e"), 1)
        act.wait_ge(S("ng_e"), 1)
        act.activation(ax[:, :], ax[:, :], ACT.Ln, bias=1.0).then_inc(S("ng_ln"), 1)

    def split_lo(pool):
        pool.memset(st[:, :, :], 0.0).then_inc(S("ng_zero"), 1)
        pool.wait_ge(S("ng_whi"), 1)
        pool.tensor_tensor(lo[:, :, :], st[:, :, :], hi[:, :, :].bitcast(F32), ALU.subtract)\
            .then_inc(S("ng_wlo"), 1)

    def products(pe):
        pe.wait_ge(S("ng_cw_in"), 16)
        for k in range(CONV):
            mm = pe.transpose(cps[:, k, 0:NCT], cwn[:, k, :], T.k[0:NCT, K_EYE:K_EYE + NCT])
        mm.then_inc(S("ng_cwT"), 1)
        pe.wait_ge(S("ng_wlo"), 1)
        project(pe, acc, hi, lo, T).then_inc(S("ng_logit"), 1)

    def free(pe):
        pe.wait_ge(S("ng_min"), 3)
        pe.wait_ge(S("ng_ebeta"), 3)

    def logs(dve):
        dve.wait_ge(S("ng_cwT"), 1)
        dve.tensor_copy(T.cw[:, :, :], cps[:, :, 0:NCT]).then_inc(S("ng_cw"), 1)
        dve.wait_ge(S("ng_logit"), 1)
        dve.wait_ge(S("ng_small_in"), 48)
        for b, (s, m) in enumerate(SPANS):
            dve.tensor_scalar(mx[:, s:s + m], acc[A0:A0 + NH, b, 0:m], dt[:, 0:1], 0.0, ALU.add, ALU.max)\
               .then_inc(S("ng_max"), 1)
        for b, (s, m) in enumerate(SPANS):
            dve.tensor_scalar(ax[:, s:s + m], acc[A0:A0 + NH, b, 0:m], dt[:, 0:1], 0.0, ALU.add, ALU.min)\
               .then_inc(S("ng_min"), 1)
        dve.wait_ge(S("ng_max"), 3)
        dve.wait_ge(S("ng_min"), 3)
        dve.tensor_tensor(ax[:, :], mx[:, :], ax[:, :], ALU.subtract).then_inc(S("ng_abs"), 1)
        dve.wait_ge(S("ng_ebeta"), 3)
        dve.tensor_scalar(be[:, :], be[:, :], 1.0, None, ALU.add).then_inc(S("ng_beta"), 1)
        dve.wait_ge(S("ng_beta"), 1)
        dve.reciprocal(be[:, :], be[:, :]).then_inc(S("ng_beta"), 3)
        dve.wait_ge(S("ng_ln"), 1)
        dve.wait_ge(S("ng_max"), 3)
        dve.wait_ge(S("ng_ea"), 1)
        dve.tensor_tensor(mx[:, :], mx[:, :], ax[:, :], ALU.add).then_inc(S("ng_sp"), 1)
        dve.wait_ge(S("ng_sp"), 1)
        dve.tensor_scalar(mx[:, :], mx[:, :], ea[:, 0:1], -1.0, ALU.mult, ALU.mult).then_inc(S("ng_sp"), 1)
        dve.wait_ge(S("ng_sp"), 2)
        dve.tensor_tensor_scan(g[:, :], cm[:, :], mx[:, :], 0.0, ALU.mult, ALU.add).then_inc(S("ng_g"), 1)
        dve.wait_ge(S("ng_cw"), 1)
    return load, store, split_hi, exponentials, split_lo, products, free, logs


def gdn_qk(nc, S, T, w_in, *gate_args):
    n = NH
    with ExitStack() as ctx:
        q = Proj(nc, S, T, ctx, "nq", w_in, lambda i, j: j * NQK + i * P)

        def sb(name, shape):
            return ctx.enter_context(nc.sbuf_tensor(name, shape, F32))
        xs = sb("nq_xs", [P, CONV - 1 + L])
        cv = sb("nq_cv", [P, L])
        xT = [sb(f"nq_x{j}", [P, L]) for j in range(2)]
        tok = [sb(f"nq_tok{j}", [P, NT, P]) for j in range(2)]
        sq = sb("nq_sq", [P, NT, P])
        ss = [sb(f"nq_ss{j}", [P, NT]) for j in range(2)]
        xn = [sb(f"nq_xn{j}", [P, L]) for j in range(2)]
        gate_load, gate_store, gate_hi, gate_exps, gate_lo, gate_products, gate_free, gate_logs = \
            gdn_gate(nc, S, T, ctx, q.acc[1], q.trA, w_in, *gate_args)
        block = ctx.enter_context(nc.Block())

        @block.sync
        def _(sp):
            def store_tok(i):
                wait(sp, q.sem("norm1"), i + 1)
                store_tokens(sp, T.gdn_k, tok[1], i * P, NQK, q.sem("tok_out"))

            def store(i, j):
                wait(sp, q.sem(f"evn{j}"), i * 3 + 3)
                sp.dma_start(T.gdn_qk[j, ds(i), :, PAD:TP].rearrange("a p n -> p (a n)"), xn[j][:, :])\
                  .then_inc(q.sem(f"out{j}"), 16)
            gate_load(sp)
            for j in range(2):
                q.load(sp, 0, j)
            for j in range(2):
                q.load(sp, 1, j)
            with sp.Fori(0, n - 2) as i:
                for j in range(2):
                    q.load(sp, i + 2, j)
                store_tok(i)
                for j in range(2):
                    store(i, j)
            for i in range(n - 2, n):
                store_tok(i)
                for j in range(2):
                    store(i, j)
            gate_store(sp)
            sp.wait_ge(q.sem("tok_out"), 32 * n)
            for j in range(2):
                sp.wait_ge(q.sem(f"out{j}"), 16 * n)

        @block.scalar
        def _(act):
            def copy(i, j):
                wait(act, q.sem(f"mm{j}"), i + 1)
                if j == 0:
                    wait(act, q.sem("conv1"), i * CONV)
                else:
                    wait(act, q.sem("conv0"), i * CONV + CONV)
                for b, (s, m) in enumerate(SPANS):
                    act.activation(xs[:, CONV - 1 + s:CONV - 1 + s + m], q.acc[j][:, b, 0:m], ACT.Copy)\
                       .then_inc(q.sem(f"free{j}"), 1)

            def silu(i, j):
                wait(act, q.sem(f"conv{j}"), i * CONV + CONV)
                wait(act, q.sem(f"tr{j}"), i * 3)
                act.activation(xT[j][:, :], cv[:, :], ACT.Silu).then_inc(q.sem(f"silu{j}"), 1)

            def square(i, j):
                wait(act, q.sem(f"ev{j}"), i * 3 + 3)
                if j == 0:
                    wait(act, q.sem("ss1"), i)
                else:
                    wait(act, q.sem("ss0"), i + 1)
                act.activation(sq[:, :, :], tok[j][:, :, :], ACT.Square).then_inc(q.sem(f"sq{j}"), 1)

            def back(i, j):
                wait(act, q.sem(f"out{j}"), i * 16)
                for b in range(3):
                    wait(act, q.sem(f"trn{j}"), i * 3 + b + 1)
                    if b < 2:
                        s = NMETA + 4 * b * P
                        act.activation(xn[j][:, s:s + 4 * P], (q.trA, q.trB)[b][:, :, :].rearrange("p a b -> p (a b)"),
                                       ACT.Copy).then_inc(q.sem(f"evn{j}"), 1)
                    else:
                        act.activation(xn[j][:, 0:NMETA], q.trA[:, 0, 0:NMETA], ACT.Copy).then_inc(q.sem(f"evn{j}"), 1)

            def body(i, first, last):
                copy(i, 0)
                if not last:
                    q.split_hi(act, i + 1, 0)
                if not first:
                    square(i - 1, 1)
                    back(i - 1, 0)
                silu(i, 0)
                copy(i, 1)
                if not last:
                    q.split_hi(act, i + 1, 1)
                square(i, 0)
                if not first:
                    back(i - 1, 1)
                silu(i, 1)
            gate_hi(act)
            for j in range(2):
                q.split_hi(act, 0, j)
            gate_exps(act)
            body(0, True, False)
            with act.Fori(1, n - 1) as i:
                body(i, False, False)
            body(n - 1, False, True)
            square(n - 1, 1)
            back(n - 1, 0)
            back(n - 1, 1)

        @block.gpsimd
        def _(pool):
            def norm(i, j):
                waits_apart(pool, T.pool_carrier,
                            (q.sem(f"ss{j}"), i + 1))
                pool.tensor_scalar(ss[j][:, :], ss[j][:, :], EPS, (float(NDK), 1.0)[j], ALU.add, ALU.mult)\
                    .then_inc(q.sem(f"sum{j}"), 1)
                wait(pool, q.sem(f"sum{j}"), i + 1)
                pool.tensor_tensor(ss[j][:, :], ss[j][:, :], bc(T.minus_half[:, 0:1], [P, NT]), ALU.pow)\
                    .then_inc(q.sem(f"rs{j}"), 1)
                wait(pool, q.sem(f"rs{j}"), i + 1)
                pool.tensor_tensor(tok[j][:, :, :], tok[j][:, :, :],
                                   bc(ss[j][:, :].rearrange("p (t o) -> p t o", o=1), [P, NT, P]), ALU.mult)\
                    .then_inc(q.sem(f"norm{j}"), 1)

            def body(i, first, last):
                if not last:
                    q.split_lo(pool, i + 1, 0)
                if not first:
                    norm(i - 1, 1)
                if not last:
                    q.split_lo(pool, i + 1, 1)
                norm(i, 0)
            gate_lo(pool)
            for j in range(2):
                pool.memset(tok[j][:, :, :], 0.0).then_inc(q.sem("tok_zero"), 1)
            for j in range(2):
                q.split_lo(pool, 0, j)
            body(0, True, False)
            with pool.Fori(1, n - 1) as i:
                body(i, False, False)
            body(n - 1, False, True)
            norm(n - 1, 1)

        @block.tensor
        def _(pe):
            def tr(i, j):
                wait(pe, q.sem(f"silu{j}"), i + 1)
                if j == 1:
                    wait(pe, q.sem("ev0"), i * 3 + 3)
                    wait(pe, q.sem("evn1"), i * 3)
                else:
                    wait(pe, q.sem("ev1"), i * 3)
                    wait(pe, q.sem("evn0"), i * 3)
                for b in range(3):
                    if b == 2:
                        wait(pe, q.sem(f"ev{j}"), i * 3 + 1)
                    transpose_out(pe, q, xT[j], b, T.eye, q.sem(f"tr{j}"))

            def back(i, j):
                wait(pe, q.sem(f"norm{j}"), i + 1)
                yield_to = q.sem("ev1") if j == 0 else q.sem("ev0")
                wait(pe, yield_to, i * 3 + 3 if j == 0 else (i * 3 + 6 if not isinstance(i, int) else min(i * 3 + 6, 3 * n)))
                if j == 1:
                    wait(pe, q.sem("evn0"), i * 3 + 3)
                for b in range(3):
                    if b == 2:
                        waits_apart(pe, T.pe_carrier,
                                    (q.sem(f"evn{j}"), i * 3 + 1))
                    bankd = (q.trA, q.trB, q.trA)[b]
                    if b < 2:
                        for c in range(4):
                            mm = pe.transpose(bankd[:, c, :], tok[j][:, 1 + 4 * b + c, :], T.eye)
                    else:
                        mm = pe.transpose(bankd[:, 0, 0:NMETA], tok[j][0:NMETA, 0, :],
                                          T.k[0:NMETA, K_EYE:K_EYE + NMETA])
                    mm.then_inc(q.sem(f"trn{j}"), 1)
            gate_products(pe)
            q.mm(pe, 0, 0, 3)
            gate_free(pe)
            q.mm(pe, 0, 1, 3)
            tr(0, 0)
            with pe.Fori(1, n) as i:
                q.mm(pe, i, 0, 3)
                tr(i - 1, 1)
                back(i - 1, 0)
                q.mm(pe, i, 1, 3)
                tr(i, 0)
                back(i - 1, 1)
            tr(n - 1, 1)
            back(n - 1, 0)
            back(n - 1, 1)

        @block.vector
        def _(dve):
            dve.memset(xs[:, 0:CONV - 1], 0.0).then_inc(q.sem("xs_zero"), 1)
            dve.wait_ge(q.sem("xs_zero"), 1)
            dve.wait_ge(q.sem("tok_zero"), 2)
            gate_logs(dve)

            def ev(i, j):
                if j == 1:
                    wait(dve, q.sem("tok_out"), i * 32)
                wait(dve, q.sem(f"trn{j}"), i * 3)
                for b in range(3):
                    wait(dve, q.sem(f"tr{j}"), i * 3 + b + 1)
                    evacuate_out(dve, dve.tensor_copy, q, tok[j], b, q.sem(f"ev{j}"))
                wait(dve, q.sem(f"sq{j}"), i + 1)
                wait(dve, q.sem(f"norm{j}"), i)
                dve.tensor_reduce(ss[j][:, :], sq[:, :, :], AX.X, ALU.add).then_inc(q.sem(f"ss{j}"), 1)

            def conv(i, j):
                wait(dve, q.sem(f"free{j}"), i * 3 + 3)
                if j == 0:
                    wait(dve, q.sem("silu1"), i)
                else:
                    wait(dve, q.sem("silu0"), i + 1)
                convolve(dve, cv, xs, T.cw, j * NH, i, q.sem(f"conv{j}"))
            conv(0, 0)
            ev(0, 0)
            conv(0, 1)
            with dve.Fori(1, n) as i:
                ev(i - 1, 1)
                conv(i, 0)
                ev(i, 0)
                conv(i, 1)
            ev(n - 1, 1)


class Chunk:

    def __init__(self, c, j):
        self.c, self.m, self.j, self.par = c, c - 1, j, 1 - j

    def ahead(self, k):
        return Chunk(self.c + k, (self.j + k) % 2)


def over_chunks(eng, chunk, tail):
    chunk(Chunk(1, 1), None, 0, 2)
    for t in (1, 2):
        chunk(Chunk(2 * t, 0), t, t - 1, 2)
        chunk(Chunk(2 * t + 1, 1), t, t - 1, 2)
    with eng.Fori(3, NT - 1) as t:
        chunk(Chunk(t * 2, 0), t, 2, 2)
        chunk(Chunk(t * 2 + 1, 1), t, 2, 2)
    chunk(Chunk(2 * NT - 2, 0), NT - 1, 2, 1)
    chunk(Chunk(2 * NT - 1, 1), NT - 1, 2, 0)
    tail()


def gdn_scan(nc, S, T, w_out, out_norm, out):
    KO = NV // P
    LV = len(LEVELS)
    R = [slice(0, C), slice(C, P)]
    with ExitStack() as ctx:
        def sb(name, shape, dt=F32):
            return ctx.enter_context(nc.sbuf_tensor("ns_" + name, shape, dt))

        def ps(name, shape):
            return ctx.enter_context(nc.psum_tensor("ns_" + name, shape, F32))
        whi = sb("whi", [P, KO, D], F32R)
        wlo = sb("wlo", [P, KO, D], F32R)
        kq = sb("kq", [P, NH, 2, C])
        kqd = sb("kqd", [P, NH, 2, C])
        kt = sb("kt", [P, HP, NDK])
        v = sb("v", [P, HP, NDV])
        og = [sb(f"og{n}", [P, HP, NDV]) for n in range(2)]
        gb = sb("gb", [P, NH, 2, C])
        gp = sb("gp", [P, HP, 2, C])
        gbc = sb("gbc", [P, HP, 2])
        St = sb("s", [P, NH, NDV])
        er = gb[:, :, 0, :]
        dec = [sb(f"dec{n}", [P, NH]) for n in range(2)]
        d1 = sb("d1", [P, HP, C])
        junk = d1[:, :, :].rearrange("p h c -> p (h c)")
        dn = [sb(f"dn{n}", [P, HP, C]) for n in range(2)]
        dx = sb("dx", [P, HP, C])
        mm2 = sb("mm2", [P, 2, HP, C])
        M, mtf = mm2[:, 0], mm2[:, 1]
        tg = mm2[:, :, :, :].rearrange("p a h c -> p (a h) c")
        low = [mtf] + [sb(f"low{n}", [P, HP, C])[:, :, :] for n in range(1, 1 + LV)]
        U = [sb(f"u{n}", [P, HP, C]) for n in range(2)]
        Ti = sb("ti", [P, HP, C])
        Pm = sb("pm", [P, HP, C])
        kdl = sb("kdl", [P, HP])
        kdec = kt
        vn = sb("vn", [P, HP, NDV])
        with nc.sbuf_tensor("ns_stage", [P, 4, D], F32) as early:
            pass
        oT_hi = sb("othi", [P, KO, P], F32R)
        oT_lo = sb("otlo", [P, KO, P], F32R)
        h = sb("h", [P, D])
        nw = vn[:, :, :].rearrange("p h v -> p (h v)")
        ss = sb("ss", [P, HP])
        ss2 = sb("ss2", [P, 1])
        pX = [ps(f"px{p}", [P, HP, NDV]) for p in range(2)]
        p4 = ps("p4", [P, 512])
        p56 = ps("p56", [P, 2, 512])
        pY = ps("py", [P, 512])
        pKK = p4[:, 0:HP * C].rearrange("p (h c) -> p h c", c=C)
        pQK = p4[:, HP * C:2 * HP * C].rearrange("p (h c) -> p h c", c=C)
        pP, pUP, pPT = pKK, pQK, pKK
        pS = [p56[:, p, :].rearrange("p (h v) -> p h v", v=NDV) for p in range(2)]
        pT = [p56[:, b, :].rearrange("p (x c) -> p x c", c=C) for b in range(2)]
        block = ctx.enter_context(nc.Block())

        stage = [early[:, b, :] for b in range(4)] + [h[:, :]]
        NS = len(stage)
        parts = [range(0, NS), range(NS, NS + 5), range(NS + 5, KO)]
        load_w, hi_w, lo_w = split_w_out(nc, S, T, "ns", w_out, whi, wlo, stage)

        def w_load(sp, part):
            load_w(sp, parts[part])

        def w_hi(act, part, nth):
            hi_w(act, list(parts[part])[nth:nth + 1 if nth < LV - 1 else None])

        def w_lo(pool, part):
            lo_w(pool, parts[part])

        def part_of(t, ch):
            return 1 if t is None else 2 if isinstance(t, int) and t == 1 and ch.j == 0 else None

        def eye_p(shape):
            return bc(T.k[:, K_EYEP:K_EYEP + C].rearrange("p (o c) -> p o c", o=1), shape)

        def mask(col):
            return bc(T.k[:, col:col + C].rearrange("p (o c) -> p o c", o=1), [P, HP, C])

        def transposed(t, ch, done):
            return t is not None and (ch.j == 1 or done)

        @block.sync
        def _(sp):
            def tokens(dst, src, ch, width, swap, sem):
                for p in range(2):
                    rows = R[1 - p] if swap else R[p]
                    sp.dma_start(dst[rows, :, :],
                                 src[ds(ch.c * C, C), :].rearrange("t (h p d) -> t h p d", p=2, d=width)[:, :, p, :])\
                      .then_inc(sem, 16)

            def load_gp(ch):
                m = ch.m
                wait(sp, S("ns_mtf"), m * 2)
                wait(sp, S("ns_kdl"), m)
                wait(sp, S("ns_d1"), m)
                wait(sp, S("ns_tg"), m)
                for p in range(2):
                    src = T.gb[ds(ch.c)].rearrange("o (h p) w c -> o h p w c", p=2)[:, :, p]
                    sp.dma_start(gp[R[p], :, :, :], bc(src, [C, HP, 2, C])).then_inc(S("ns_in_g"), 16)

            def load_kq(ch):
                m = ch.m
                wait(sp, S("ns_kqd"), m * 3)
                wait(sp, S("ns_g"), m)
                for w_ in range(2):
                    for p in range(2):
                        src = T.gdn_qk[w_].rearrange("(h p) d n -> d h p n", p=2)[:, :, p, ds(ch.c * C, C)]
                        slot = 1 - w_ if p == 0 else w_
                        sp.dma_start(kq[:, p::2, slot, :], src).then_inc(S("ns_in_kq"), 16)
                wait(sp, S("ns_dec"), m)
                sp.dma_start(gb[:, :, :, :], bc(T.gb[ds(ch.c)], [P, NH, 2, C])).then_inc(S("ns_in_gb"), 16)

            def load_v(ch):
                wait(sp, S("ns_v"), ch.m)
                tokens(v, T.gdn_v, ch, NDV, False, S("ns_in_v"))

            def load_kt(ch):
                wait(sp, S("ns_ds"), ch.m * 2)
                tokens(kt, T.gdn_k, ch, NDK, False, S("ns_in_kt"))

            def load_z(ch):
                m = ch.m
                if isinstance(m, int) and m == 2:
                    sp.wait_ge(S("ns_og"), 8)
                wait(sp, S("ns_oT"), m * 2 - 4)
                tokens(og[ch.par], T.gdn_z, ch, NDV, True, S(f"ns_in_z{ch.par}"))

            def load_h(t):
                sp.dma_start(h[:, :], T.h1[ds(t * P, P), :]).then_inc(S("ns_in_h"), 16)

            def load_nw(t):
                wait(sp, S("ns_ss2"), t)
                sp.dma_start(nw, bc(out_norm, [P, D])).then_inc(S("ns_nw_in"), 16)

            def store_out(t):
                wait(sp, S("ns_final"), t)
                sp.dma_start(out[ds((t - 1) * P, P), :], h[:, :]).then_inc(S("ns_out"), 16)
                wait(sp, S("ns_out"), t * 16)

            def chunk(ch, left):
                if left > 1:
                    load_gp(ch.ahead(2))
                if left > 0:
                    load_v(ch.ahead(1))
                if left > 1:
                    load_kq(ch.ahead(2))
                if left > 0:
                    load_kt(ch.ahead(1))
                    load_z(ch.ahead(1))

            first = Chunk(1, 1)
            load_gp(first)
            load_kq(first)
            load_v(first)
            load_kt(first)
            load_z(first)
            w_load(sp, 0)
            load_gp(first.ahead(1))
            load_kq(first.ahead(1))
            chunk(first, 2)
            w_load(sp, 1)
            chunk(Chunk(2, 0), 2)
            w_load(sp, 2)
            chunk(Chunk(3, 1), 2)
            sp.wait_ge(S("ns_wlo"), KO)
            load_h(1)
            chunk(Chunk(4, 0), 2)
            chunk(Chunk(5, 1), 2)
            with sp.Fori(3, NT - 1) as t:
                load_nw(t - 2)
                store_out(t - 2)
                load_h(t - 1)
                chunk(Chunk(t * 2, 0), 2)
                chunk(Chunk(t * 2 + 1, 1), 2)
            load_nw(NT - 3)
            store_out(NT - 3)
            load_h(NT - 2)
            chunk(Chunk(2 * NT - 2, 0), 1)
            chunk(Chunk(2 * NT - 1, 1), 0)
            load_nw(NT - 2)
            store_out(NT - 2)
            load_h(NT - 1)
            load_nw(NT - 1)
            store_out(NT - 1)

        @block.tensor
        def _(pe):
            def pairs():
                for hp in range(HP):
                    for p in range(2):
                        yield hp, p, R[p]

            def out_stream(t):
                steps = []
                n = 3 * KO
                for half in range(2):
                    for kk in range(KO):
                        hp, d, x = kk // 4, kk // 2 % 2, kk % 2
                        row = (2 * hp + 1 - x) * 2 + d
                        for e, (o, w_) in enumerate(((oT_hi, whi), (oT_hi, wlo), (oT_lo, whi))):
                            def step(i=3 * kk + e, o=o, w_=w_, kk=kk, row=row, half=half):
                                if i == 0:
                                    if half == 0:
                                        wait(pe, S("ns_otlo"), t * 4)
                                    wait(pe, S("ns_yd"), t * 2 - 2 + half)
                                mm = pe.matmul(pY[:, :], o[:, kk, :], w_[:, row, half * 512:half * 512 + 512],
                                               start=(i == 0), stop=(i == n - 1))
                                if i == n - 1:
                                    mm.then_inc(S("ns_y"), 1)
                            steps.append(step)
                return steps

            def outputs(m, m_par):
                wait(pe, S("ns_otlo"), m * 2 - 2)
                wait(pe, S("ns_og"), m * 8 + 8)
                for b in range(2):
                    for a in range(2):
                        for d in range(2):
                            i0 = (a * 2 + d) * 2
                            mm = pe.transpose(pT[b][:, i0:i0 + 2, :], og[m_par][:, 2 * b + a, d * P:(d + 1) * P], T.eye)
                    mm.then_inc(S("ns_oT"), 1)

            def scores(ch):
                m = ch.m
                wait(pe, S("ns_in_kq"), m * 64 + 64)
                wait(pe, S("ns_u"), m * (LV + 1))
                for hp, p, r in pairs():
                    kk_, qq_ = (0, 1) if p == 0 else (1, 0)
                    hd = 2 * hp + p
                    pe.matmul(pKK[r, hp, :], kq[:, hd, kk_, :], kq[:, hd, kk_, :], start=True, stop=True)
                    mm = pe.matmul(pQK[r, hp, :], kq[:, hd, kk_, :], kq[:, hd, qq_, :], start=True, stop=True)
                mm.then_inc(S("ns_g"), 1)

            def level_p(ch, l):
                m = ch.m
                waits_apart(pe, T.pe_carrier,
                            (S("ns_u"), m * (LV + 1) + l + 1),
                            (S("ns_low"), m * LV + l + 1),
                            (S("ns_at"), (m + 1) if l == 0 else 0),
                            (S("ns_t"), m * LV + l + 1))
                for hp, p, r in pairs():
                    mm = pe.matmul(pP[r, hp, :], low[l + 1][r, hp, :], U[ch.par][r, hp, :], start=True, stop=True)
                mm.then_inc(S("ns_p"), 1)

            def level_u(ch, l):
                m = ch.m
                waits_apart(pe, T.pe_carrier,
                            (S("ns_pm"), m * LV + l + 1))
                for hp, p, r in pairs():
                    mm = pe.matmul(pUP[r, hp, :], Ti[r, hp, :], Pm[r, hp, :], start=True, stop=True)
                mm.then_inc(S("ns_up"), 1)
                if l < LV - 1:
                    for hp, p, r in pairs():
                        mm = pe.matmul(pPT[r, hp, :], Pm[r, hp, :], Ti[r, hp, :], start=True, stop=True)
                    mm.then_inc(S("ns_pt"), 1)

            def chunk(ch, t, done, left):
                m, j = ch.m, ch.j
                nxt = ch.ahead(1)
                stream = []
                if done:
                    stream = out_stream(t - 1)
                    stream = stream[48:] if j else stream[:48]

                def fill(k):
                    for _ in range(k):
                        if stream:
                            stream.pop(0)()
                wait(pe, S("ns_kqd"), m * 3 + 3)
                wait(pe, S("ns_su"), m * 8)
                wait(pe, S("ns_og"), m * 8)
                for hp, p, r in pairs():
                    hd = 2 * hp + p
                    mm = pe.matmul(pX[p][:, hp, :], kqd[:, hd, :, :].rearrange("p w c -> p (w c)"), St[:, hd, :],
                                   start=(hp % 2 == 0), stop=False, skip_group_check=True)
                mm.then_inc(S("ns_x"), 1)
                if j == 0 and transposed(t, ch, done):
                    outputs(m - 1, 1 - ch.par)
                if j:
                    fill(4)
                if left > 0:
                    scores(nxt)
                waits_apart(pe, T.pe_carrier,
                            (S("ns_r"), m * 2 + 2),
                            (S("ns_u"), m * (LV + 1) + LV + 1))
                for hp, p, r in pairs():
                    mm = pe.matmul(pX[p][r, hp, :], U[ch.par][r, hp, :], v[r, hp, :],
                                   start=(hp % 2 == 0), stop=True, skip_group_check=True)
                mm.then_inc(S("ns_v"), 1)
                fill(8)
                waits_apart(pe, T.pe_carrier,
                            (S("ns_vn0"), m + 1),
                            (S("ns_vn1"), m + 1),
                            (S("ns_at"), m + 1))
                for hp, p, r in pairs():
                    mm = pe.matmul(pX[p][R[1 - p], hp, :], dn[ch.par][r, hp, :], vn[r, hp, :], start=False, stop=True,
                                   skip_group_check=True)
                mm.then_inc(S("ns_o"), 1)
                fill(8)
                for rnd in range(2):
                    if rnd:
                        wait(pe, S("ns_su"), m * 8 + 4)
                    else:
                        waits_apart(pe, T.pe_carrier,
                                    (S("ns_kdec"), m + 1),
                                    (S("ns_otlo"), m * 2 - 2 if j == 0 and transposed(t, ch, done) else 0))
                    for a in range(2):
                        for p in range(2):
                            hp = 2 * rnd + a
                            mm = pe.matmul(pS[p][:, a, :], kdec[R[p], hp, :], vn[R[p], hp, :], start=True, stop=True)
                    mm.then_inc(S("ns_ds"), 1)
                    if rnd == 0 and left > 0:
                        level_p(nxt, 0)
                    if rnd == 0:
                        fill(4)
                if left > 0:
                    level_u(nxt, 0)
                    for l in range(1, LV):
                        k = 4 if j == 0 and l < 3 else 3
                        fill(k)
                        level_p(nxt, l)
                        fill(k)
                        level_u(nxt, l)
                fill(len(stream))
                if j and transposed(t, ch, done):
                    wait(pe, S("ns_su"), m * 8 + 8)
                    outputs(m - 1, 1 - ch.par)

            def tail():
                outputs(2 * NT - 2, (2 * NT - 2) % 2)
                for step in out_stream(NT - 1):
                    step()
            first = Chunk(1, 1)
            pe.wait_ge(S("ns_init"), 1)
            scores(first)
            for l in range(LV):
                level_p(first, l)
                level_u(first, l)
            over_chunks(pe, chunk, tail)

        @block.scalar
        def _(act):
            def high(m, half):
                for b in range(2):
                    wait(act, S("ns_oT"), (m - 1) * 2 + b + 1)
                    act.activation(oT_hi[:, 8 * b:8 * b + 8, half * C:half * C + C], pT[b], ACT.Copy)\
                       .then_inc(S("ns_othi"), 1)

            def decays(ch):
                m = ch.m
                wait(act, S("ns_in_gb"), m * 16 + 16)
                wait(act, S("ns_su"), (m - 1) * 8)
                act.activation(dec[ch.par][:, :], gb[:, :, 0, C - 1], ACT.Exp).then_inc(S("ns_dec"), 1)
                wait(act, S("ns_dec"), m + 1)
                act.activation(er[:, :, :], gb[:, :, 0, :], ACT.Exp).then_inc(S("ns_er"), 1)
                wait(act, S("ns_kdl"), m + 1)
                act.activation(kdl[:, :], kdl[:, :], ACT.Exp).then_inc(S("ns_ekdl"), 1)
                wait(act, S("ns_dn"), m + 1)
                act.activation(dn[ch.par][:, :, :], dn[ch.par][:, :, :], ACT.Exp).then_inc(S("ns_edn"), 1)
                wait(act, S("ns_dx"), m + 1)
                act.activation(dx[:, :, :], dx[:, :, :], ACT.Exp, scale=-1.0).then_inc(S("ns_edx"), 1)

            def level(ch, l):
                m = ch.m
                wait(act, S("ns_p"), m * LV + l + 1)
                if l:
                    wait(act, S("ns_pt"), m * (LV - 1) + l)
                else:
                    wait(act, S("ns_up"), m * LV)
                act.activation(Pm[:, :, :], pP, ACT.Copy).then_inc(S("ns_pm"), 1)

            def chunk(ch, t, done, left):
                m, j = ch.m, ch.j
                nxt = ch.ahead(1)
                if left > 0:
                    decays(nxt)
                if j == 0 and transposed(t, ch, done):
                    high(m - 1, 1)
                wait(act, S("ns_v"), m + 1)
                wait(act, S("ns_ds"), m * 2)
                if j == 0 and done > 1:
                    wait(act, S("ns_final"), t - 2)
                act.activation(vn[R[0], :, :], pX[0][R[0], :, :], ACT.Copy).then_inc(S("ns_vn0"), 1)
                wait(act, S("ns_o"), m + 1)
                wait(act, S("ns_rs"), m * 2)
                if left > 0:
                    wait(act, S("ns_u"), (m + 1) * (LV + 1) + 1)
                for n, (hp, p) in enumerate((hp, p) for hp in range(HP) for p in range(2)):
                    r = R[1 - p]
                    act.activation(junk[r, :], pX[p][r, hp, :], ACT.Square, accum_out=ss[r, hp:hp + 1])\
                       .then_inc(S("ns_ss"), 1)
                    wait(act, S("ns_ss"), m * 8 + n + 1)
                if left > 0:
                    for l in range(LV):
                        level(nxt, l)
                        if part_of(t, ch):
                            w_hi(act, part_of(t, ch), l)
                if j == 1 and transposed(t, ch, done):
                    if not done:
                        act.wait_ge(S("ns_wlo"), KO)
                    high(m - 1, 0)
                if j and done:
                    norm2(t - 1)

            def norm2(t):
                wait(act, S("ns_yd"), t * 2)
                wait(act, S("ns_ds"), t * 4 + 6)
                act.activation(vn[:, :, :].rearrange("p a b -> p (a b)"), h[:, :], ACT.Square, accum_out=ss2[:, :])\
                   .then_inc(S("ns_ss2"), 1)

            def tail():
                high(2 * NT - 2, 1)
                wait(act, S("ns_yd"), 2 * NT - 2)
                wait(act, S("ns_final"), NT - 2)
                act.activation(vn[:, :, :].rearrange("p a b -> p (a b)"), h[:, :], ACT.Square, accum_out=ss2[:, :])\
                   .then_inc(S("ns_ss2"), 1)
            first = Chunk(1, 1)
            decays(first)
            for l in range(LV):
                level(first, l)
                w_hi(act, 0, l)
            over_chunks(act, chunk, tail)

        @block.vector
        def _(dve):
            dve.memset(St[:, :, :], 0.0).then_inc(S("ns_init"), 1)

            def lo(m, half):
                for b in range(2):
                    wait(dve, S("ns_othi"), (m - 1) * 2 + b + 1)
                    dve.tensor_tensor(oT_lo[:, 8 * b:8 * b + 8, half * C:half * C + C], pT[b],
                                      oT_hi[:, 8 * b:8 * b + 8, half * C:half * C + C].bitcast(F32), ALU.subtract)\
                       .then_inc(S("ns_otlo"), 1)

            def residual(t, half):
                wait(dve, S("ns_y"), t * 2 - 1 + half)
                wait(dve, S("ns_in_h"), t * 16)
                c = slice(half * 512, half * 512 + 512)
                dve.tensor_tensor(h[:, c], pY[:, :], h[:, c], ALU.add).then_inc(S("ns_yd"), 1)

            def final(t):
                wait(dve, S("ns_nw_in"), t * 16)
                wait(dve, S("ns_rs2"), t)
                wait(dve, S("ns_yd"), t * 2)
                dve.scalar_tensor_tensor(h[:, :], h[:, :], ss2[:, 0:1], nw, ALU.mult, ALU.mult)\
                   .then_inc(S("ns_final"), 1)

            def differences(ch):
                m = ch.m
                wait(dve, S("ns_tg"), m + 1)
                wait(dve, S("ns_vb"), m)
                dve.tensor_reduce(gbc[:, :, :].rearrange("p h w -> p (h w)"), tg, AX.X, ALU.add).then_inc(S("ns_gbc"), 1)
                wait(dve, S("ns_gbc"), m + 1)
                wait(dve, S("ns_in_g"), m * 32 + 32)
                wait(dve, S("ns_dx"), m)
                wait(dve, S("ns_ss"), (m - 1) * 8)
                dve.tensor_tensor(d1[:, :, :], gp[:, :, 0, :], bc(gbc[:, :, 0:1], [P, HP, C]), ALU.subtract)\
                   .then_inc(S("ns_d1"), 1)
                wait(dve, S("ns_kdec"), m)
                dve.tensor_tensor(kdl[:, :], gp[:, :, 0, C - 1], gbc[:, :, 0], ALU.subtract).then_inc(S("ns_kdl"), 1)
                wait(dve, S("ns_d1"), m + 1)
                wait(dve, S("ns_o"), m - 1)
                dve.tensor_scalar(dn[ch.par][:, :, :], d1[:, :, :], 0.0, None, ALU.min).then_inc(S("ns_dn"), 1)
                wait(dve, S("ns_m"), m)
                dve.tensor_scalar(dx[:, :, :], d1[:, :, :], 0.0, None, ALU.max).then_inc(S("ns_dx"), 1)

            def first_inverse(ch):
                m = ch.m
                wait(dve, S("ns_g"), m + 1)
                wait(dve, S("ns_dxb"), m + 1)
                wait(dve, S("ns_low"), m * LV)
                dve.tensor_tensor(M, pKK, dx[:, :, :], ALU.mult).then_inc(S("ns_m"), 1)
                wait(dve, S("ns_mtf"), m * 2 + 2)
                dve.tensor_tensor(d1[:, :, :], pKK, mtf, ALU.mult).then_inc(S("ns_mt"), 1)
                wait(dve, S("ns_mt"), m + 1)
                wait(dve, S("ns_v"), m - 1)
                dve.tensor_tensor(U[ch.par][:, :, :], eye_p([P, HP, C]), d1[:, :, :], ALU.subtract)\
                   .then_inc(S("ns_u"), 1)
                wait(dve, S("ns_dnm"), m + 1)
                dve.tensor_tensor(dn[ch.par][:, :, :], pQK, dn[ch.par][:, :, :], ALU.mult).then_inc(S("ns_at"), 1)

            def level(ch, l):
                m = ch.m
                wait(dve, S("ns_up"), m * LV + l + 1)
                wait(dve, S("ns_u"), m * (LV + 1) + l + 1)
                if l < LV - 1:
                    wait(dve, S("ns_pt"), m * (LV - 1) + l + 1)
                dve.tensor_tensor(U[ch.par][:, :, :], U[ch.par][:, :, :], pUP, ALU.subtract).then_inc(S("ns_u"), 1)
                if l < LV - 1:
                    wait(dve, S("ns_t"), m * LV + l + 1)
                    dve.tensor_tensor(Ti[:, :, :], Ti[:, :, :], pPT, ALU.subtract).then_inc(S("ns_t"), 1)

            def chunk(ch, t, done, left):
                m, j = ch.m, ch.j
                nxt = ch.ahead(1)
                if left > 0:
                    differences(nxt)
                for p in range(2):
                    wait(dve, S("ns_vb"), m + 1)
                    wait(dve, S("ns_x"), m + 1)
                    dve.tensor_tensor(v[R[p], :, :], v[R[p], :, :], pX[p][R[p], :, :], ALU.subtract)\
                       .then_inc(S("ns_r"), 1)
                if j == 0 and transposed(t, ch, done):
                    lo(m - 1, 1)
                if j == 0 and done > 1:
                    final(t - 2)
                wait(dve, S("ns_v"), m + 1)
                wait(dve, S("ns_ds"), m * 2)
                if j == 0 and done > 1:
                    wait(dve, S("ns_final"), t - 2)
                dve.tensor_copy(vn[R[1], :, :], pX[1][R[1], :, :]).then_inc(S("ns_vn1"), 1)
                if left > 0:
                    first_inverse(nxt)
                for rnd in range(2):
                    wait(dve, S("ns_ds"), m * 2 + rnd + 1)
                    for a in range(2):
                        for p in range(2):
                            hd = 2 * (2 * rnd + a) + p
                            wait(dve, S("ns_dec"), m + 1)
                            dve.scalar_tensor_tensor(St[:, hd, :], St[:, hd, :], dec[ch.par][:, hd:hd + 1],
                                                     pS[p][:, a, :], ALU.mult, ALU.add).then_inc(S("ns_su"), 1)
                if left > 0:
                    level(nxt, 0)
                wait(dve, S("ns_rs"), m * 2 + 2)
                wait(dve, S(f"ns_in_z{ch.par}"), (m - ch.par) * 16 + 32)
                og_ = og[ch.par]
                for hp in range(HP):
                    for p in range(2):
                        r = R[1 - p]
                        dve.scalar_tensor_tensor(og_[r, hp, :], pX[p][r, hp, :], ss[r, hp:hp + 1], og_[r, hp, :],
                                                 ALU.mult, ALU.mult).then_inc(S("ns_og"), 1)
                    if hp == 1 and left > 0:
                        level(nxt, 1)
                if left > 0:
                    level(nxt, 2)
                    level(nxt, 3)
                    level(nxt, 4)
                if done:
                    residual(t - 1, j)
                if j and transposed(t, ch, done):
                    if not done:
                        dve.wait_ge(S("ns_wlo"), KO)
                    lo(m - 1, 0)

            def tail():
                final(NT - 2)
                lo(2 * NT - 2, 1)
                residual(NT - 1, 0)
                residual(NT - 1, 1)
                final(NT - 1)
            first = Chunk(1, 1)
            dve.wait_ge(S("ns_init"), 1)
            differences(first)
            first_inverse(first)
            for l in range(LV):
                level(first, l)
            over_chunks(dve, chunk, tail)

        @block.gpsimd
        def _(pool):
            def mult(dst, a, b, sem):
                pool.tensor_tensor(dst, a, b, ALU.mult).then_inc(S(sem), 1)

            def prepare(ch, between=lambda: None):
                m = ch.m
                dn_ = dn[ch.par]
                wait(pool, S("ns_in_g"), m * 32 + 32)
                wait(pool, S("ns_gbc"), m)
                wait(pool, S("ns_low"), m * LV)
                wait(pool, S("ns_t"), m * LV)
                mult(tg, gp[:, :, :, :].rearrange("p h w c -> p (h w) c"), eye_p([P, 2 * HP, C]), "ns_tg")
                between()
                wait(pool, S("ns_gbc"), m + 1)
                wait(pool, S("ns_edn"), m + 1)
                mult(mtf, dn_[:, :, :], gp[:, :, 1, :], "ns_mtf")
                wait(pool, S("ns_mtf"), m * 2 + 1)
                mult(mtf, mtf, mask(K_LOW1T), "ns_mtf")
                wait(pool, S("ns_edx"), m + 1)
                mult(dx[:, :, :], dx[:, :, :], bc(gbc[:, :, 1:2], [P, HP, C]), "ns_dxb")
                mult(dn_[:, :, :], dn_[:, :, :], mask(K_CAUSP), "ns_dnm")
                wait(pool, S("ns_m"), m + 1)
                wait(pool, S("ns_mt"), m + 1)
                wait(pool, S("ns_p"), m * LV)
                mult(low[0], M, mask(K_LOW), "ns_low1")
                mult(low[1], M, mask(K_LOW + C), "ns_low")
                wait(pool, S("ns_low1"), m + 1)
                wait(pool, S("ns_up"), m * LV)
                pool.tensor_tensor(Ti[:, :, :], eye_p([P, HP, C]), low[0], ALU.subtract).then_inc(S("ns_t"), 1)
                for l in range(1, LV):
                    mult(low[l + 1], M, mask(K_LOW + (l + 1) * C), "ns_low")

            def decayed(ch):
                m = ch.m
                wait(pool, S("ns_er"), m + 1)
                wait(pool, S("ns_in_kq"), m * 64 + 64)
                wait(pool, S("ns_x"), m)
                mult(kqd[:, :, :, :], kq[:, :, :, :], bc(gb[:, :, 0:1, :], [P, NH, 2, C]), "ns_kqd")
                wait(pool, S("ns_kqd"), m * 3 + 1)
                for p in range(2):
                    mult(kqd[:, p::2, p, :], kqd[:, p::2, p, :], gb[:, p::2, 1, :], "ns_kqd")

            def weighed(ch):
                m = ch.m
                wait(pool, S("ns_in_v"), m * 32 + 32)
                wait(pool, S("ns_gbc"), m + 1)
                mult(v[:, :, :], v[:, :, :], bc(gbc[:, :, 1:2], [P, HP, NDV]), "ns_vb")
                wait(pool, S("ns_ekdl"), m + 1)
                wait(pool, S("ns_in_kt"), m * 32 + 32)
                mult(kdec[:, :, :], kt[:, :, :], bc(kdl[:, :].rearrange("p (h o) -> p h o", o=1), [P, HP, NDK]),
                     "ns_kdec")

            def chunk(ch, t, done, left):
                m, j = ch.m, ch.j
                nxt = ch.ahead(1)
                if left > 0:
                    prepare(nxt, (lambda: norm2(t - 2)) if j == 0 and done > 1 else lambda: None)
                    decayed(nxt)
                waits_apart(pool, T.pool_carrier,
                            (S("ns_ss"), m * 8 + 8),
                            (S("ns_og"), m * 8))
                rsqrt(ss, NDV, m, "ns_rs")
                if left > 0:
                    weighed(nxt)
                if part_of(t, ch):
                    w_lo(pool, part_of(t, ch))

            def rsqrt(x, width, i, sem):
                pool.tensor_scalar(x[:, :], x[:, :], 1.0 / width, EPS, ALU.mult, ALU.add).then_inc(S(sem), 1)
                wait(pool, S(sem), i * 2 + 1)
                pool.tensor_tensor(x[:, :], x[:, :], bc(T.minus_half[:, 0:1], list(x.shape)), ALU.pow)\
                    .then_inc(S(sem), 1)

            def norm2(t):
                waits_apart(pool, T.pool_carrier,
                            (S("ns_ss2"), t))
                pool.tensor_scalar(ss2[:, :], ss2[:, :], 1.0 / D, EPS, ALU.mult, ALU.add).then_inc(S("ns_mean2"), 1)
                wait(pool, S("ns_mean2"), t)
                pool.tensor_tensor(ss2[:, :], ss2[:, :], T.minus_half[:, 0:1], ALU.pow).then_inc(S("ns_rs2"), 1)

            def tail():
                norm2(NT - 2)
                norm2(NT - 1)
            first = Chunk(1, 1)
            prepare(first)
            decayed(first)
            weighed(first)
            w_lo(pool, 0)
            over_chunks(pool, chunk, tail)


class Tensors:
    pass


def build(nc, a, out):
    T = Tensors()
    with ExitStack() as ctx:
        S = Sems(nc)

        def sb(name, shape, dt=F32, where=ctx):
            return where.enter_context(nc.sbuf_tensor(name, shape, dt))

        def dram(name, shape):
            return nc.dram_tensor(name, shape, F32).ap()
        T.k_dram, T.starts_dram = a["k"], a["starts"]
        T.gla_qk = dram("gla_qk", [GH, 2, P, TP])
        T.gla_ko = dram("gla_ko", [TP, GQK])
        T.gla_v = dram("gla_v", [TP, GV])
        T.gla_z = dram("gla_z", [TP, GV])
        T.h1 = dram("h1", [TP, D])
        T.gdn_qk = dram("gdn_qk", [2, NH, P, TP])
        T.gdn_k = dram("gdn_k", [TP, NQK])
        T.gdn_v = dram("gdn_v", [TP, NV])
        T.gdn_z = dram("gdn_z", [TP, NV])
        T.gb = dram("gdn_gb", [2 * NT, NH, 2, C])
        T.k = sb("consts", [P, K_END])
        T.eye = T.k[:, K_EYE:K_EYE + P]
        T.causal = T.k[:, K_CAUSAL:K_CAUSAL + P].rearrange("p (o c) -> p o c", o=1)
        T.minus_half = sb("minus_half", [P, 1])
        zero_w = sb("zero_weights", [P, 32], mybir.dt.bfloat16)
        spare = [sb(f"carrier{n}", [P, 2]) for n in range(2)]
        with nc.Block() as block:
            @block.vector
            def _(dve):
                dve.memset(zero_w[:, :], 0.0)
                for x in spare:
                    dve.memset(x[:, :], 0.0)
        T.pe_carrier = lambda: nc.tensor.ldweights(zero_w[:, :], tile_position=(0, 0))
        T.dve_carrier = lambda: nc.vector.tensor_copy(spare[0][:, 0:1], spare[0][:, 1:2])
        T.pool_carrier = lambda: nc.gpsimd.tensor_tensor(spare[1][:, 0:1], spare[1][:, 1:2], spare[1][:, 1:2], ALU.add)
        T.cw = sb("conv_taps", [P, CONV, (2 * NQK + NV) // P])
        T.hnw = sb("gla_hn", [P, GV // P])
        T.hnw2 = sb("gdn_hn", [P, NV // P])
        with ExitStack() as hctx:
            T.hn_hi = sb("hn_hi", [P, KT, TP], F32R, hctx)
            T.hn_lo = sb("hn_lo", [P, KT, TP], F32R, hctx)
            with ExitStack() as zctx:
                T.zeros = sb("zeros", [P, NV], F32, zctx)

                def pads():
                    found = [(d[0:PAD, :], T.zeros[0:PAD, 0:d.shape[1]])
                             for d in (T.gla_ko, T.gla_v, T.gla_z, T.gdn_k, T.gdn_v, T.gdn_z)]
                    found += [(T.gla_qk[g, :, :, 0:PAD].rearrange("w p n -> p w n"),
                               T.zeros[:, 0:2 * PAD].rearrange("p (w n) -> p w n", w=2)) for g in range(GH)]
                    found += [(T.gdn_qk[w, :, :, 0:PAD].rearrange("h p n -> p h n"),
                               T.zeros[:, 0:NH * PAD].rearrange("p (h n) -> p h n", h=NH)) for w in range(2)]
                    found += [(T.gb[c].rearrange("h w c -> h (w c)"), T.zeros[0:NH, 0:2 * C]) for c in range(2)]
                    return found
                T.pads = pads
                embed(nc, S, T, a["x"], a["meta"], a["gla_norm"])
            with ExitStack() as gctx:
                T.dec = sb("gla_dec", [P, GH, 2 * NT], F32, gctx)
                with ExitStack() as ectx:
                    T.Eb = sb("gla_eb", [P, GH, L], F32, ectx)
                    T.Enb = sb("gla_enb", [P, GH, L], F32, ectx)
                    T.Eout = sb("gla_eout", [P, GH, L], F32, ectx)
                    project_vz(nc, S, T, "av", a["gla_w_in"], 2 * GQK, 2 * GQK + GV, GV // P, T.gla_v, T.gla_z, T.hnw,
                               gate_of=lambda ctx, acc: GlaGate(nc, S, T, ctx, acc, a["gla_w_in"], a["gla_w_gk"],
                                                                a["gla_b_gk"], a["gla_head_norm"]))
                    gla_qk(nc, S, T, a["gla_w_in"])
                gla_scan(nc, S, T, a["gla_w_out"], a["x"], a["meta"], a["gdn_norm"])
                S.give_back()
            gdn_qk(nc, S, T, a["gdn_w_in"], a["gdn_a_log"], a["gdn_dt_bias"], a["gdn_conv_w"], a["gdn_head_norm"])
            project_vz(nc, S, T, "nv", a["gdn_w_in"], 2 * NQK, 2 * NQK + NV, NV // P, T.gdn_v, T.gdn_z, T.hnw2,
                       conv=2 * NQK // P)
        gdn_scan(nc, S, T, a["gdn_w_out"], a["final_norm"], out)


def kernel(x, meta_tokens, gla_norm, gla_w_in, gla_w_gk, gla_b_gk, gla_head_norm, gla_w_out, gdn_norm, gdn_w_in,
           gdn_conv_w, gdn_a_log, gdn_dt_bias, gdn_head_norm, gdn_w_out, final_norm):
    import concourse.bacc as bacc
    from concourse.bass_utils import run_bass_kernel_spmd

    def by_channel(w, width):
        return np.tile(w.reshape(-1, P).T, (1, width // w.size))

    arrays = {
        "x": x[0], "meta": meta_tokens, "gla_norm": gla_norm, "gla_w_in": gla_w_in[0], "gla_w_gk": gla_w_gk[0],
        "gla_b_gk": gla_b_gk[0].reshape(GH, P).T, "gla_head_norm": by_channel(gla_head_norm[0], GV), "gla_w_out": gla_w_out[0], "gdn_norm": gdn_norm,
        "gdn_w_in": gdn_w_in[0], "gdn_conv_w": gdn_conv_w[0], "gdn_a_log": gdn_a_log[0],
        "gdn_dt_bias": gdn_dt_bias[0], "gdn_head_norm": by_channel(gdn_head_norm[0], NV), "gdn_w_out": gdn_w_out[0],
        "final_norm": final_norm.reshape(1, D), "k": constants(), "starts": chunk_starts(),
    }
    arrays = {name: np.ascontiguousarray(v) for name, v in arrays.items()}
    nc = bacc.Bacc("TRN2", target_bir_lowering=False, num_devices=1)
    a = {name: nc.dram_tensor("in_" + name, v.shape, mybir.dt.from_np(v.dtype), kind="ExternalInput").ap()
         for name, v in arrays.items()}
    out = nc.dram_tensor("out", [SEQ, D], F32, kind="ExternalOutput").ap()
    build(nc, a, out)
    r = run_bass_kernel_spmd(nc, [{"in_" + name: v for name, v in arrays.items()}], core_ids=[0])
    return r.results[0]["out"].reshape(1, SEQ, D)
```
